# Optimizing a Trainium2 kernel written in Bass

```python
import math
import jax, jax.numpy as jnp
from jax import lax
import numpy as np

D_MODEL = 1024
BATCH = 1
SEQ = 1024
DEPTH = 1

HEAD_DIM = 64
N_DIFF_HEADS = 4
DIFF_V_DIM = 2 * HEAD_DIM
N_FOX_HEADS = 8
DIFF_WIDTH = N_DIFF_HEADS * DIFF_V_DIM
FOX_WIDTH = N_FOX_HEADS * HEAD_DIM
MIX_WIDTH = DIFF_WIDTH + FOX_WIDTH
ROT_DIM = HEAD_DIM // 4
ROPE_THETA = 500000.0
Q_BLOCK = 128
DQ_W = N_DIFF_HEADS * 2 * HEAD_DIM
DK_W = N_DIFF_HEADS * 2 * HEAD_DIM
DV_W = DIFF_WIDTH
FQ_W = FOX_WIDTH
FK_W = FOX_WIDTH
FV_W = FOX_WIDTH
FF_W = N_FOX_HEADS
IN_WIDTH = DQ_W + DK_W + DV_W + FQ_W + FK_W + FV_W + FF_W
IN_SPLITS = [DQ_W, DQ_W + DK_W, DQ_W + DK_W + DV_W, DQ_W + DK_W + DV_W + FQ_W,
             DQ_W + DK_W + DV_W + FQ_W + FK_W, DQ_W + DK_W + DV_W + FQ_W + FK_W + FV_W]
N_EXPERTS = 32
TOP_K = 4
D_EXPERT = D_MODEL
SWIGLU_ALPHA = 1.702
SWIGLU_LIMIT = 7.0
MOE_BLOCK = 128
PLE_DIM = 256
NORM_EPS = 1e-5

kernel_name = "hymba_style_diff_fox_moe_block"

def rms_norm(x, g):
    xf = x.astype(jnp.float32)
    y = xf * lax.rsqrt(jnp.mean(xf * xf, axis=-1, keepdims=True) + NORM_EPS)
    return (y * g.astype(jnp.float32)).astype(x.dtype)

def partial_rope(x, positions):
    inv_freq = ROPE_THETA ** (-jnp.arange(0, ROT_DIM, 2, dtype=jnp.float32) / ROT_DIM)
    ang = positions.astype(jnp.float32)[:, :, None] * inv_freq
    ang = ang.reshape(ang.shape[:2] + (1,) * (x.ndim - 3) + (ROT_DIM // 2,))
    cos, sin = jnp.cos(ang), jnp.sin(ang)
    xf = x.astype(jnp.float32)
    x1 = xf[..., :ROT_DIM // 2]
    x2 = xf[..., ROT_DIM // 2:ROT_DIM]
    out = jnp.concatenate([x1 * cos - x2 * sin, x2 * cos + x1 * sin, xf[..., ROT_DIM:]], axis=-1)
    return out.astype(x.dtype)

def diff_attention(q, k, v, lam):
    b, s, h, _, dh = q.shape
    nb = s // Q_BLOCK
    q = q.transpose(0, 2, 3, 1, 4)
    k = k.transpose(0, 2, 3, 1, 4)
    v = v.transpose(0, 2, 1, 3)
    qb = jnp.moveaxis(q.reshape(b, h, 2, nb, Q_BLOCK, dh), 3, 0)
    scale = dh ** -0.5
    k_pos = jnp.arange(s)

    def block(args):
        q_blk, qi = args
        sc = jnp.einsum('bhmqd,bhmkd->bhmqk', q_blk, k).astype(jnp.float32) * scale
        mask = k_pos[None, :] <= (qi * Q_BLOCK + jnp.arange(Q_BLOCK))[:, None]
        a = jax.nn.softmax(jnp.where(mask, sc, -jnp.inf), axis=-1)
        a = a[:, :, 0] - lam * a[:, :, 1]
        return jnp.einsum('bhqk,bhkd->bhqd', a.astype(v.dtype), v)

    o = lax.map(block, (qb, jnp.arange(nb)))
    return jnp.moveaxis(o, 0, 2).reshape(b, h, s, -1).transpose(0, 2, 1, 3)

def forgetting_attention(q, k, v, c):
    b, s, h, dh = q.shape
    nb = s // Q_BLOCK
    q = q.transpose(0, 2, 1, 3)
    k = k.transpose(0, 2, 1, 3)
    v = v.transpose(0, 2, 1, 3)
    c = c.transpose(0, 2, 1)
    qb = jnp.moveaxis(q.reshape(b, h, nb, Q_BLOCK, dh), 2, 0)
    cb = jnp.moveaxis(c.reshape(b, h, nb, Q_BLOCK), 2, 0)
    scale = dh ** -0.5
    k_pos = jnp.arange(s)

    def block(args):
        q_blk, c_blk, qi = args
        sc = jnp.einsum('bhqd,bhkd->bhqk', q_blk, k).astype(jnp.float32) * scale
        sc = sc + c_blk[..., :, None] - c[..., None, :]
        mask = k_pos[None, :] <= (qi * Q_BLOCK + jnp.arange(Q_BLOCK))[:, None]
        a = jax.nn.softmax(jnp.where(mask, sc, -jnp.inf), axis=-1)
        return jnp.einsum('bhqk,bhkd->bhqd', a.astype(v.dtype), v)

    o = lax.map(block, (qb, cb, jnp.arange(nb)))
    return jnp.moveaxis(o, 0, 2).reshape(b, h, s, dh).transpose(0, 2, 1, 3)

def hybrid_mixer(xn, positions, w_in, lq1, lk1, lq2, lk2, g_subln, b_forget, w_out, lambda_init):
    b, s, _ = xn.shape
    proj = xn @ w_in
    dq, dk, dv, fq, fk, fv, fz = jnp.split(proj, IN_SPLITS, axis=-1)
    dq = partial_rope(dq.reshape(b, s, N_DIFF_HEADS, 2, HEAD_DIM), positions)
    dk = partial_rope(dk.reshape(b, s, N_DIFF_HEADS, 2, HEAD_DIM), positions)
    dv = dv.reshape(b, s, N_DIFF_HEADS, DIFF_V_DIM)
    f32 = jnp.float32
    lam = (jnp.exp(jnp.sum(lq1.astype(f32) * lk1.astype(f32)))
           - jnp.exp(jnp.sum(lq2.astype(f32) * lk2.astype(f32))) + lambda_init)
    d_out = diff_attention(dq, dk, dv, lam)
    d_out = rms_norm(d_out, g_subln) * (1.0 - lambda_init)
    logf = jax.nn.log_sigmoid(fz.astype(f32) + b_forget.astype(f32))
    c = jnp.cumsum(logf, axis=1)
    f_out = forgetting_attention(fq.reshape(b, s, N_FOX_HEADS, HEAD_DIM),
                                 fk.reshape(b, s, N_FOX_HEADS, HEAD_DIM),
                                 fv.reshape(b, s, N_FOX_HEADS, HEAD_DIM), c)
    mixed = jnp.concatenate([d_out.reshape(b, s, DIFF_WIDTH), f_out.reshape(b, s, FOX_WIDTH)], axis=-1)
    return mixed @ w_out

def moe(xn, w_router, b_router, w1, b1, w2, b2):
    b, s, d = xn.shape
    n = b * s
    xf = xn.reshape(n, d)
    logits = xf.astype(jnp.float32) @ w_router.astype(jnp.float32) + b_router.astype(jnp.float32)
    top_vals, top_idx = lax.top_k(logits, TOP_K)
    gates = jax.nn.softmax(top_vals, axis=-1)
    a = n * TOP_K
    flat_e = top_idx.reshape(a).astype(jnp.int32)
    flat_tok = jnp.arange(a, dtype=jnp.int32) // TOP_K
    flat_w = gates.reshape(a)
    counts = jnp.zeros((N_EXPERTS,), jnp.int32).at[flat_e].add(1)
    padded_counts = (counts + MOE_BLOCK - 1) // MOE_BLOCK * MOE_BLOCK
    padded_ends = jnp.cumsum(padded_counts)
    padded_starts = padded_ends - padded_counts
    starts = jnp.cumsum(counts) - counts
    order = jnp.argsort(flat_e)
    sorted_e = flat_e[order]
    dest = padded_starts[sorted_e] + (jnp.arange(a, dtype=jnp.int32) - starts[sorted_e])
    n_rows = a + N_EXPERTS * MOE_BLOCK
    n_blocks = n_rows // MOE_BLOCK
    row_tok = jnp.zeros((n_rows,), jnp.int32).at[dest].set(flat_tok[order])
    row_w = jnp.zeros((n_rows,), jnp.float32).at[dest].set(flat_w[order])
    block_e = jnp.clip(jnp.searchsorted(padded_ends, jnp.arange(n_blocks) * MOE_BLOCK, side='right'),
                       0, N_EXPERTS - 1).astype(jnp.int32)
    x_rows = xf[row_tok].reshape(n_blocks, MOE_BLOCK, d)

    def expert_block(args):
        xb, e = args
        h = xb @ w1[e] + b1[e]
        glu = jnp.minimum(h[..., ::2], SWIGLU_LIMIT)
        lin = jnp.clip(h[..., 1::2], -SWIGLU_LIMIT, SWIGLU_LIMIT)
        act = glu * jax.nn.sigmoid(SWIGLU_ALPHA * glu) * (lin + 1.0)
        return act @ w2[e] + b2[e]

    y = lax.map(expert_block, (x_rows, block_e)).reshape(n_rows, d)
    out = jnp.zeros((n, d), y.dtype).at[row_tok].add(y * row_w.astype(y.dtype)[:, None])
    return out.reshape(b, s, d)

def setup_inputs(seed: int = 0) -> dict:
    key = jax.random.key(seed)
    ks = jax.random.split(key, 24)
    nrm = jax.random.normal
    L, D, E, I = DEPTH, D_MODEL, N_EXPERTS, D_EXPERT
    return {
        "x": nrm(ks[0], (BATCH, SEQ, D), jnp.float32),
        "p": nrm(ks[1], (L, BATCH, SEQ, PLE_DIM), jnp.float32),
        "positions": (jnp.arange(SEQ, dtype=jnp.int32)[None, :]
                      + jax.random.randint(ks[2], (BATCH, 1), 0, 4096, dtype=jnp.int32)),
        "g_attn": 1.0 + 0.02 * nrm(ks[3], (L, D), jnp.float32),
        "w_in": nrm(ks[4], (L, D, IN_WIDTH), jnp.float32) * D ** -0.5,
        "lambda_q1": 0.1 * nrm(ks[5], (L, HEAD_DIM), jnp.float32),
        "lambda_k1": 0.1 * nrm(ks[6], (L, HEAD_DIM), jnp.float32),
        "lambda_q2": 0.1 * nrm(ks[7], (L, HEAD_DIM), jnp.float32),
        "lambda_k2": 0.1 * nrm(ks[8], (L, HEAD_DIM), jnp.float32),
        "g_subln": 1.0 + 0.02 * nrm(ks[9], (L, DIFF_V_DIM), jnp.float32),
        "b_forget": 2.0 + 0.5 * nrm(ks[10], (L, N_FOX_HEADS), jnp.float32),
        "w_out": nrm(ks[11], (L, MIX_WIDTH, D), jnp.float32) * MIX_WIDTH ** -0.5,
        "g_moe": 1.0 + 0.02 * nrm(ks[12], (L, D), jnp.float32),
        "w_router": nrm(ks[13], (L, D, E), jnp.float32) * D ** -0.5,
        "b_router": 0.01 * nrm(ks[14], (L, E), jnp.float32),
        "w_e1": nrm(ks[15], (L, E, D, 2 * I), jnp.float32) * D ** -0.5,
        "b_e1": 0.01 * nrm(ks[16], (L, E, 2 * I), jnp.float32),
        "w_e2": nrm(ks[17], (L, E, I, D), jnp.float32) * I ** -0.5,
        "b_e2": 0.01 * nrm(ks[18], (L, E, D), jnp.float32),
        "g_ple": 1.0 + 0.02 * nrm(ks[19], (L, D), jnp.float32),
        "w_ple_gate": nrm(ks[20], (L, D, D), jnp.float32) * D ** -0.5,
        "w_ple_proj": nrm(ks[21], (L, PLE_DIM, D), jnp.float32) * PLE_DIM ** -0.5,
        "g_final": 1.0 + 0.02 * nrm(ks[22], (D,), jnp.float32),
    }

def reference(x, p, positions, g_attn, w_in, lambda_q1, lambda_k1, lambda_q2, lambda_k2,
              g_subln, b_forget, w_out, g_moe, w_router, b_router, w_e1, b_e1, w_e2, b_e2,
              g_ple, w_ple_gate, w_ple_proj, g_final):
    h = x
    for i in range(DEPTH):
        lambda_init = 0.8 - 0.6 * math.exp(-0.3 * i)
        h = h + hybrid_mixer(rms_norm(h, g_attn[i]), positions, w_in[i],
                             lambda_q1[i], lambda_k1[i], lambda_q2[i], lambda_k2[i],
                             g_subln[i], b_forget[i], w_out[i], lambda_init)
        h = h + moe(rms_norm(h, g_moe[i]), w_router[i], b_router[i],
                    w_e1[i], b_e1[i], w_e2[i], b_e2[i])
        gate = jax.nn.sigmoid(rms_norm(h, g_ple[i]) @ w_ple_gate[i])
        h = h + gate * (p[i] @ w_ple_proj[i])
    return rms_norm(h, g_final)


_drawn_inputs = setup_inputs


def setup_inputs(seed=0):
    import zlib

    import numpy as np

    out = dict(_drawn_inputs(seed))
    spreads = {}
    factors = {'lambda_q1': 32.06, 'b_e1': 8.0, 'b_e2': 8.0, 'g_ple': 45.312, 'g_final': 7.969}
    for name, (base, spread) in spreads.items():
        noise = np.random.default_rng([zlib.crc32(name.encode()), seed]).standard_normal(out[name].shape)
        drawn = base * np.exp(spread * noise) if base else spread * noise
        out[name] = __import__('jax').numpy.asarray(drawn.astype(out[name].dtype))
    for name, factor in factors.items():
        out[name] = (out[name] * factor).astype(out[name].dtype)
    return out
```

```python
from contextlib import ExitStack

import numpy as np
import concourse.bass as bass
from concourse import mybir

F32 = mybir.dt.float32
F32R = mybir.dt.float32r
I32 = mybir.dt.int32
U32 = mybir.dt.uint32
ALU = mybir.AluOpType
ACT = mybir.ActivationFunctionType
AX = mybir.AxisListType
ds = bass.ds

P = 128
D = 1024
T = 1024
KD = D // P
NT = T // P
HD = 64
N_DIFF = 4
N_FOX = 8
ROT = HD // 4
EPS = 1e-5
SCALE = HD ** -0.5
LAMBDA_INIT = 0.8 - 0.6
NEG = -1e30
E_ = 32
TOPK = 4
FE = 1024
PLE = 256
LIMIT = 7.0
ALPHA = 1.702
BR = 256
NPASS = (T * TOPK + E_ * (BR - 1)) // BR + 1
DQ0, DK0, DV0 = 0, 512, 1024
FQ0, FK0, FV0, FF0 = 1536, 2048, 2560, 3072
TWO_PI_1 = 6.28125
TWO_PI_2 = float(np.float32(2 * np.pi - 6.28125) // np.float32(2.0 ** -21) * 2.0 ** -21)
TWO_PI_3 = 2 * np.pi - 6.28125 - TWO_PI_2
PI_BELOW = 3.1415925
ROUND = 1.5 * 2.0 ** 23


class Steps:

    def __init__(self, eng, sem, start=0):
        self.eng, self.sem, self.start, self.n = eng, sem, start, 0

    def step(self, ins):
        self.n += 1
        ins.then_inc(self.sem, 1)
        self.eng.wait_ge(self.sem, self.start + self.n)


def settle(eng, sem):
    eng.sem_inc(sem("settled"), 1)


def phase_prepare(nc, dram, g, sem):
    with ExitStack() as ctx:
        def sb(name, shape, dt=F32):
            return ctx.enter_context(nc.sbuf_tensor(name, shape, dt))

        def ps(name, shape, dt=F32):
            return ctx.enter_context(nc.psum_tensor(name, shape, dt))

        x_in = [sb(f"x_in{j}", [P, D]) for j in range(2)]
        x_scaled = [sb(f"x_scaled{j}", [P, D]) for j in range(2)]
        squares = [sb(f"squares{j}", [P, D]) for j in range(2)]
        ssq = sb("ssq", [P, 2])
        rstd = sb("rstd", [P, 2])
        g_attn = sb("g_attn", [P, KD])
        pos_i = sb("pos_i", [P, T], I32)
        inv_freq = sb("inv_freq", [P, 1])
        ang = sb("ang", [P, T])
        turns = sb("turns", [P, T])
        reduced = sb("reduced", [P, T])
        lam_in = sb("lam_in", [P, 4, HD])
        lam_junk = sb("lam_junk", [P, HD])
        lam_s = sb("lam_s", [P, 2])
        lam_e = sb("lam_e", [P, 2])
        w_f = sb("w_f", [P, KD, N_FOX])
        b_f = sb("b_f", [N_FOX, 1])
        z = sb("z", [N_FOX, T])
        z_e = sb("z_e", [N_FOX, T])
        z_l = sb("z_l", [N_FOX, T])
        ones8 = sb("ones8", [N_FOX, T])
        turned = [ps(f"turned{j}", [P, KD, P]) for j in range(2)]
        z_ps = ps("z_ps", [N_FOX, T])
        xT, ident = g["xT"], g["ident"]
        block = ctx.enter_context(nc.Block())

        @block.sync
        def _(sp):
            sp.dma_start(ident[:, :], dram["c_ident"]).then_inc(sem("a_ident"), 16)
            sp.dma_start(g_attn[:, :], dram["g_attn"]).then_inc(sem("a_g"), 16)
            with sp.Fori(0, NT // 2) as i:
                for j in range(2):
                    sp.wait_ge(sem("a_x_free"), 2 * i + j + 1)
                    sp.dma_start(x_in[j][:, :], dram["x"][0, ds((2 * i + j) * P, P), :]).then_inc(sem(f"a_x{j}"), 16)
            sp.dma_start(pos_i[:, :], dram["positions"][0].partition_broadcast(P)).then_inc(sem("a_pos"), 16)
            sp.dma_start(inv_freq[:, :], dram["c_inv_freq"]).then_inc(sem("a_inv"), 16)
            sp.dma_start(w_f[:, :, :], dram["w_in"][0].rearrange("(k p) n -> p k n", p=P)[:, :, FF0:FF0 + N_FOX]).then_inc(sem("a_wf"), 16)
            sp.dma_start(b_f[:, :], dram["b_forget"]).then_inc(sem("a_bf"), 16)
            for n, name in enumerate(("lambda_q1", "lambda_k1", "lambda_q2", "lambda_k2")):
                sp.dma_start(lam_in[:, n, :], dram[name][0].partition_broadcast(P)).then_inc(sem("a_lam"), 16)
            sp.dma_start(g["mask"][:, :], dram["c_mask"]).then_inc(sem("a_mask"), 16)
            sp.dma_start(g["rot"][:, :], dram["c_rot"]).then_inc(sem("a_rot"), 16)
            sp.dma_start(g["gain"][:, 0:1], dram["g_subln"]).then_inc(sem("a_gain"), 16)
            sp.wait_ge(sem("a_negc"), 1)
            sp.dma_start(dram["negc"], z_e[:, :]).then_inc(sem("a_out"), 16)
            sp.wait_ge(sem("a_out"), 16)
            sp.wait_ge(sem("a_mask"), 16)
            sp.wait_ge(sem("a_rot"), 16)

        @block.scalar
        def _(act):
            with act.Fori(0, NT // 2) as i:
                for j in range(2):
                    act.wait_ge(sem(f"a_x{j}"), 16 * i + 16)
                    nc.scalar.activation(squares[j][:, :], x_in[j][:, :], ACT.Square,
                                         accum_out=ssq[:, j:j + 1]).then_inc(sem("a_ssq"), 1)
            act.wait_ge(sem("a_z"), 2)
            nc.scalar.activation(z_e[:, :], z_l[:, :], ACT.Exp).then_inc(sem("a_ze"), 1)
            act.wait_ge(sem("a_z"), 3)
            nc.scalar.activation(z_l[:, :], z_e[:, :], ACT.Ln).then_inc(sem("a_zl"), 1)
            act.wait_ge(sem("a_lams"), 2)
            nc.scalar.activation(lam_e[:, :], lam_s[:, :], ACT.Exp).then_inc(sem("a_lame"), 1)
            act.wait_ge(sem("a_red"), 1)
            nc.scalar.activation(g["sin"][:, :], reduced[:, :], ACT.Sin).then_inc(sem("a_sin"), 1)
            act.wait_ge(sem("a_red"), 2)
            nc.scalar.activation(g["cos"][:, :], reduced[:, :], ACT.Sin).then_inc(sem("a_sin"), 1)

        @block.gpsimd
        def _(pool):
            nc.gpsimd.memset(g["minus_half"][:, :], -0.5).then_inc(sem("a_half"), 1)
            pool.wait_ge(sem("a_half"), 1)
            with pool.Fori(0, NT // 2) as i:
                for j in range(2):
                    pool.wait_ge(sem("a_mean"), 2 * i + j + 1)
                    nc.gpsimd.tensor_tensor(rstd[:, j:j + 1], rstd[:, j:j + 1], g["minus_half"][:, 0:1], ALU.pow).then_inc(sem("a_rstd"), 1)

        @block.tensor
        def _(pe):
            pe.wait_ge(sem("a_ident"), 16)
            with pe.Fori(0, NT // 2) as i:
                for j in range(2):
                    pe.wait_ge(sem("a_xs"), 2 * i + j + 1)
                    pe.wait_ge(sem("a_turned_free"), 2 * i + j + 1)
                    for k in range(KD):
                        ins = nc.tensor.transpose(turned[j][:, k, :], x_scaled[j][:, k * P:(k + 1) * P], ident[:, :])
                    ins.then_inc(sem("a_turned"), 1)
            pe.wait_ge(sem("a_turned_free"), NT + 2)
            pe.wait_ge(sem("a_wf"), 16)
            for h in range(2):
                for k in range(KD):
                    ins = nc.tensor.matmul(z_ps[:, h * 512:(h + 1) * 512], w_f[:, k, :],
                                           xT[:, k, h * 512:(h + 1) * 512], start=k == 0, stop=k == KD - 1)
            ins.then_inc(sem("a_zps"), 1)

        @block.vector
        def _(dve):
            dve.sem_inc(sem("a_x_free"), 2)
            dve.sem_inc(sem("a_turned_free"), 2)
            dve.wait_ge(sem("a_g"), 16)
            with dve.Fori(0, NT // 2) as i:
                for j in range(2):
                    dve.wait_ge(sem("a_ssq"), 2 * i + j + 1)
                    nc.vector.tensor_scalar(rstd[:, j:j + 1], ssq[:, j:j + 1], 1.0 / D, EPS, ALU.mult, ALU.add).then_inc(sem("a_mean"), 1)
                for j in range(2):
                    dve.wait_ge(sem("a_rstd"), 2 * i + j + 1)
                    nc.vector.tensor_scalar(x_scaled[j][:, :], x_in[j][:, :], rstd[:, j:j + 1], None,
                                            ALU.mult).then_inc(sem("a_xs"), 1)
                    dve.wait_ge(sem("a_xs"), 2 * i + j + 1)
                    dve.sem_inc(sem("a_x_free"), 1)
                for j in range(2):
                    dve.wait_ge(sem("a_turned"), 2 * i + j + 1)
                    nc.vector.tensor_tensor(xT[:, :, ds((2 * i + j) * P, P)], turned[j][:, :, :],
                                            g_attn[:, :].unsqueeze(2).broadcast_to([P, KD, P]),
                                            ALU.mult).then_inc(sem("a_turned_free"), 1)
            own = Steps(dve, sem("a_dve"))
            dve.wait_ge(sem("a_zps"), 1)
            dve.wait_ge(sem("a_bf"), 16)
            own.step(nc.vector.memset(ones8[:, :], 1.0))
            nc.vector.tensor_scalar(z[:, :], z_ps[:, :], b_f[:, 0:1], None, ALU.add).then_inc(sem("a_z"), 1)
            dve.wait_ge(sem("a_z"), 1)
            nc.vector.scalar_tensor_tensor(z_l[:, :], z[:, :], -1.0, z[:, :], ALU.mult, ALU.min).then_inc(sem("a_z"), 1)
            dve.wait_ge(sem("a_ze"), 1)
            nc.vector.tensor_scalar(z_e[:, :], z_e[:, :], 1.0, None, ALU.add).then_inc(sem("a_z"), 1)
            dve.wait_ge(sem("a_zl"), 1)
            own.step(nc.vector.tensor_scalar(z[:, :], z[:, :], 0.0, None, ALU.min))
            own.step(nc.vector.tensor_tensor(z_l[:, :], z_l[:, :], z[:, :], ALU.subtract))
            nc.vector.tensor_tensor_scan(z_e[:, :], ones8[:, :], z_l[:, :], 0.0, ALU.mult, ALU.add).then_inc(sem("a_negc"), 1)
            dve.wait_ge(sem("a_lam"), 64)
            for n in range(2):
                nc.vector.tensor_tensor_reduce(lam_junk[:, :], lam_in[:, 2 * n, :], lam_in[:, 2 * n + 1, :], 1.0, 0.0,
                                               ALU.mult, ALU.add, lam_s[:, n:n + 1]).then_inc(sem("a_lams"), 1)
                dve.wait_ge(sem("a_lams"), n + 1)
            dve.wait_ge(sem("a_lame"), 1)
            own.step(nc.vector.tensor_tensor(g["neg_lam"][:, :], lam_e[:, 1:2], lam_e[:, 0:1], ALU.subtract))
            own.step(nc.vector.tensor_scalar(g["neg_lam"][:, :], g["neg_lam"][:, :], -LAMBDA_INIT, None, ALU.add))
            dve.wait_ge(sem("a_gain"), 16)
            own.step(nc.vector.tensor_scalar(g["gain"][:, :], g["gain"][:, :], 1.0 - LAMBDA_INIT, None, ALU.mult))
            dve.wait_ge(sem("a_pos"), 16)
            dve.wait_ge(sem("a_inv"), 16)
            own.step(nc.vector.tensor_copy(ang[:, :], pos_i[:, :]))
            own.step(nc.vector.tensor_scalar(ang[:, :], ang[:, :], inv_freq[:, 0:1], None, ALU.mult))
            for n, quarter in enumerate((0.0, 0.25)):
                own.step(nc.vector.tensor_scalar(turns[:, :], ang[:, :], float(1 / (2 * np.pi)), quarter, ALU.mult, ALU.add))
                own.step(nc.vector.tensor_scalar(turns[:, :], turns[:, :], ROUND, None, ALU.add))
                own.step(nc.vector.tensor_scalar(turns[:, :], turns[:, :], ROUND, None, ALU.subtract))
                if n:
                    dve.wait_ge(sem("a_sin"), 1)
                own.step(nc.vector.scalar_tensor_tensor(reduced[:, :], turns[:, :], -TWO_PI_1, ang[:, :], ALU.mult, ALU.add))
                own.step(nc.vector.scalar_tensor_tensor(reduced[:, :], turns[:, :], -TWO_PI_2, reduced[:, :], ALU.mult, ALU.add))
                own.step(nc.vector.scalar_tensor_tensor(reduced[:, :], turns[:, :], -TWO_PI_3, reduced[:, :], ALU.mult, ALU.add))
                own.step(nc.vector.tensor_scalar(reduced[:, :], reduced[:, :], quarter * 2 * np.pi, None, ALU.add))
                nc.vector.tensor_scalar(reduced[:, :], reduced[:, :], PI_BELOW, -PI_BELOW, ALU.min, ALU.max).then_inc(sem("a_red"), 1)


def phase_attention(nc, dram, g, sem, diff):
    tag = "d" if diff else "f"
    q0, k0, v0 = (DQ0, DK0, DV0) if diff else (FQ0, FK0, FV0)
    NH = 4
    with ExitStack() as ctx:
        def sb(name, shape, dt=F32):
            return ctx.enter_context(nc.sbuf_tensor(f"{tag}_{name}", shape, dt))

        def ps(name, shape, dt=F32):
            return ctx.enter_context(nc.psum_tensor(f"{tag}_{name}", shape, dt))

        def s(name):
            return sem(f"{tag}_{name}")

        w_qkv = [sb(f"w_qkv{j}", [P, 3, KD, P]) for j in range(2)]
        q_raw = sb("q_raw", [P, T])
        k_raw = sb("k_raw", [P, T])
        qT = sb("qT", [P, T]) if diff else q_raw
        kT = sb("kT", [P, T]) if diff else k_raw
        v = sb("v", [P, NT, P])
        prob = [[sb(f"prob{b}{m}", [P, T]) for m in range(2)] for b in range(2)]
        probT = [[sb(f"probT{b}{m}", [P, NT, P]) for m in range(1 if diff else 2)] for b in range(2)]
        stat = sb("stat", [P, NT, 2, 5])
        o_row = sb("o_row", [P, NT, P])
        o_sq = sb("o_sq", [P, NT, P])
        o_ss = sb("o_ss", [P, NT])
        if diff:
            zeros = sb("zeros", [P, D])
        if not diff:
            negc = [sb(f"negc{m}", [P, T]) for m in range(2)]
            negc_d = [sb(f"negc_d{m}", [P, NT, P]) for m in range(2)]
        score = [ps(f"score{m}", [P, T]) for m in range(2)]
        turned = ps("turned", [P, NT, P])
        o_ps = [ps(f"o_ps{b}", [P, P]) for b in range(2)]
        xT, mixT, ident = g["xT"], g["mixT"], g["ident"]
        nm = 1 if diff else 2
        wv = P // nm
        wr = dram["w_in"][0].rearrange("(k p) n -> p k n", p=P)
        block = ctx.enter_context(nc.Block())

        @block.sync
        def _(sp):
            with sp.Fori(0, NH // 2) as i:
                for j in range(2):
                    sp.wait_ge(s("w_free"), 2 * i + j + 1)
                    for n, c0 in enumerate((q0, k0, v0)):
                        sp.dma_start(w_qkv[j][:, n, :, :], wr[:, :, ds((2 * i + j) * P + c0, P)]).then_inc(s(f"w{j}"), 16)
                    if diff:
                        share = NPASS * BR // NH
                        sp.wait_ge(s("zeros"), 1)
                        sp.dma_start(dram["y"][ds((2 * i + j) * share, share), :].rearrange("(n p) d -> p n d", p=P),
                                     zeros[:, :].unsqueeze(1).broadcast_to([P, share // P, D])).then_inc(s("cleared"), 16)
                    if not diff:
                        sp.wait_ge(s("negc_free"), 2 * i + j + 1)
                        for m in range(2):
                            sp.dma_start(negc[m][:, :], dram["negc"][ds((2 * i + j) * 2 + m, 1), :].broadcast_to([P, T])
                                         ).then_inc(s("negc"), 16)
            if diff:
                sp.wait_ge(s("cleared"), 16 * NH)

        @block.tensor
        def _(pe):
            pe.sem_inc(s("w_free"), 2)
            with pe.Fori(0, NH // 2) as i:
                for j in range(2):
                    n_head = 2 * i + j
                    pe.wait_ge(s(f"w{j}"), 48 * i + 48)
                    for n in range(2):
                        pe.wait_ge(s("score_free"), (n_head + 1) * 2 * NT)
                        for h in range(2):
                            for k in range(KD):
                                ins = nc.tensor.matmul(score[n][:, h * 512:(h + 1) * 512], w_qkv[j][:, n, k, :],
                                                       xT[:, k, h * 512:(h + 1) * 512], start=k == 0, stop=k == KD - 1)
                        ins.then_inc(s("proj"), 1)
                    if diff:
                        for n, raw in enumerate((q_raw, k_raw)):
                            pe.wait_ge(s("raw"), 3 * n_head + n + 1)
                            for h in range(2):
                                ins = nc.tensor.matmul(score[n][:, h * 512:(h + 1) * 512], g["rot"][:, :],
                                                       raw[:, h * 512:(h + 1) * 512], start=True, stop=True)
                            ins.then_inc(s("rotated"), 1)
                    pe.wait_ge(s("turned_free"), n_head * (nm * NT + 1) + 1)
                    for t in range(NT):
                        for k in range(KD):
                            ins = nc.tensor.matmul(turned[:, t, :], xT[:, k, t * P:(t + 1) * P], w_qkv[j][:, 2, k, :],
                                                   start=k == 0, stop=k == KD - 1)
                    ins.then_inc(s("v"), 1)
                    pe.wait_ge(s("v"), n_head + 1)
                    pe.sem_inc(s("w_free"), 1)
                    if diff:
                        pe.wait_ge(s("roped"), 2 * n_head + 2)
                    else:
                        pe.wait_ge(s("raw"), 3 * n_head + 2)
                    for step in range(NT + 2):
                        if step < NT:
                            width = (step + 1) * P
                            for m in range(2):
                                if step:
                                    pe.wait_ge(s("score_free"), (n_head + 1) * 2 * NT + 2 * step - 1 + m)
                                for c in range(0, width, 512):
                                    ins = nc.tensor.matmul(score[m][:, c:min(c + 512, width)],
                                                           qT[m * HD:(m + 1) * HD, step * P:(step + 1) * P],
                                                           kT[m * HD:(m + 1) * HD, c:min(c + 512, width)],
                                                           start=True, stop=True)
                                ins.then_inc(s("score"), 1)
                        if step >= 2:
                            b = step - 2
                            pe.wait_ge(s("o_free"), n_head * NT + b + 1)
                            if b == 0:
                                pe.wait_ge(s("raw"), 3 * n_head + 3)
                            for m in range(nm):
                                pe.wait_ge(s("probT"), (n_head * NT + b) * nm + m + 1)
                                for kb in range(b + 1):
                                    ins = nc.tensor.matmul(o_ps[b % 2][:, m * wv:(m + 1) * wv], probT[b % 2][m][:, kb, :],
                                                           v[:, kb, m * wv:(m + 1) * wv], start=kb == 0, stop=kb == b)
                            ins.then_inc(s("o"), 1)
                        if 1 <= step <= NT:
                            b = step - 1
                            for m in range(nm):
                                pe.wait_ge(s("prob"), (n_head * NT + b) * nm + m + 1)
                                pe.wait_ge(s("turned_free"), n_head * (nm * NT + 1) + b * nm + m + 1)
                                if b == 0 and m == 0:
                                    pe.wait_ge(s("raw"), 3 * n_head + 3)
                                for kb in range(b + 1):
                                    ins = nc.tensor.transpose(turned[:, kb, :], prob[b % 2][m][:, kb * P:(kb + 1) * P], ident[:, :])
                                ins.then_inc(s("turned"), 1)
                    pe.wait_ge(s("o_row"), n_head + 1)
                    pe.wait_ge(s("turned_free"), n_head * (nm * NT + 1) + nm * NT + 1)
                    for t in range(NT):
                        ins = nc.tensor.transpose(turned[:, t, :], o_row[:, t, :], ident[:, :])
                    ins.then_inc(s("o_turned"), 1)

        @block.scalar
        def _(act):
            act.sem_inc(s("turned_free"), 1)
            with act.Fori(0, NH // 2) as i:
                for j in range(2):
                    n_head = 2 * i + j
                    act.wait_ge(s("proj"), 2 * n_head + 1)
                    nc.scalar.activation(q_raw[:, :], score[0][:, :], ACT.Copy, scale=SCALE).then_inc(s("raw"), 1)
                    act.wait_ge(s("proj"), 2 * n_head + 2)
                    nc.scalar.activation(k_raw[:, :], score[1][:, :], ACT.Copy).then_inc(s("raw"), 1)
                    act.wait_ge(s("v"), n_head + 1)
                    nc.scalar.activation(v[:, :, :], turned[:, :, :], ACT.Copy).then_inc(s("raw"), 1)
                    for step in range(NT + 1):
                        if step < NT:
                            width = (step + 1) * P
                            for m in range(2):
                                act.wait_ge(s("negmax"), (n_head * NT + step) * 2 + m + 1)
                                nc.scalar.activation(prob[step % 2][m][:, 0:width], prob[step % 2][m][:, 0:width], ACT.Exp,
                                                     bias=stat[:, step, m, 2:3], accum_out=stat[:, step, m, 3:4]
                                                     ).then_inc(s("exp") if diff else s("prob"), 1)
                        if step >= 1:
                            b = step - 1
                            for m in range(nm):
                                act.wait_ge(s("turned"), (n_head * NT + b) * nm + m + 1)
                                if b >= 2:
                                    act.wait_ge(s("o"), n_head * NT + b - 1)
                                nc.scalar.activation(probT[b % 2][m][:, 0:b + 1, :], turned[:, 0:b + 1, :], ACT.Copy
                                                     ).then_inc(s("probT"), 1)
                                act.wait_ge(s("probT"), (n_head * NT + b) * nm + m + 1)
                                act.sem_inc(s("turned_free"), 1)
                    act.wait_ge(s("o_turned"), n_head + 1)
                    out = mixT[:, ds(n_head + (0 if diff else N_DIFF), 1), :].rearrange("p a t -> p (a t)")
                    nc.scalar.activation(out, turned[:, :, :].rearrange("p a t -> p (a t)"), ACT.Copy,
                                         scale=g["gain"][:, 0:1] if diff else 1.0).then_inc(s("turned_free"), 1)

        @block.gpsimd
        def _(pool):
            if diff:
                nc.gpsimd.memset(zeros[:, :], 0.0).then_inc(s("zeros"), 1)
                with pool.Fori(0, NH // 2) as i:
                    for j in range(2):
                        n_head = 2 * i + j
                        for n, (raw, to) in enumerate(((q_raw, qT), (k_raw, kT))):
                            pool.wait_ge(s("raw"), 3 * n_head + n + 1)
                            nc.gpsimd.tensor_tensor(to[:, :], raw[:, :], g["cos"][:, :], ALU.mult).then_inc(s("cos"), 1)
                        pool.wait_ge(s("mean"), n_head + 1)
                        nc.gpsimd.tensor_tensor(o_ss[:, :], o_ss[:, :], g["minus_half"][:, :], ALU.pow).then_inc(s("rstd"), 1)
            else:
                pool.sem_inc(s("negc_free"), 1)
                with pool.Fori(0, NH // 2) as i:
                    for j in range(2):
                        n_head = 2 * i + j
                        for m in range(2):
                            pool.wait_ge(s("negc"), 32 * n_head + 32)
                            nc.gpsimd.tensor_tensor(negc_d[m][:, :, :], negc[m][:, :].rearrange("p (a t) -> p a t", t=P),
                                                    g["mask"][:, T - P:T].unsqueeze(1).broadcast_to([P, NT, P]),
                                                    ALU.add).then_inc(s("negc_d"), 1)

        @block.vector
        def _(dve):
            dve.sem_inc(s("score_free"), 2 * NT)
            dve.sem_inc(s("o_free"), 2)
            per = DVE_STEPS_DIFF if diff else DVE_STEPS_FOX
            with dve.Fori(0, NH // 2) as i:
                own = Steps(dve, s("dve"), i * per)
                for j in range(2):
                    n_head = 2 * i + j
                    if diff:
                        for n, to in enumerate((qT, kT)):
                            dve.wait_ge(s("rotated"), 2 * n_head + n + 1)
                            own.step(nc.vector.tensor_tensor(prob[0][n][:, :], score[n][:, :], g["sin"][:, :], ALU.mult))
                            dve.wait_ge(s("cos"), 2 * n_head + n + 1)
                            nc.vector.tensor_tensor(to[:, :], to[:, :], prob[0][n][:, :], ALU.add).then_inc(s("roped"), 1)
                    else:
                        dve.wait_ge(s("negc_d"), 2 * n_head + 2)

                    def normalise(b):
                        dve.wait_ge(s("exp"), (n_head * NT + b) * 2 + 2)
                        w = (b + 1) * P
                        own.step(nc.vector.reciprocal(stat[:, b, :, 4:5], stat[:, b, :, 3:4]))
                        own.step(nc.vector.tensor_tensor(stat[:, b, 1, 4:5], stat[:, b, 1, 4:5], g["neg_lam"][:, :], ALU.mult))
                        own.step(nc.vector.tensor_scalar(prob[b % 2][1][:, 0:w], prob[b % 2][1][:, 0:w],
                                                         stat[:, b, 1, 4:5], None, ALU.mult))
                        nc.vector.scalar_tensor_tensor(prob[b % 2][0][:, 0:w], prob[b % 2][0][:, 0:w], stat[:, b, 0, 4:5],
                                                       prob[b % 2][1][:, 0:w], ALU.mult, ALU.add).then_inc(s("prob"), 1)

                    def collect(b):
                        dve.wait_ge(s("o"), n_head * NT + b + 1)
                        if diff:
                            ins = nc.vector.tensor_copy(o_row[:, b, :], o_ps[b % 2][:, :])
                        else:
                            own.step(nc.vector.reciprocal(stat[:, b, :, 4:5], stat[:, b, :, 3:4]))
                            for m in range(2):
                                ins = nc.vector.tensor_scalar(o_row[:, b, m * wv:(m + 1) * wv], o_ps[b % 2][:, m * wv:(m + 1) * wv],
                                                              stat[:, b, m, 4:5], None, ALU.mult)
                                if m == 0:
                                    own.step(ins)
                        own.step(ins)
                        dve.sem_inc(s("o_free"), 1)

                    dve.wait_ge(s("turned_free"), n_head * (nm * NT + 1) + 1)
                    for step in range(NT + 2):
                        if diff and 1 <= step <= NT:
                            normalise(step - 1)
                        if step < NT:
                            width = (step + 1) * P
                            for m in range(2):
                                dve.wait_ge(s("score"), (n_head * NT + step) * 2 + m + 1)
                                if step >= 2:
                                    dve.wait_ge(s("turned"), (n_head * NT + step - 2) * nm + min(m, nm - 1) + 1)
                                p = prob[step % 2][m]
                                st = stat[:, step, m, :]
                                settle(dve, s)
                                if diff:
                                    own.step(nc.vector.tensor_tensor_reduce(
                                        p[:, 0:width], score[m][:, 0:width], g["mask"][:, T - width:T], 1.0, 3 * NEG,
                                        ALU.add, ALU.max, st[:, 0:1]))
                                    last = st[:, 0:1]
                                else:
                                    own.step(nc.vector.tensor_tensor_reduce(
                                        p[:, width - P:width], score[m][:, width - P:width], negc_d[m][:, step, :], 1.0, 3 * NEG,
                                        ALU.add, ALU.max, st[:, 0:1]))
                                    last = st[:, 0:1]
                                    if step:
                                        settle(dve, s)
                                        own.step(nc.vector.tensor_tensor_reduce(
                                            p[:, 0:width - P], score[m][:, 0:width - P], negc[m][:, 0:width - P], 1.0, st[:, 0:1],
                                            ALU.add, ALU.max, st[:, 1:2]))
                                        last = st[:, 1:2]
                                dve.sem_inc(s("score_free"), 1)
                                nc.vector.tensor_scalar(st[:, 2:3], last, -1.0, None, ALU.mult).then_inc(s("negmax"), 1)
                        if step >= 2:
                            collect(step - 2)
                    if diff:
                        own.step(nc.vector.tensor_tensor(o_sq[:, :, :], o_row[:, :, :], o_row[:, :, :], ALU.mult))
                        own.step(nc.vector.tensor_reduce(o_ss[:, :], o_sq[:, :, :], AX.X, ALU.add))
                        nc.vector.tensor_scalar(o_ss[:, :], o_ss[:, :], 1.0 / P, EPS, ALU.mult, ALU.add).then_inc(s("mean"), 1)
                        dve.wait_ge(s("rstd"), n_head + 1)
                        nc.vector.tensor_tensor(o_row[:, :, :], o_row[:, :, :],
                                                o_ss[:, :].unsqueeze(2).broadcast_to([P, NT, P]), ALU.mult).then_inc(s("o_row"), 1)
                    else:
                        dve.sem_inc(s("o_row"), 1)
                        dve.sem_inc(s("negc_free"), 1)
                assert own.n == per, own.n


DVE_STEPS_DIFF = 2 * (2 + 3 * NT + 2 * NT + NT + 2)
DVE_STEPS_FOX = 2 * (2 * NT + 2 * (NT - 1) + 3 * NT)


def phase_route(nc, dram, g, sem):
    with ExitStack() as ctx:
        def sb(name, shape, dt=F32):
            return ctx.enter_context(nc.sbuf_tensor(f"c_{name}", shape, dt))

        def ps(name, shape, dt=F32):
            return ctx.enter_context(nc.psum_tensor(f"c_{name}", shape, dt))

        def s(name):
            return sem(f"c_{name}")

        w_out = sb("w_out", [P, KD, D])
        w_r = sb("w_r", [P, KD, E_])
        b_r = sb("b_r", [P, E_])
        g_moe = g["g_moe"]
        before = sb("before", [P, P])
        ones = sb("ones", [P, P])
        tokens = sb("tokens", [P, NT], I32)
        zeros = sb("zeros", [P, E_ * T // P], I32)
        experts = sb("experts", [P, E_])
        experts_i = sb("experts_i", [P, E_], I32)
        passes_i = sb("passes_i", [1, NPASS], I32)
        passes = sb("passes", [1, NPASS])
        stage = [sb(f"stage{j}", [P, KD, P]) for j in range(2)]
        x_in = [sb(f"x_in{j}", [P, D]) for j in range(2)]
        h1 = [sb(f"h1{j}", [P, D]) for j in range(2)]
        hn = [sb(f"hn{j}", [P, D]) for j in range(2)]
        hT = [sb(f"hT{j}", [P, KD, P]) for j in range(2)]
        squares = [sb(f"squares{j}", [P, D]) for j in range(2)]
        ssq = sb("ssq", [P, 2])
        rstd = sb("rstd", [P, 2])
        logits = sb("logits", [P, E_])
        top = sb("top", [P, 8])
        top_i = sb("top_i", [P, 8], U32)
        top_f = sb("top_f", [P, 8])
        neg_top = sb("neg_top", [P, 1])
        gsum = sb("gsum", [P, 1])
        onehot = sb("onehot", [P, NT, TOPK, E_])
        chosen = sb("chosen", [P, E_])
        chosen_sum = sb("chosen_sum", [P, E_])
        place = sb("place", [P, NT, TOPK])
        place_e = sb("place_e", [P, TOPK, E_])
        lists = sb("lists", [P, NT, TOPK])
        lists_i = sb("lists_i", [P, NT, TOPK], I32)
        first = sb("first", [P, NT, TOPK])
        tmp4 = sb("tmp4", [P, TOPK])
        n_pass = sb("n_pass", [P, E_])
        n_tmp = sb("n_tmp", [P, E_])
        pass_end = sb("pass_end", [P, E_])
        pass_start = sb("pass_start", [P, E_])
        counts = sb("counts", [P, E_])
        ones32 = sb("ones32", [P, E_])
        big = sb("big", [P, NT * TOPK, E_])
        in_pass = sb("in_pass", [1, NPASS, E_])
        in_tmp = sb("in_tmp", [1, NPASS, E_])
        tab = sb("tab", [1, 3, NPASS])
        tab_t = sb("tab_t", [1, NPASS])
        acc = [ps(f"acc{j}", [P, D]) for j in range(2)]
        turned = ps("turned", [P, KD, P])
        rt_ps = ps("rt_ps", [P, E_])
        pl_ps = ps("pl_ps", [P, E_])
        ident, gates, dense = g["ident"], g["gates"], g["dense"]
        block = ctx.enter_context(nc.Block())
        H = KD // 2

        @block.sync
        def _(sp):
            wr = dram["w_out"][0].rearrange("(k p) n -> p k n", p=P)
            for k in range(0, KD, 2):
                sp.dma_start(w_out[:, k:k + 2, :], wr[:, k:k + 2, :]).then_inc(s("w_out"), 16)
            sp.dma_start(w_r[:, :, :], dram["w_router"][0].rearrange("(k p) n -> p k n", p=P)).then_inc(s("w_r"), 16)
            sp.dma_start(b_r[:, :], dram["b_router"][0].partition_broadcast(P)).then_inc(s("w_r"), 16)
            sp.dma_start(g_moe[:, :], dram["g_moe"]).then_inc(s("w_r"), 16)
            sp.dma_start(before[:, :], dram["c_before"]).then_inc(s("w_r"), 16)
            sp.dma_start(tokens[:, :], dram["c_tokens"]).then_inc(s("tokens"), 16)
            sp.wait_ge(s("zeros"), 1)
            sp.dma_start(dram["lists"].rearrange("(p n) a -> p (n a)", p=P), zeros[:, :]).then_inc(s("cleared"), 16)
            with sp.Fori(0, NT // 2) as i:
                for j in range(2):
                    sp.wait_ge(s("x_free"), 2 * i + j + 1)
                    sp.dma_start(x_in[j][:, :], dram["x"][0, ds((2 * i + j) * P, P), :]).then_inc(s(f"x{j}"), 16)
            sp.wait_ge(s("cleared"), 16)

        @block.gpsimd
        def _(pool):
            nc.gpsimd.memset(zeros[:, :], 0).then_inc(s("zeros"), 1)
            nc.gpsimd.iota(experts_i[:, :], pattern=[[1, E_]], base=0, channel_multiplier=0).then_inc(s("iota"), 1)
            nc.gpsimd.iota(passes_i[:, :], pattern=[[1, NPASS]], base=0, channel_multiplier=0).then_inc(s("iota"), 1)
            nc.gpsimd.memset(ones[:, :], 1.0).then_inc(s("ones"), 1)
            with pool.Fori(0, NT // 2) as i:
                for j in range(2):
                    pool.wait_ge(s("stage_free"), 2 * i + j + 1)
                    nc.gpsimd.tensor_copy(stage[j][:, :, :], g["mixT"][:, :, ds((2 * i + j) * P, P)]).then_inc(s("stage"), 1)
                for j in range(2):
                    pool.wait_ge(s("mean"), 2 * i + j + 1)
                    nc.gpsimd.tensor_tensor(rstd[:, j:j + 1], rstd[:, j:j + 1], g["minus_half"][:, 0:1], ALU.pow).then_inc(s("rstd"), 1)
            pool.wait_ge(s("cleared"), 16)
            pool.wait_ge(s("tokens"), 16)
            pool.wait_ge(s("lists"), 1)
            for t in range(NT):
                for k in range(TOPK):
                    nc.gpsimd.indirect_dma_start(
                        out=dram["lists"], out_offset=bass.IndirectOffsetOnAxis(ap=lists_i[:, t, k:k + 1], axis=0),
                        in_=tokens[:, t:t + 1], in_offset=None).then_inc(s("scattered"), 16)
            pool.wait_ge(s("scattered"), 16 * NT * TOPK)

        @block.tensor
        def _(pe):
            pe.sem_inc(s("stage_free"), 2)
            pe.wait_ge(s("w_out"), 64)
            pe.wait_ge(s("w_r"), 64)
            pe.wait_ge(s("ones"), 1)
            with pe.Fori(0, NT // 2) as i:
                for j in range(2):
                    t = 2 * i + j
                    pe.wait_ge(s("stage"), t + 1)
                    pe.wait_ge(s("x_free"), t + 1)
                    for c in range(2):
                        for k in range(KD):
                            ins = nc.tensor.matmul(acc[j][:, c * 512:(c + 1) * 512], stage[j][:, k, :],
                                                   w_out[:, k, c * 512:(c + 1) * 512], start=k == 0, stop=k == KD - 1)
                    ins.then_inc(s("acc"), 1)
                    pe.wait_ge(s("acc"), t + 1)
                    pe.sem_inc(s("stage_free"), 1)
                for j in range(2):
                    t = 2 * i + j
                    pe.wait_ge(s("hn"), t + 1)
                    pe.wait_ge(s("turned_free"), t + 1)
                    for k in range(KD):
                        ins = nc.tensor.transpose(turned[:, k, :], hn[j][:, k * P:(k + 1) * P], ident[:, :])
                    ins.then_inc(s("turned"), 1)
                    pe.wait_ge(s("hT"), t + 1)
                    for k in range(KD):
                        ins = nc.tensor.matmul(rt_ps[:, :], hT[j][:, k, :], w_r[:, k, :], start=k == 0, stop=k == KD - 1)
                    ins.then_inc(s("logits"), 1)
                    pe.wait_ge(s("chosen"), t + 1)
                    nc.tensor.matmul(pl_ps[:, :], before[:, :], chosen[:, :], start=True, stop=False)
                    nc.tensor.matmul(pl_ps[:, :], ones[:, :], chosen_sum[:, :], start=False, stop=True).then_inc(s("place"), 1)
            pe.wait_ge(s("chosen"), NT + 1)
            nc.tensor.matmul(pl_ps[:, :], ones[:, :], chosen_sum[:, :], start=True, stop=True).then_inc(s("place"), 1)

        @block.scalar
        def _(act):
            for j in range(2):
                act.sem_inc(s(f"h1_out{j}"), 16)
                act.sem_inc(s(f"hn_out{j}"), 16)
            with act.Fori(0, NT // 2) as i:
                for j in range(2):
                    t = 2 * i + j
                    act.wait_ge(s("h1"), t + 1)
                    nc.scalar.activation(squares[j][:, :], h1[j][:, :], ACT.Square, accum_out=ssq[:, j:j + 1]).then_inc(s("ssq"), 1)
                    act.dma_start(dram["h1"][ds(t * P, P), :], h1[j][:, :]).then_inc(s(f"h1_out{j}"), 16)
                for j in range(2):
                    t = 2 * i + j
                    act.wait_ge(s("hn"), t + 1)
                    act.dma_start(dram["hn"][ds(t * P, P), :], hn[j][:, :]).then_inc(s(f"hn_out{j}"), 16)
                    act.wait_ge(s("neg_top"), t + 1)
                    nc.scalar.activation(gates[:, ds(t * TOPK, TOPK)], top[:, 0:TOPK], ACT.Exp, bias=neg_top[:, 0:1],
                                         accum_out=gsum[:, 0:1]).then_inc(s("gates"), 1)
            for j in range(2):
                act.wait_ge(s(f"h1_out{j}"), 16 * (NT // 2) + 16)
                act.wait_ge(s(f"hn_out{j}"), 16 * (NT // 2) + 16)

        @block.vector
        def _(dve):
            dve.sem_inc(s("x_free"), 2)
            dve.sem_inc(s("turned_free"), 1)
            nc.vector.memset(chosen_sum[:, :], 0.0).then_inc(s("init"), 1)
            nc.vector.memset(ones32[:, :], 1.0).then_inc(s("init"), 1)
            dve.wait_ge(s("iota"), 2)
            nc.vector.tensor_copy(experts[:, :], experts_i[:, :]).then_inc(s("init"), 1)
            nc.vector.tensor_copy(passes[:, :], passes_i[:, :]).then_inc(s("init"), 1)
            dve.wait_ge(s("init"), 4)
            dve.wait_ge(s("w_r"), 64)
            per = 2 * (3 + 1 + TOPK + 4 + 5)
            with dve.Fori(0, NT // 2) as i:
                own = Steps(dve, s("dve"), i * per)
                for j in range(2):
                    t = 2 * i + j
                    dve.wait_ge(s("acc"), t + 1)
                    dve.wait_ge(s(f"x{j}"), 16 * i + 16)
                    dve.wait_ge(s(f"h1_out{j}"), 16 * i + 16)
                    dve.wait_ge(s(f"hn_out{j}"), 16 * i + 16)
                    nc.vector.tensor_tensor(h1[j][:, :], acc[j][:, :], x_in[j][:, :], ALU.add).then_inc(s("h1"), 1)
                    dve.wait_ge(s("h1"), t + 1)
                    dve.sem_inc(s("x_free"), 1)
                    dve.wait_ge(s("ssq"), t + 1)
                    nc.vector.tensor_scalar(rstd[:, j:j + 1], ssq[:, j:j + 1], 1.0 / D, EPS, ALU.mult, ALU.add).then_inc(s("mean"), 1)
                for j in range(2):
                    t = 2 * i + j
                    dve.wait_ge(s("rstd"), t + 1)
                    nc.vector.tensor_scalar(hn[j][:, :], h1[j][:, :], rstd[:, j:j + 1], None, ALU.mult).then_inc(s("hn"), 1)
                for j in range(2):
                    t = 2 * i + j
                    dve.wait_ge(s("turned"), t + 1)
                    nc.vector.tensor_tensor(hT[j][:, :, :], turned[:, :, :], g_moe[:, :].unsqueeze(2).broadcast_to([P, KD, P]),
                                            ALU.mult).then_inc(s("hT"), 1)
                    dve.wait_ge(s("hT"), t + 1)
                    dve.sem_inc(s("turned_free"), 1)
                    dve.wait_ge(s("logits"), t + 1)
                    own.step(nc.vector.tensor_tensor(logits[:, :], rt_ps[:, :], b_r[:, :], ALU.add))
                    settle(dve, s)
                    own.step(nc.vector.max(top[:, :], logits[:, :]))
                    settle(dve, s)
                    own.step(nc.vector.max_index(top_i[:, :], top[:, :], logits[:, :]))
                    nc.vector.tensor_scalar(neg_top[:, :], top[:, 0:1], -1.0, None, ALU.mult).then_inc(s("neg_top"), 1)
                    own.step(nc.vector.tensor_copy(top_f[:, :], top_i[:, :]))
                    for k in range(TOPK):
                        own.step(nc.vector.tensor_scalar(onehot[:, ds(t, 1), k, :].rearrange("p a e -> p (a e)"), experts[:, :],
                                                         top_f[:, k:k + 1], None, ALU.is_equal))
                    oh = onehot[:, ds(t, 1), :, :].rearrange("p a k e -> p (a k) e")
                    settle(dve, s)
                    nc.vector.tensor_reduce(chosen[:, :], oh.rearrange("p k e -> p e k"), AX.X, ALU.add).then_inc(s("chosen"), 1)
                    dve.wait_ge(s("gates"), t + 1)
                    gt = gates[:, ds(t * TOPK, TOPK)]
                    own.step(nc.vector.reciprocal(gsum[:, :], gsum[:, :]))
                    own.step(nc.vector.tensor_scalar(gt, gt, gsum[:, 0:1], None, ALU.mult))
                    own.step(nc.vector.tensor_tensor(place_e[:, :, :], oh, gt.unsqueeze(2).broadcast_to([P, TOPK, E_]), ALU.mult))
                    settle(dve, s)
                    own.step(nc.vector.tensor_reduce(dense[:, ds(t, 1), :].rearrange("p a e -> p (a e)"),
                                                     place_e[:, :, :].rearrange("p k e -> p e k"), AX.X, ALU.add))
                    dve.wait_ge(s("place"), t + 1)
                    own.step(nc.vector.tensor_copy(n_tmp[:, :], pl_ps[:, :]))
                    own.step(nc.vector.tensor_tensor(place_e[:, :, :], oh, n_tmp[:, :].unsqueeze(1).broadcast_to([P, TOPK, E_]), ALU.mult))
                    settle(dve, s)
                    own.step(nc.vector.tensor_reduce(place[:, ds(t, 1), :].rearrange("p a k -> p (a k)"),
                                                     place_e[:, :, :], AX.X, ALU.add))
                    own.step(nc.vector.tensor_tensor(chosen_sum[:, :], chosen_sum[:, :], chosen[:, :], ALU.add))
                    own.step(nc.vector.tensor_copy(lists[:, ds(t, 1), :].rearrange("p a k -> p (a k)"), top_f[:, 0:TOPK]))
                assert own.n == per, own.n
            own = Steps(dve, s("dve"), (NT // 2) * per)
            own.step(nc.vector.scalar_tensor_tensor(lists[:, :, :], lists[:, :, :], float(T), place[:, :, :], ALU.mult, ALU.add))
            nc.vector.tensor_copy(lists_i[:, :, :], lists[:, :, :]).then_inc(s("lists"), 1)
            dve.sem_inc(s("chosen"), 1)
            dve.wait_ge(s("place"), NT + 1)
            own.step(nc.vector.tensor_copy(counts[:, :], pl_ps[:, :]))
            own.step(nc.vector.tensor_scalar(n_pass[:, :], counts[:, :], 0.0, None, ALU.is_gt))
            for b in range(1, T // BR):
                own.step(nc.vector.tensor_scalar(n_tmp[:, :], counts[:, :], float(b * BR), None, ALU.is_gt))
                own.step(nc.vector.tensor_tensor(n_pass[:, :], n_pass[:, :], n_tmp[:, :], ALU.add))
            own.step(nc.vector.tensor_tensor_scan(pass_end[:, :], ones32[:, :], n_pass[:, :], 0.0, ALU.mult, ALU.add))
            own.step(nc.vector.tensor_tensor(pass_start[:, :], pass_end[:, :], n_pass[:, :], ALU.subtract))
            own.step(nc.vector.tensor_tensor(big[:, :, :], onehot[:, :, :, :].rearrange("p t k e -> p (t k) e"),
                                             pass_start[:, :].unsqueeze(1).broadcast_to([P, NT * TOPK, E_]), ALU.mult))
            own.step(nc.vector.tensor_reduce(first[:, :, :].rearrange("p t k -> p (t k)"), big[:, :, :], AX.X, ALU.add))
            own.step(nc.vector.scalar_tensor_tensor(first[:, :, :], first[:, :, :], float(BR), place[:, :, :], ALU.mult, ALU.add))
            own.step(nc.vector.tensor_copy(g["y_row"][:, :], first[:, :, :].rearrange("p t k -> p (t k)")))
            p_b = passes[0:1, :].unsqueeze(2).broadcast_to([1, NPASS, E_])

            def over(x):
                return x[0:1, :].unsqueeze(1).broadcast_to([1, NPASS, E_])

            own.step(nc.vector.tensor_tensor(in_pass[:, :, :], p_b, over(pass_start), ALU.is_ge))
            own.step(nc.vector.tensor_tensor(in_tmp[:, :, :], p_b, over(pass_end), ALU.is_ge))
            own.step(nc.vector.tensor_tensor(in_pass[:, :, :], in_pass[:, :, :], in_tmp[:, :, :], ALU.subtract))
            for n, values in enumerate((experts, pass_start, counts)):
                own.step(nc.vector.tensor_tensor(in_tmp[:, :, :], in_pass[:, :, :], over(values), ALU.mult))
                own.step(nc.vector.tensor_reduce(tab[:, n, :], in_tmp[:, :, :], AX.X, ALU.add))
            own.step(nc.vector.tensor_tensor(tab_t[:, :], passes[0:1, :], tab[:, 1, :], ALU.subtract))
            own.step(nc.vector.tensor_scalar(tab_t[:, :], tab_t[:, :], float(BR), None, ALU.mult))
            own.step(nc.vector.tensor_tensor(tab[:, 2, :], tab[:, 2, :], tab_t[:, :], ALU.subtract))
            own.step(nc.vector.tensor_scalar(tab[:, 2, :], tab[:, 2, :], 0.0, None, ALU.max))
            own.step(nc.vector.scalar_tensor_tensor(tab[:, 1, :], tab[:, 0, :], float(T), tab_t[:, :], ALU.mult, ALU.add))
            own.step(nc.vector.tensor_scalar(tab[:, 1, :], tab[:, 1, :], float(E_ * T - BR), None, ALU.min))
            own.step(nc.vector.tensor_copy(g["table"][:, 0:3 * NPASS], tab[:, :, :].rearrange("p a n -> p (a n)")))
            own.step(nc.vector.tensor_copy(g["table"][:, 3 * NPASS:], pass_end[0:1, E_ - 1:E_]))


def phase_experts(nc, dram, g, sem):
    with ExitStack() as ctx:
        def sb(name, shape, dt=F32):
            return ctx.enter_context(nc.sbuf_tensor(f"e_{name}", shape, dt))

        def ps(name, shape, dt=F32):
            return ctx.enter_context(nc.psum_tensor(f"e_{name}", shape, dt))

        def s(name):
            return sem(f"e_{name}")

        C1, C2, W = 2 * FE // 512, D // 512, 512
        NF = FE // P
        PB = BR // P
        w = [sb(f"w{c}", [P, KD, W]) for c in range(C1 + C2)]
        b1 = sb("b1", [P, E_, NF, 2])
        b1_now = sb("b1_now", [P, NF, 2])
        rows_i = [sb(f"rows_i{b}", [P, 1], I32) for b in range(PB)]
        x_rows = sb("x_rows", [P, PB, D])
        xT = sb("xT", [P, KD, BR])
        gate = [sb(f"gate{n}", [P, BR]) for n in range(2)]
        lin = [sb(f"lin{n}", [P, BR]) for n in range(2)]
        sig = [sb(f"sig{n}", [P, BR]) for n in range(2)]
        act_t = sb("act_t", [P, NF, BR])
        y = sb("y", [P, PB, D])
        h_ps = [ps(f"h_ps{n}", [P, 2, BR]) for n in range(2)]
        y_ps = [ps(f"y_ps{c}", [P, PB, W]) for c in range(C2)]
        turned = ps("turned", [P, KD, P])
        ident, table, g_moe = g["ident"], g["table"], g["g_moe"]
        block = ctx.enter_context(nc.Block())

        def expert(eng, p):
            return eng.value_load(table[0:1, ds(p, 1)], min_val=0, max_val=E_ - 1)

        def first_row(eng, p):
            return eng.value_load(table[0:1, ds(p + NPASS, 1)], min_val=0, max_val=E_ * T - BR)

        def rows_left(eng, p):
            return eng.value_load(table[0:1, ds(p + 2 * NPASS, 1)], min_val=0, max_val=T)

        @block.sync
        def _(sp):
            sp.dma_start(b1[:, :, :, :].rearrange("p e f g -> p (e f g)"), dram["b_e1"]).then_inc(s("b1"), 16)
            w1 = dram["w_e1"][0].rearrange("e (k p) n -> p e k n", p=P)
            w2 = dram["w_e2"][0].rearrange("e (k p) n -> p e k n", p=P)
            with sp.Fori(0, NPASS - 1) as p:
                with sp.If(rows_left(sp, p) > 0):
                    e = expert(sp, p)
                    for c in range(C1 + C2):
                        if c < C1:
                            sp.wait_ge(s("h"), NF * p + 2 * c + 2)
                        else:
                            sp.wait_ge(s("y"), C2 * p + c - C1 + 1)
                        src, n = (w1, c) if c < C1 else (w2, c - C1)
                        sp.dma_start(w[c][:, :, :], src[:, ds(e, 1), :, n * W:(n + 1) * W].rearrange("p e k n -> p (e k) n")
                                     ).then_inc(s(f"w{c}"), 16)

        @block.gpsimd
        def _(pool):
            def gather(start, n):
                for b in range(PB):
                    pool.dma_start(rows_i[b][:, :], dram["lists"][ds(start + b * P, P), :]).then_inc(s(f"rows{b}"), 16)
                for b in range(PB):
                    pool.wait_ge(s(f"rows{b}"), 16 * n + 16)
                    pool.wait_ge(s("x_turned"), PB * n + b + 1)
                    settle(pool, s)
                    nc.gpsimd.indirect_dma_start(out=x_rows[:, b, :], out_offset=None, in_=dram["hn"],
                                                 in_offset=bass.IndirectOffsetOnAxis(ap=rows_i[b][:, 0:1], axis=0)
                                                 ).then_inc(s(f"x{b}"), 16)

            gather(first_row(pool, 0), 0)
            with pool.Fori(0, NPASS - 1) as p:
                with pool.If(rows_left(pool, p) > 0):
                    for b in range(PB):
                        pool.wait_ge(s(f"x{b}"), 16 * p + 16)
                    gather(first_row(pool, p + 1), p + 1)

        @block.tensor
        def _(pe):
            pe.sem_inc(s("h"), NF)
            pe.sem_inc(s("y"), C2)
            pe.sem_inc(s("x_turned"), PB)

            def turn(n):
                for b in range(PB):
                    pe.wait_ge(s(f"x{b}"), 16 * n + 16)
                    pe.wait_ge(s("turned_free"), PB * n + b + 1)
                    for k in range(KD):
                        ins = nc.tensor.transpose(turned[:, k, :], x_rows[:, b, k * P:(k + 1) * P], ident[:, :])
                    ins.then_inc(s("x_turned"), 1)

            def up(p, c, n):
                for m in range(2):
                    q = 2 * c + m
                    pe.wait_ge(s("h_free"), NF * p + q + 1)
                    for part in range(2):
                        for k in range(KD):
                            ins = nc.tensor.matmul(h_ps[q % 2][:, part, 0:n],
                                                   w[c][:, k, 2 * m * P + part:2 * (m + 1) * P:2], xT[:, k, 0:n],
                                                   start=k == 0, stop=k == KD - 1)
                    ins.then_inc(s("h"), 1)

            def down(c, blocks):
                for b in range(blocks):
                    for f in range(NF):
                        ins = nc.tensor.matmul(y_ps[c][:, b, :], act_t[:, f, b * P:(b + 1) * P], w[C1 + c][:, f, :],
                                               start=f == 0, stop=f == NF - 1)
                ins.then_inc(s("y"), 1)

            turn(0)
            with pe.Fori(0, NPASS - 1) as p:
                rows = rows_left(pe, p)
                with pe.If(rows > 0):
                    pe.wait_ge(s("xT"), PB * p + PB)
                    for c in range(C1):
                        pe.wait_ge(s(f"w{c}"), 16 * p + 16)
                        with pe.If(rows > 192):
                            up(p, c, 256)
                        with pe.Else():
                            with pe.If(rows > 128):
                                up(p, c, 192)
                            with pe.Else():
                                up(p, c, 128)
                    turn(p + 1)
                    pe.wait_ge(s("act"), NF * p + NF)
                    for c in range(C2):
                        pe.wait_ge(s(f"w{C1 + c}"), 16 * p + 16)
                        pe.wait_ge(s("y_free"), C2 * p + c + 1)
                        with pe.If(rows > P):
                            down(c, 2)
                        with pe.Else():
                            down(c, 1)

        @block.scalar
        def _(act):
            act.sem_inc(s("y_out"), 16)
            act.sem_inc(s("y_free"), C2)
            with act.Fori(0, NPASS - 1) as p:
                rows = rows_left(act, p)
                with act.If(rows > 0):
                    for q in range(NF):
                        act.wait_ge(s("gate"), NF * p + q + 1)
                        nc.scalar.activation(sig[q % 2][:, :], gate[q % 2][:, :], ACT.Sigmoid, scale=ALPHA).then_inc(s("sig"), 1)
                    y_rows = dram["y"][ds(p * BR, BR), :].rearrange("(b q) d -> q b d", q=P)
                    act.wait_ge(s("y_out"), 16 * p + 16)

                    def evacuate(blocks):
                        for c in range(C2):
                            act.wait_ge(s("y"), C2 * p + C2 + c + 1)
                            nc.scalar.activation(y[:, 0:blocks, c * W:(c + 1) * W], y_ps[c][:, 0:blocks, :], ACT.Copy
                                                 ).then_inc(s("y_free"), 1)
                        act.wait_ge(s("y_free"), C2 * p + 2 * C2)
                        act.dma_start(y_rows[:, 0:blocks, :], y[:, 0:blocks, :]).then_inc(s("y_out"), 16)

                    settle(act, s)
                    with act.If(rows > P):
                        evacuate(2)
                    with act.Else():
                        evacuate(1)
            n = act.value_load(table[0:1, 3 * NPASS:3 * NPASS + 1], min_val=1, max_val=NPASS)
            act.wait_ge(s("y_out"), 16 * n + 16)
            settle(act, s)

        @block.vector
        def _(dve):
            for n in range(2):
                nc.vector.memset(h_ps[n][:, :, :], 0.0).then_inc(s("init"), 1)
            dve.wait_ge(s("init"), 2)
            dve.sem_inc(s("h_free"), 2)
            dve.sem_inc(s("turned_free"), 1)
            dve.wait_ge(s("b1"), 16)
            own = Steps(dve, s("dve"))
            own.step(nc.vector.tensor_scalar(b1[:, :, :, 1], b1[:, :, :, 1], 1.0, None, ALU.add))

            def turn(n):
                for b in range(PB):
                    dve.wait_ge(s("x_turned"), PB * n + PB + b + 1)
                    nc.vector.tensor_tensor(xT[:, :, b * P:(b + 1) * P], turned[:, :, :],
                                            g_moe[:, :].unsqueeze(2).broadcast_to([P, KD, P]), ALU.mult).then_inc(s("xT"), 1)
                    dve.wait_ge(s("xT"), PB * n + b + 1)
                    dve.sem_inc(s("turned_free"), 1)

            turn(0)
            per = 1 + 2 * NF
            with dve.Fori(0, NPASS - 1) as p:
                own = Steps(dve, s("dve"), p * per + 1)
                with dve.If(rows_left(dve, p) > 0):
                    e = expert(dve, p)
                    own.step(nc.vector.tensor_copy(b1_now[:, :, :], b1[:, ds(e, 1), :, :].rearrange("p e f g -> p (e f) g")))
                    for q in range(NF):
                        dve.wait_ge(s("h"), NF * p + NF + q + 1)
                        nc.vector.tensor_scalar(gate[q % 2][:, :], h_ps[q % 2][:, 0, :], b1_now[:, q, 0:1], LIMIT,
                                                ALU.add, ALU.min).then_inc(s("gate"), 1)
                        own.step(nc.vector.tensor_scalar(lin[q % 2][:, :], h_ps[q % 2][:, 1, :], b1_now[:, q, 1:2], LIMIT + 1,
                                                         ALU.add, ALU.min))
                        dve.sem_inc(s("h_free"), 1)
                        dve.wait_ge(s("sig"), NF * p + q + 1)
                        own.step(nc.vector.tensor_tensor(gate[q % 2][:, :], gate[q % 2][:, :], sig[q % 2][:, :], ALU.mult))
                        nc.vector.scalar_tensor_tensor(act_t[:, q, :], lin[q % 2][:, :], 1 - LIMIT, gate[q % 2][:, :],
                                                       ALU.max, ALU.mult).then_inc(s("act"), 1)
                    turn(p + 1)
                assert own.n == per, own.n


def phase_finish(nc, dram, g, sem, out):
    with ExitStack() as ctx:
        def sb(name, shape, dt=F32):
            return ctx.enter_context(nc.sbuf_tensor(f"z_{name}", shape, dt))

        def ps(name, shape, dt=F32):
            return ctx.enter_context(nc.psum_tensor(f"z_{name}", shape, dt))

        def s(name):
            return sem(f"z_{name}")

        KP = PLE // P
        w_gate = sb("w_gate", [P, KD, D])
        w_proj = sb("w_proj", [P, KP, D])
        b2 = sb("b2", [E_, D])
        g_ple = sb("g_ple", [P, KD])
        g_final = sb("g_final", [P, D])
        y_rows = [sb(f"y_rows{j}", [P, TOPK, D]) for j in range(2)]
        dense_t = [sb(f"dense_t{j}", [P, E_]) for j in range(2)]
        denseT = [sb(f"denseT{j}", [E_, P]) for j in range(2)]
        h = [sb(f"h{j}", [P, D]) for j in range(2)]
        p_in = [sb(f"p_in{j}", [P, PLE]) for j in range(2)]
        pT = [sb(f"pT{j}", [P, KP, P]) for j in range(2)]
        hn = [sb(f"hn{j}", [P, D]) for j in range(2)]
        hT = [sb(f"hT{j}", [P, KD, P]) for j in range(2)]
        sig = [sb(f"sig{j}", [P, D]) for j in range(2)]
        squares = [sb(f"squares{j}", [P, D]) for j in range(2)]
        stat = [sb(f"stat{j}", [P, 2]) for j in range(2)]
        turned = ps("turned", [P, KD, P])
        bias_ps = ps("bias_ps", [P, D])
        gate_ps = ps("gate_ps", [P, D])
        proj_ps = ps("proj_ps", [P, D])
        ident, gates, dense = g["ident"], g["gates"], g["dense"]
        block = ctx.enter_context(nc.Block())
        TURNS = 6

        @block.sync
        def _(sp):
            sp.dma_start(b2[:, :], dram["b_e2"][0]).then_inc(s("w"), 16)
            sp.dma_start(w_proj[:, :, :], dram["w_ple_proj"][0].rearrange("(k p) n -> p k n", p=P)).then_inc(s("w"), 16)
            sp.dma_start(w_gate[:, :, :], dram["w_ple_gate"][0].rearrange("(k p) n -> p k n", p=P)).then_inc(s("w"), 16)
            sp.dma_start(g_ple[:, :], dram["g_ple"]).then_inc(s("w"), 16)
            sp.dma_start(g_final[:, :], dram["g_final"].partition_broadcast(P)).then_inc(s("w"), 16)
            for j in range(2):
                sp.sem_inc(s(f"out{j}"), 16)
            with sp.Fori(0, NT // 2) as i:
                for j in range(2):
                    t = 2 * i + j
                    sp.wait_ge(s(f"out{j}"), 16 * i + 16)
                    sp.dma_start(h[j][:, :], dram["h1"][ds(t * P, P), :]).then_inc(s(f"h{j}"), 16)
                    sp.wait_ge(s("p_free"), t + 1)
                    sp.dma_start(p_in[j][:, :], dram["p"][0, 0, ds(t * P, P), :]).then_inc(s(f"p{j}"), 16)
                for j in range(2):
                    t = 2 * i + j
                    sp.wait_ge(s("final"), t + 1)
                    sp.dma_start(out[0, ds(t * P, P), :], h[j][:, :]).then_inc(s(f"out{j}"), 16)
            for j in range(2):
                sp.wait_ge(s(f"out{j}"), 16 * (NT // 2) + 16)

        @block.gpsimd
        def _(pool):
            def gather(t):
                if t >= 2:
                    pool.wait_ge(s("h2"), t - 1)
                for k in range(TOPK):
                    nc.gpsimd.indirect_dma_start(out=y_rows[t % 2][:, k, :], out_offset=None, in_=dram["y"],
                                                 in_offset=bass.IndirectOffsetOnAxis(
                                                     ap=g["y_row"][:, t * TOPK + k:t * TOPK + k + 1], axis=0)
                                                 ).then_inc(s(f"y{t % 2}"), 16)

            def root(n, of):
                for j in range(2):
                    pool.wait_ge(s(f"mean{of}"), 2 * n + j + 1)
                    nc.gpsimd.tensor_tensor(stat[j][:, of:of + 1], stat[j][:, of:of + 1], g["minus_half"][:, 0:1],
                                            ALU.pow).then_inc(s(f"rstd{of}"), 1)

            for t in range(2):
                gather(t)
            for n in range(NT // 2):
                for j in range(2):
                    if n:
                        pool.wait_ge(s("dense_turned"), 2 * n - 1 + j)
                    nc.gpsimd.tensor_copy(dense_t[j][:, :], dense[:, 2 * n + j, :]).then_inc(s("dense"), 1)
                root(n, 0)
                for j in range(2):
                    if n + 1 < NT // 2:
                        gather(2 * n + 2 + j)
                root(n, 1)

        @block.tensor
        def _(pe):
            pe.sem_inc(s("p_free"), 2)
            pe.wait_ge(s("w"), 80)
            with pe.Fori(0, NT // 2) as i:
                for j in range(2):
                    t = 2 * i + j
                    pe.wait_ge(s("dense"), t + 1)
                    pe.wait_ge(s("turned_free"), TURNS * i + j + 1)
                    nc.tensor.transpose(turned[0:E_, 0, :], dense_t[j][:, :], ident[:, :]).then_inc(s("dense_turned"), 1)
                    pe.wait_ge(s("denseT"), t + 1)
                    pe.wait_ge(s("bias_free"), t + 1)
                    for c in range(2):
                        ins = nc.tensor.matmul(bias_ps[:, c * 512:(c + 1) * 512], denseT[j][:, :], b2[:, c * 512:(c + 1) * 512],
                                               start=True, stop=True)
                    ins.then_inc(s("bias"), 1)
                for j in range(2):
                    t = 2 * i + j
                    pe.wait_ge(s(f"p{j}"), 16 * i + 16)
                    pe.wait_ge(s("turned_free"), TURNS * i + j + 3)
                    for k in range(KP):
                        ins = nc.tensor.transpose(turned[:, k, :], p_in[j][:, k * P:(k + 1) * P], ident[:, :])
                    ins.then_inc(s("p_free"), 1)
                for j in range(2):
                    t = 2 * i + j
                    pe.wait_ge(s("pT"), t + 1)
                    pe.wait_ge(s("gate_free"), t + 1)
                    for c in range(2):
                        for k in range(KP):
                            nc.tensor.matmul(proj_ps[:, c * 512:(c + 1) * 512], pT[j][:, k, :],
                                             w_proj[:, k, c * 512:(c + 1) * 512], start=k == 0, stop=k == KP - 1)
                    pe.wait_ge(s("hn"), t + 1)
                    pe.wait_ge(s("turned_free"), TURNS * i + j + 5)
                    for k in range(KD):
                        ins = nc.tensor.transpose(turned[:, k, :], hn[j][:, k * P:(k + 1) * P], ident[:, :])
                    ins.then_inc(s("h_turned"), 1)
                    pe.wait_ge(s("hT"), t + 1)
                    for c in range(2):
                        for k in range(KD):
                            ins = nc.tensor.matmul(gate_ps[:, c * 512:(c + 1) * 512], hT[j][:, k, :],
                                                   w_gate[:, k, c * 512:(c + 1) * 512], start=k == 0, stop=k == KD - 1)
                    ins.then_inc(s("gate"), 1)

        @block.scalar
        def _(act):
            act.sem_inc(s("turned_free"), 1)
            with act.Fori(0, NT // 2) as i:
                for j in range(2):
                    t = 2 * i + j
                    act.wait_ge(s("dense_turned"), t + 1)
                    nc.scalar.activation(denseT[j][:, :], turned[0:E_, 0, :], ACT.Copy).then_inc(s("denseT"), 1)
                    act.wait_ge(s("denseT"), t + 1)
                    act.sem_inc(s("turned_free"), 1)
                for j in range(2):
                    t = 2 * i + j
                    act.wait_ge(s("p_free"), t + 3)
                    nc.scalar.activation(pT[j][:, :, :], turned[:, 0:KP, :], ACT.Copy).then_inc(s("pT"), 1)
                    act.wait_ge(s("pT"), t + 1)
                    act.sem_inc(s("turned_free"), 1)
                for j in range(2):
                    t = 2 * i + j
                    act.wait_ge(s("h2"), t + 1)
                    nc.scalar.activation(squares[j][:, :], h[j][:, :], ACT.Square, accum_out=stat[j][:, 0:1]).then_inc(s("ssq0"), 1)
                for j in range(2):
                    t = 2 * i + j
                    act.wait_ge(s("gate"), t + 1)
                    nc.scalar.activation(sig[j][:, :], gate_ps[:, :], ACT.Sigmoid).then_inc(s("sig"), 1)
                for j in range(2):
                    t = 2 * i + j
                    act.wait_ge(s("h3"), t + 1)
                    nc.scalar.activation(squares[j][:, :], h[j][:, :], ACT.Square, accum_out=stat[j][:, 1:2]).then_inc(s("ssq1"), 1)

        @block.vector
        def _(dve):
            dve.sem_inc(s("bias_free"), 1)
            dve.sem_inc(s("gate_free"), 1)
            dve.wait_ge(s("w"), 80)
            per = 2 * (TOPK + 2)
            with dve.Fori(0, NT // 2) as i:
                own = Steps(dve, s("dve"), i * per)
                for j in range(2):
                    t = 2 * i + j
                    dve.wait_ge(s(f"h{j}"), 16 * i + 16)
                    dve.wait_ge(s("bias"), t + 1)
                    own.step(nc.vector.tensor_tensor(h[j][:, :], h[j][:, :], bias_ps[:, :], ALU.add))
                    dve.sem_inc(s("bias_free"), 1)
                    dve.wait_ge(s(f"y{j}"), 16 * TOPK * i + 16 * TOPK)
                    for k in range(TOPK):
                        ins = nc.vector.scalar_tensor_tensor(h[j][:, :], y_rows[j][:, k, :], gates[:, ds(t * TOPK + k, 1)],
                                                             h[j][:, :], ALU.mult, ALU.add)
                        if k < TOPK - 1:
                            own.step(ins)
                    ins.then_inc(s("h2"), 1)
                for j in range(2):
                    t = 2 * i + j
                    dve.wait_ge(s("ssq0"), t + 1)
                    nc.vector.tensor_scalar(stat[j][:, 0:1], stat[j][:, 0:1], 1.0 / D, EPS, ALU.mult, ALU.add).then_inc(s("mean0"), 1)
                for j in range(2):
                    t = 2 * i + j
                    dve.wait_ge(s("rstd0"), t + 1)
                    nc.vector.tensor_scalar(hn[j][:, :], h[j][:, :], stat[j][:, 0:1], None, ALU.mult).then_inc(s("hn"), 1)
                for j in range(2):
                    t = 2 * i + j
                    dve.wait_ge(s("h_turned"), t + 1)
                    nc.vector.tensor_tensor(hT[j][:, :, :], turned[:, :, :], g_ple[:, :].unsqueeze(2).broadcast_to([P, KD, P]),
                                            ALU.mult).then_inc(s("hT"), 1)
                    dve.wait_ge(s("hT"), t + 1)
                    dve.sem_inc(s("turned_free"), 1)
                    dve.wait_ge(s("sig"), t + 1)
                    own.step(nc.vector.tensor_tensor(sig[j][:, :], sig[j][:, :], proj_ps[:, :], ALU.mult))
                    dve.sem_inc(s("gate_free"), 1)
                    nc.vector.tensor_tensor(h[j][:, :], h[j][:, :], sig[j][:, :], ALU.add).then_inc(s("h3"), 1)
                for j in range(2):
                    t = 2 * i + j
                    dve.wait_ge(s("ssq1"), t + 1)
                    nc.vector.tensor_scalar(stat[j][:, 1:2], stat[j][:, 1:2], 1.0 / D, EPS, ALU.mult, ALU.add).then_inc(s("mean1"), 1)
                for j in range(2):
                    t = 2 * i + j
                    dve.wait_ge(s("rstd1"), t + 1)
                    own.step(nc.vector.tensor_scalar(h[j][:, :], h[j][:, :], stat[j][:, 1:2], None, ALU.mult))
                    nc.vector.tensor_tensor(h[j][:, :], h[j][:, :], g_final[:, :], ALU.mult).then_inc(s("final"), 1)
                assert own.n == per, own.n


def constants():
    k = np.arange(P)
    ident = np.eye(P, dtype=np.float32)
    mask = np.zeros((P, T), np.float32)
    mask[:, T - P:][k[None, :] > k[:, None]] = NEG
    inv = np.zeros((P, 1), np.float32)
    rot = np.zeros((P, P), np.float32)
    half = ROT // 2
    for h in range(0, P, HD):
        for n in range(half):
            f = np.float32(500000.0) ** np.float32(-2.0 * n / ROT)
            inv[h + n] = inv[h + half + n] = f
            rot[h + half + n, h + n] = -1.0
            rot[h + n, h + half + n] = 1.0
    before = (k[:, None] < k[None, :]).astype(np.float32)
    tokens = (np.arange(NT)[None, :] * P + k[:, None]).astype(np.int32)
    return {"c_ident": ident, "c_mask": mask, "c_inv_freq": inv, "c_rot": rot, "c_before": before,
            "c_tokens": tokens}


def build(nc, dram, out):
    for name, shape, dt in (("negc", (N_FOX, T), F32), ("h1", (T, D), F32), ("hn", (T, D), F32),
                            ("lists", (E_ * T, 1), I32), ("y", (NPASS * BR, D), F32)):
        dram[name] = nc.dram_tensor(f"scratch_{name}", shape, dt, kind="Internal").ap()
    with ExitStack() as ctx:
        sems = {}

        def sem(name):
            if name not in sems:
                sems[name] = nc.alloc_semaphore(name=name)
            return sems[name]

        def clear():
            nc.clear_and_free_semaphores(list(sems.values()))
            sems.clear()
            nc.all_engine_barrier()

        def sb(name, shape, dt=F32):
            return ctx.enter_context(nc.sbuf_tensor(name, shape, dt))

        g = {"ident": sb("ident", [P, P]), "minus_half": sb("minus_half", [P, NT]), "g_moe": sb("g_moe", [P, KD]), "gates": sb("gates", [P, NT * TOPK]),
             "dense": sb("dense", [P, NT, E_]), "y_row": sb("y_row", [P, NT * TOPK], I32),
             "table": sb("table", [1, 3 * NPASS + 1], I32)}
        with nc.sbuf_tensor("mixT", [P, KD, T], F32) as mixT:
            g["mixT"] = mixT
            with ExitStack() as inner:
                for name, shape in (("xT", [P, KD, T]), ("mask", [P, T]), ("rot", [P, P]), ("gain", [P, 1]),
                                    ("neg_lam", [P, 1]), ("sin", [P, T]), ("cos", [P, T])):
                    g[name] = inner.enter_context(nc.sbuf_tensor(name, shape, F32))
                phase_prepare(nc, dram, g, sem)
                clear()
                phase_attention(nc, dram, g, sem, True)
                clear()
                phase_attention(nc, dram, g, sem, False)
            clear()
            phase_route(nc, dram, g, sem)
            clear()
        phase_experts(nc, dram, g, sem)
        clear()
        phase_finish(nc, dram, g, sem, out)


_INS = ["x", "p", "positions", "g_attn", "w_in", "lambda_q1", "lambda_k1", "lambda_q2", "lambda_k2",
        "g_subln", "b_forget", "w_out", "g_moe", "w_router", "b_router", "w_e1", "b_e1", "w_e2", "b_e2",
        "g_ple", "w_ple_gate", "w_ple_proj", "g_final"]


def kernel(**inputs):
    import numpy as _np
    import concourse.bacc as _bacc
    from concourse import mybir as _mybir
    from concourse.bass_utils import run_bass_kernel_spmd as _run

    nc = _bacc.Bacc("TRN2", target_bir_lowering=False, num_devices=1)
    arrays, dram = {}, {}
    given = {name: _np.ascontiguousarray(inputs[name]) for name in _INS}
    for name in ("g_attn", "g_moe", "g_ple"):
        given[name] = _np.ascontiguousarray(given[name].reshape(KD, P).T)
    for name in ("b_forget", "g_subln"):
        given[name] = _np.ascontiguousarray(given[name].T)
    given["b_e1"] = _np.ascontiguousarray(
        given["b_e1"].reshape(E_, FE // P, P, 2).transpose(2, 0, 1, 3).reshape(P, E_ * FE // P * 2))
    given.update(constants())
    for name, a in given.items():
        arrays[f"in_{name}_dram"] = a
        dram[name] = nc.dram_tensor(f"in_{name}_dram", a.shape, _mybir.dt.from_np(a.dtype), kind="ExternalInput").ap()
    out = nc.dram_tensor("out_0_dram", (1, T, D), _mybir.dt.float32, kind="ExternalOutput").ap()
    build(nc, dram, out)
    r = _run(nc, [arrays], core_ids=[0])
    return r.results[0]["out_0_dram"]
```

```python
from contextlib import ExitStack

import numpy as np
import concourse.bass as bass
from concourse import mybir

F32 = mybir.dt.float32
F32R = mybir.dt.float32r
I32 = mybir.dt.int32
U32 = mybir.dt.uint32
ALU = mybir.AluOpType
ACT = mybir.ActivationFunctionType
AX = mybir.AxisListType
ds = bass.ds

P = 128
D = 1024
T = 1024
KD = D // P
NT = T // P
HD = 64
N_DIFF = 4
N_FOX = 8
ROT = HD // 4
EPS = 1e-5
SCALE = HD ** -0.5
LAMBDA_INIT = 0.8 - 0.6
NEG = -1e30
E_ = 32
TOPK = 4
FE = 1024
PLE = 256
LIMIT = 7.0
ALPHA = 1.702
BR = 256
NPASS = (T * TOPK + E_ * (BR - 1)) // BR + 1
DQ0, DK0, DV0 = 0, 512, 1024
FQ0, FK0, FV0, FF0 = 1536, 2048, 2560, 3072
TWO_PI_1 = 6.28125
TWO_PI_2 = float(np.float32(2 * np.pi - 6.28125) // np.float32(2.0 ** -21) * 2.0 ** -21)
TWO_PI_3 = 2 * np.pi - 6.28125 - TWO_PI_2
PI_BELOW = 3.1415925
ROUND = 1.5 * 2.0 ** 23


class Steps:

    def __init__(self, eng, sem, start=0):
        self.eng, self.sem, self.start, self.n = eng, sem, start, 0

    def step(self, ins):
        self.n += 1
        ins.then_inc(self.sem, 1)
        self.eng.wait_ge(self.sem, self.start + self.n)


def settle(eng, sem):
    eng.sem_inc(sem("settled"), 1)


def phase_prepare(nc, dram, g, sem):
    with ExitStack() as ctx:
        def sb(name, shape, dt=F32):
            return ctx.enter_context(nc.sbuf_tensor(name, shape, dt))

        def ps(name, shape, dt=F32):
            return ctx.enter_context(nc.psum_tensor(name, shape, dt))

        x_in = [sb(f"x_in{j}", [P, D]) for j in range(2)]
        x_scaled = [sb(f"x_scaled{j}", [P, D]) for j in range(2)]
        squares = [sb(f"squares{j}", [P, D]) for j in range(2)]
        ssq = sb("ssq", [P, 2])
        rstd = sb("rstd", [P, 2])
        g_attn = sb("g_attn", [P, KD])
        pos_i = sb("pos_i", [P, T], I32)
        inv_freq = sb("inv_freq", [P, 1])
        ang = sb("ang", [P, T])
        turns = sb("turns", [P, T])
        reduced = sb("reduced", [P, T])
        lam_in = sb("lam_in", [P, 4, HD])
        lam_junk = sb("lam_junk", [P, HD])
        lam_s = sb("lam_s", [P, 2])
        lam_e = sb("lam_e", [P, 2])
        w_f = sb("w_f", [P, KD, N_FOX])
        b_f = sb("b_f", [N_FOX, 1])
        z = sb("z", [N_FOX, T])
        z_e = sb("z_e", [N_FOX, T])
        z_l = sb("z_l", [N_FOX, T])
        ones8 = sb("ones8", [N_FOX, T])
        turned = [ps(f"turned{j}", [P, KD, P]) for j in range(2)]
        z_ps = ps("z_ps", [N_FOX, T])
        xT, ident = g["xT"], g["ident"]
        block = ctx.enter_context(nc.Block())

        @block.sync
        def _(sp):
            sp.dma_start(ident[:, :], dram["c_ident"]).then_inc(sem("a_ident"), 16)
            sp.dma_start(g_attn[:, :], dram["g_attn"]).then_inc(sem("a_g"), 16)
            with sp.Fori(0, NT // 2) as i:
                for j in range(2):
                    sp.wait_ge(sem("a_x_free"), 2 * i + j + 1)
                    sp.dma_start(x_in[j][:, :], dram["x"][0, ds((2 * i + j) * P, P), :]).then_inc(sem(f"a_x{j}"), 16)
            sp.dma_start(pos_i[:, :], dram["positions"][0].partition_broadcast(P)).then_inc(sem("a_pos"), 16)
            sp.dma_start(inv_freq[:, :], dram["c_inv_freq"]).then_inc(sem("a_inv"), 16)
            sp.dma_start(w_f[:, :, :], dram["w_in"][0].rearrange("(k p) n -> p k n", p=P)[:, :, FF0:FF0 + N_FOX]).then_inc(sem("a_wf"), 16)
            sp.dma_start(b_f[:, :], dram["b_forget"]).then_inc(sem("a_bf"), 16)
            for n, name in enumerate(("lambda_q1", "lambda_k1", "lambda_q2", "lambda_k2")):
                sp.dma_start(lam_in[:, n, :], dram[name][0].partition_broadcast(P)).then_inc(sem("a_lam"), 16)
            sp.dma_start(g["mask"][:, :], dram["c_mask"]).then_inc(sem("a_mask"), 16)
            sp.dma_start(g["rot"][:, :], dram["c_rot"]).then_inc(sem("a_rot"), 16)
            sp.dma_start(g["gain"][:, 0:1], dram["g_subln"]).then_inc(sem("a_gain"), 16)
            sp.wait_ge(sem("a_negc"), 1)
            sp.dma_start(dram["negc"], z_e[:, :]).then_inc(sem("a_out"), 16)
            sp.wait_ge(sem("a_out"), 16)
            sp.wait_ge(sem("a_mask"), 16)
            sp.wait_ge(sem("a_rot"), 16)

        @block.scalar
        def _(act):
            with act.Fori(0, NT // 2) as i:
                for j in range(2):
                    act.wait_ge(sem(f"a_x{j}"), 16 * i + 16)
                    nc.scalar.activation(squares[j][:, :], x_in[j][:, :], ACT.Square,
                                         accum_out=ssq[:, j:j + 1]).then_inc(sem("a_ssq"), 1)
            act.wait_ge(sem("a_z"), 2)
            nc.scalar.activation(z_e[:, :], z_l[:, :], ACT.Exp).then_inc(sem("a_ze"), 1)
            act.wait_ge(sem("a_z"), 3)
            nc.scalar.activation(z_l[:, :], z_e[:, :], ACT.Ln).then_inc(sem("a_zl"), 1)
            act.wait_ge(sem("a_lams"), 2)
            nc.scalar.activation(lam_e[:, :], lam_s[:, :], ACT.Exp).then_inc(sem("a_lame"), 1)
            act.wait_ge(sem("a_red"), 1)
            nc.scalar.activation(g["sin"][:, :], reduced[:, :], ACT.Sin).then_inc(sem("a_sin"), 1)
            act.wait_ge(sem("a_red"), 2)
            nc.scalar.activation(g["cos"][:, :], reduced[:, :], ACT.Sin).then_inc(sem("a_sin"), 1)

        @block.gpsimd
        def _(pool):
            nc.gpsimd.memset(g["minus_half"][:, :], -0.5).then_inc(sem("a_half"), 1)
            pool.wait_ge(sem("a_half"), 1)
            with pool.Fori(0, NT // 2) as i:
                for j in range(2):
                    pool.wait_ge(sem("a_mean"), 2 * i + j + 1)
                    nc.gpsimd.tensor_tensor(rstd[:, j:j + 1], rstd[:, j:j + 1], g["minus_half"][:, 0:1], ALU.pow).then_inc(sem("a_rstd"), 1)

        @block.tensor
        def _(pe):
            pe.wait_ge(sem("a_ident"), 16)
            with pe.Fori(0, NT // 2) as i:
                for j in range(2):
                    pe.wait_ge(sem("a_xs"), 2 * i + j + 1)
                    pe.wait_ge(sem("a_turned_free"), 2 * i + j + 1)
                    for k in range(KD):
                        ins = nc.tensor.transpose(turned[j][:, k, :], x_scaled[j][:, k * P:(k + 1) * P], ident[:, :])
                    ins.then_inc(sem("a_turned"), 1)
            pe.wait_ge(sem("a_turned_free"), NT + 2)
            pe.wait_ge(sem("a_wf"), 16)
            for h in range(2):
                for k in range(KD):
                    ins = nc.tensor.matmul(z_ps[:, h * 512:(h + 1) * 512], w_f[:, k, :],
                                           xT[:, k, h * 512:(h + 1) * 512], start=k == 0, stop=k == KD - 1)
            ins.then_inc(sem("a_zps"), 1)

        @block.vector
        def _(dve):
            dve.sem_inc(sem("a_x_free"), 2)
            dve.sem_inc(sem("a_turned_free"), 2)
            dve.wait_ge(sem("a_g"), 16)
            with dve.Fori(0, NT // 2) as i:
                for j in range(2):
                    dve.wait_ge(sem("a_ssq"), 2 * i + j + 1)
                    nc.vector.tensor_scalar(rstd[:, j:j + 1], ssq[:, j:j + 1], 1.0 / D, EPS, ALU.mult, ALU.add).then_inc(sem("a_mean"), 1)
                for j in range(2):
                    dve.wait_ge(sem("a_rstd"), 2 * i + j + 1)
                    nc.vector.tensor_scalar(x_scaled[j][:, :], x_in[j][:, :], rstd[:, j:j + 1], None,
                                            ALU.mult).then_inc(sem("a_xs"), 1)
                    dve.wait_ge(sem("a_xs"), 2 * i + j + 1)
                    dve.sem_inc(sem("a_x_free"), 1)
                for j in range(2):
                    dve.wait_ge(sem("a_turned"), 2 * i + j + 1)
                    nc.vector.tensor_tensor(xT[:, :, ds((2 * i + j) * P, P)], turned[j][:, :, :],
                                            g_attn[:, :].unsqueeze(2).broadcast_to([P, KD, P]),
                                            ALU.mult).then_inc(sem("a_turned_free"), 1)
            own = Steps(dve, sem("a_dve"))
            dve.wait_ge(sem("a_zps"), 1)
            dve.wait_ge(sem("a_bf"), 16)
            own.step(nc.vector.memset(ones8[:, :], 1.0))
            nc.vector.tensor_scalar(z[:, :], z_ps[:, :], b_f[:, 0:1], None, ALU.add).then_inc(sem("a_z"), 1)
            dve.wait_ge(sem("a_z"), 1)
            nc.vector.scalar_tensor_tensor(z_l[:, :], z[:, :], -1.0, z[:, :], ALU.mult, ALU.min).then_inc(sem("a_z"), 1)
            dve.wait_ge(sem("a_ze"), 1)
            nc.vector.tensor_scalar(z_e[:, :], z_e[:, :], 1.0, None, ALU.add).then_inc(sem("a_z"), 1)
            dve.wait_ge(sem("a_zl"), 1)
            own.step(nc.vector.tensor_scalar(z[:, :], z[:, :], 0.0, None, ALU.min))
            own.step(nc.vector.tensor_tensor(z_l[:, :], z_l[:, :], z[:, :], ALU.subtract))
            nc.vector.tensor_tensor_scan(z_e[:, :], ones8[:, :], z_l[:, :], 0.0, ALU.mult, ALU.add).then_inc(sem("a_negc"), 1)
            dve.wait_ge(sem("a_lam"), 64)
            for n in range(2):
                nc.vector.tensor_tensor_reduce(lam_junk[:, :], lam_in[:, 2 * n, :], lam_in[:, 2 * n + 1, :], 1.0, 0.0,
                                               ALU.mult, ALU.add, lam_s[:, n:n + 1]).then_inc(sem("a_lams"), 1)
                dve.wait_ge(sem("a_lams"), n + 1)
            dve.wait_ge(sem("a_lame"), 1)
            own.step(nc.vector.tensor_tensor(g["neg_lam"][:, :], lam_e[:, 1:2], lam_e[:, 0:1], ALU.subtract))
            own.step(nc.vector.tensor_scalar(g["neg_lam"][:, :], g["neg_lam"][:, :], -LAMBDA_INIT, None, ALU.add))
            dve.wait_ge(sem("a_gain"), 16)
            own.step(nc.vector.tensor_scalar(g["gain"][:, :], g["gain"][:, :], 1.0 - LAMBDA_INIT, None, ALU.mult))
            dve.wait_ge(sem("a_pos"), 16)
            dve.wait_ge(sem("a_inv"), 16)
            own.step(nc.vector.tensor_copy(ang[:, :], pos_i[:, :]))
            own.step(nc.vector.tensor_scalar(ang[:, :], ang[:, :], inv_freq[:, 0:1], None, ALU.mult))
            for n, quarter in enumerate((0.0, 0.25)):
                own.step(nc.vector.tensor_scalar(turns[:, :], ang[:, :], float(1 / (2 * np.pi)), quarter, ALU.mult, ALU.add))
                own.step(nc.vector.tensor_scalar(turns[:, :], turns[:, :], ROUND, None, ALU.add))
                own.step(nc.vector.tensor_scalar(turns[:, :], turns[:, :], ROUND, None, ALU.subtract))
                if n:
                    dve.wait_ge(sem("a_sin"), 1)
                own.step(nc.vector.scalar_tensor_tensor(reduced[:, :], turns[:, :], -TWO_PI_1, ang[:, :], ALU.mult, ALU.add))
                own.step(nc.vector.scalar_tensor_tensor(reduced[:, :], turns[:, :], -TWO_PI_2, reduced[:, :], ALU.mult, ALU.add))
                own.step(nc.vector.scalar_tensor_tensor(reduced[:, :], turns[:, :], -TWO_PI_3, reduced[:, :], ALU.mult, ALU.add))
                own.step(nc.vector.tensor_scalar(reduced[:, :], reduced[:, :], quarter * 2 * np.pi, None, ALU.add))
                nc.vector.tensor_scalar(reduced[:, :], reduced[:, :], PI_BELOW, -PI_BELOW, ALU.min, ALU.max).then_inc(sem("a_red"), 1)


def phase_attention(nc, dram, g, sem, diff):
    tag = "d" if diff else "f"
    q0, k0, v0 = (DQ0, DK0, DV0) if diff else (FQ0, FK0, FV0)
    NH = 4
    with ExitStack() as ctx:
        def sb(name, shape, dt=F32):
            return ctx.enter_context(nc.sbuf_tensor(f"{tag}_{name}", shape, dt))

        def ps(name, shape, dt=F32):
            return ctx.enter_context(nc.psum_tensor(f"{tag}_{name}", shape, dt))

        def s(name):
            return sem(f"{tag}_{name}")

        w_qkv = [sb(f"w_qkv{j}", [P, 3, KD, P]) for j in range(2)]
        q_raw = sb("q_raw", [P, T])
        k_raw = sb("k_raw", [P, T])
        qT = sb("qT", [P, T]) if diff else q_raw
        kT = sb("kT", [P, T]) if diff else k_raw
        v = sb("v", [P, NT, P])
        prob = [[sb(f"prob{b}{m}", [P, T]) for m in range(2)] for b in range(2)]
        probT = [[sb(f"probT{b}{m}", [P, NT, P]) for m in range(1 if diff else 2)] for b in range(2)]
        stat = sb("stat", [P, NT, 2, 5])
        o_row = sb("o_row", [P, NT, P])
        o_sq = sb("o_sq", [P, NT, P])
        o_ss = sb("o_ss", [P, NT])
        if diff:
            zeros = sb("zeros", [P, D])
        if not diff:
            negc = [sb(f"negc{m}", [P, T]) for m in range(2)]
            negc_d = [sb(f"negc_d{m}", [P, NT, P]) for m in range(2)]
        score = [ps(f"score{m}", [P, T]) for m in range(2)]
        turned = ps("turned", [P, NT, P])
        o_ps = [ps(f"o_ps{b}", [P, P]) for b in range(2)]
        xT, mixT, ident = g["xT"], g["mixT"], g["ident"]
        nm = 1 if diff else 2
        wv = P // nm
        wr = dram["w_in"][0].rearrange("(k p) n -> p k n", p=P)
        block = ctx.enter_context(nc.Block())

        @block.sync
        def _(sp):
            with sp.Fori(0, NH // 2) as i:
                for j in range(2):
                    sp.wait_ge(s("w_free"), 2 * i + j + 1)
                    for n, c0 in enumerate((q0, k0, v0)):
                        sp.dma_start(w_qkv[j][:, n, :, :], wr[:, :, ds((2 * i + j) * P + c0, P)]).then_inc(s(f"w{j}"), 16)
                    if diff:
                        share = NPASS * BR // NH
                        sp.wait_ge(s("zeros"), 1)
                        sp.dma_start(dram["y"][ds((2 * i + j) * share, share), :].rearrange("(n p) d -> p n d", p=P),
                                     zeros[:, :].unsqueeze(1).broadcast_to([P, share // P, D])).then_inc(s("cleared"), 16)
                    if not diff:
                        sp.wait_ge(s("negc_free"), 2 * i + j + 1)
                        for m in range(2):
                            sp.dma_start(negc[m][:, :], dram["negc"][ds((2 * i + j) * 2 + m, 1), :].broadcast_to([P, T])
                                         ).then_inc(s("negc"), 16)
            if diff:
                sp.wait_ge(s("cleared"), 16 * NH)

        @block.tensor
        def _(pe):
            pe.sem_inc(s("w_free"), 2)
            with pe.Fori(0, NH // 2) as i:
                for j in range(2):
                    n_head = 2 * i + j
                    pe.wait_ge(s(f"w{j}"), 48 * i + 48)
                    for n in range(2):
                        pe.wait_ge(s("score_free"), (n_head + 1) * 2 * NT)
                        for h in range(2):
                            for k in range(KD):
                                ins = nc.tensor.matmul(score[n][:, h * 512:(h + 1) * 512], w_qkv[j][:, n, k, :],
                                                       xT[:, k, h * 512:(h + 1) * 512], start=k == 0, stop=k == KD - 1)
                        ins.then_inc(s("proj"), 1)
                    if diff:
                        for n, raw in enumerate((q_raw, k_raw)):
                            pe.wait_ge(s("raw"), 3 * n_head + n + 1)
                            for h in range(2):
                                ins = nc.tensor.matmul(score[n][:, h * 512:(h + 1) * 512], g["rot"][:, :],
                                                       raw[:, h * 512:(h + 1) * 512], start=True, stop=True)
                            ins.then_inc(s("rotated"), 1)
                    pe.wait_ge(s("turned_free"), n_head * (nm * NT + 1) + 1)
                    for t in range(NT):
                        for k in range(KD):
                            ins = nc.tensor.matmul(turned[:, t, :], xT[:, k, t * P:(t + 1) * P], w_qkv[j][:, 2, k, :],
                                                   start=k == 0, stop=k == KD - 1)
                    ins.then_inc(s("v"), 1)
                    pe.wait_ge(s("v"), n_head + 1)
                    pe.sem_inc(s("w_free"), 1)
                    if diff:
                        pe.wait_ge(s("roped"), 2 * n_head + 2)
                    else:
                        pe.wait_ge(s("raw"), 3 * n_head + 2)
                    for step in range(NT + 2):
                        if step < NT:
                            width = (step + 1) * P
                            for m in range(2):
                                if step:
                                    pe.wait_ge(s("score_free"), (n_head + 1) * 2 * NT + 2 * step - 1 + m)
                                for c in range(0, width, 512):
                                    ins = nc.tensor.matmul(score[m][:, c:min(c + 512, width)],
                                                           qT[m * HD:(m + 1) * HD, step * P:(step + 1) * P],
                                                           kT[m * HD:(m + 1) * HD, c:min(c + 512, width)],
                                                           start=True, stop=True)
                                ins.then_inc(s("score"), 1)
                        if step >= 2:
                            b = step - 2
                            pe.wait_ge(s("o_free"), n_head * NT + b + 1)
                            if b == 0:
                                pe.wait_ge(s("raw"), 3 * n_head + 3)
                            for m in range(nm):
                                pe.wait_ge(s("probT"), (n_head * NT + b) * nm + m + 1)
                                for kb in range(b + 1):
                                    ins = nc.tensor.matmul(o_ps[b % 2][:, m * wv:(m + 1) * wv], probT[b % 2][m][:, kb, :],
                                                           v[:, kb, m * wv:(m + 1) * wv], start=kb == 0, stop=kb == b)
                            ins.then_inc(s("o"), 1)
                        if 1 <= step <= NT:
                            b = step - 1
                            for m in range(nm):
                                pe.wait_ge(s("prob"), (n_head * NT + b) * nm + m + 1)
                                pe.wait_ge(s("turned_free"), n_head * (nm * NT + 1) + b * nm + m + 1)
                                if b == 0 and m == 0:
                                    pe.wait_ge(s("raw"), 3 * n_head + 3)
                                for kb in range(b + 1):
                                    ins = nc.tensor.transpose(turned[:, kb, :], prob[b % 2][m][:, kb * P:(kb + 1) * P], ident[:, :])
                                ins.then_inc(s("turned"), 1)
                    pe.wait_ge(s("o_row"), n_head + 1)
                    pe.wait_ge(s("turned_free"), n_head * (nm * NT + 1) + nm * NT + 1)
                    for t in range(NT):
                        ins = nc.tensor.transpose(turned[:, t, :], o_row[:, t, :], ident[:, :])
                    ins.then_inc(s("o_turned"), 1)

        @block.scalar
        def _(act):
            act.sem_inc(s("turned_free"), 1)
            with act.Fori(0, NH // 2) as i:
                for j in range(2):
                    n_head = 2 * i + j
                    act.wait_ge(s("proj"), 2 * n_head + 1)
                    nc.scalar.activation(q_raw[:, :], score[0][:, :], ACT.Copy, scale=SCALE).then_inc(s("raw"), 1)
                    act.wait_ge(s("proj"), 2 * n_head + 2)
                    nc.scalar.activation(k_raw[:, :], score[1][:, :], ACT.Copy).then_inc(s("raw"), 1)
                    act.wait_ge(s("v"), n_head + 1)
                    nc.scalar.activation(v[:, :, :], turned[:, :, :], ACT.Copy).then_inc(s("raw"), 1)
                    for step in range(NT + 1):
                        if step < NT:
                            width = (step + 1) * P
                            for m in range(2):
                                act.wait_ge(s("negmax"), (n_head * NT + step) * 2 + m + 1)
                                nc.scalar.activation(prob[step % 2][m][:, 0:width], prob[step % 2][m][:, 0:width], ACT.Exp,
                                                     bias=stat[:, step, m, 2:3], accum_out=stat[:, step, m, 3:4]
                                                     ).then_inc(s("exp") if diff else s("prob"), 1)
                        if step >= 1:
                            b = step - 1
                            for m in range(nm):
                                act.wait_ge(s("turned"), (n_head * NT + b) * nm + m + 1)
                                if b >= 2:
                                    act.wait_ge(s("o"), n_head * NT + b - 1)
                                nc.scalar.activation(probT[b % 2][m][:, 0:b + 1, :], turned[:, 0:b + 1, :], ACT.Copy
                                                     ).then_inc(s("probT"), 1)
                                act.wait_ge(s("probT"), (n_head * NT + b) * nm + m + 1)
                                act.sem_inc(s("turned_free"), 1)
                    act.wait_ge(s("o_turned"), n_head + 1)
                    out = mixT[:, ds(n_head + (0 if diff else N_DIFF), 1), :].rearrange("p a t -> p (a t)")
                    nc.scalar.activation(out, turned[:, :, :].rearrange("p a t -> p (a t)"), ACT.Copy,
                                         scale=g["gain"][:, 0:1] if diff else 1.0).then_inc(s("turned_free"), 1)

        @block.gpsimd
        def _(pool):
            if diff:
                nc.gpsimd.memset(zeros[:, :], 0.0).then_inc(s("zeros"), 1)
                with pool.Fori(0, NH // 2) as i:
                    for j in range(2):
                        n_head = 2 * i + j
                        for n, (raw, to) in enumerate(((q_raw, qT), (k_raw, kT))):
                            pool.wait_ge(s("raw"), 3 * n_head + n + 1)
                            nc.gpsimd.tensor_tensor(to[:, :], raw[:, :], g["cos"][:, :], ALU.mult).then_inc(s("cos"), 1)
                        pool.wait_ge(s("mean"), n_head + 1)
                        nc.gpsimd.tensor_tensor(o_ss[:, :], o_ss[:, :], g["minus_half"][:, :], ALU.pow).then_inc(s("rstd"), 1)
            else:
                pool.sem_inc(s("negc_free"), 1)
                with pool.Fori(0, NH // 2) as i:
                    for j in range(2):
                        n_head = 2 * i + j
                        for m in range(2):
                            pool.wait_ge(s("negc"), 32 * n_head + 32)
                            nc.gpsimd.tensor_tensor(negc_d[m][:, :, :], negc[m][:, :].rearrange("p (a t) -> p a t", t=P),
                                                    g["mask"][:, T - P:T].unsqueeze(1).broadcast_to([P, NT, P]),
                                                    ALU.add).then_inc(s("negc_d"), 1)

        @block.vector
        def _(dve):
            dve.sem_inc(s("score_free"), 2 * NT)
            dve.sem_inc(s("o_free"), 2)
            per = DVE_STEPS_DIFF if diff else DVE_STEPS_FOX
            with dve.Fori(0, NH // 2) as i:
                own = Steps(dve, s("dve"), i * per)
                for j in range(2):
                    n_head = 2 * i + j
                    if diff:
                        for n, to in enumerate((qT, kT)):
                            dve.wait_ge(s("rotated"), 2 * n_head + n + 1)
                            own.step(nc.vector.tensor_tensor(prob[0][n][:, :], score[n][:, :], g["sin"][:, :], ALU.mult))
                            dve.wait_ge(s("cos"), 2 * n_head + n + 1)
                            nc.vector.tensor_tensor(to[:, :], to[:, :], prob[0][n][:, :], ALU.add).then_inc(s("roped"), 1)
                    else:
                        dve.wait_ge(s("negc_d"), 2 * n_head + 2)

                    def normalise(b):
                        dve.wait_ge(s("exp"), (n_head * NT + b) * 2 + 2)
                        w = (b + 1) * P
                        own.step(nc.vector.reciprocal(stat[:, b, :, 4:5], stat[:, b, :, 3:4]))
                        own.step(nc.vector.tensor_tensor(stat[:, b, 1, 4:5], stat[:, b, 1, 4:5], g["neg_lam"][:, :], ALU.mult))
                        own.step(nc.vector.tensor_scalar(prob[b % 2][1][:, 0:w], prob[b % 2][1][:, 0:w],
                                                         stat[:, b, 1, 4:5], None, ALU.mult))
                        nc.vector.scalar_tensor_tensor(prob[b % 2][0][:, 0:w], prob[b % 2][0][:, 0:w], stat[:, b, 0, 4:5],
                                                       prob[b % 2][1][:, 0:w], ALU.mult, ALU.add).then_inc(s("prob"), 1)

                    def collect(b):
                        dve.wait_ge(s("o"), n_head * NT + b + 1)
                        if diff:
                            ins = nc.vector.tensor_copy(o_row[:, b, :], o_ps[b % 2][:, :])
                        else:
                            own.step(nc.vector.reciprocal(stat[:, b, :, 4:5], stat[:, b, :, 3:4]))
                            for m in range(2):
                                ins = nc.vector.tensor_scalar(o_row[:, b, m * wv:(m + 1) * wv], o_ps[b % 2][:, m * wv:(m + 1) * wv],
                                                              stat[:, b, m, 4:5], None, ALU.mult)
                                if m == 0:
                                    own.step(ins)
                        own.step(ins)
                        dve.sem_inc(s("o_free"), 1)

                    dve.wait_ge(s("turned_free"), n_head * (nm * NT + 1) + 1)
                    for step in range(NT + 2):
                        if diff and 1 <= step <= NT:
                            normalise(step - 1)
                        if step < NT:
                            width = (step + 1) * P
                            for m in range(2):
                                dve.wait_ge(s("score"), (n_head * NT + step) * 2 + m + 1)
                                if step >= 2:
                                    dve.wait_ge(s("turned"), (n_head * NT + step - 2) * nm + min(m, nm - 1) + 1)
                                p = prob[step % 2][m]
                                st = stat[:, step, m, :]
                                settle(dve, s)
                                if diff:
                                    own.step(nc.vector.tensor_tensor_reduce(
                                        p[:, 0:width], score[m][:, 0:width], g["mask"][:, T - width:T], 1.0, 3 * NEG,
                                        ALU.add, ALU.max, st[:, 0:1]))
                                    last = st[:, 0:1]
                                else:
                                    own.step(nc.vector.tensor_tensor_reduce(
                                        p[:, width - P:width], score[m][:, width - P:width], negc_d[m][:, step, :], 1.0, 3 * NEG,
                                        ALU.add, ALU.max, st[:, 0:1]))
                                    last = st[:, 0:1]
                                    if step:
                                        settle(dve, s)
                                        own.step(nc.vector.tensor_tensor_reduce(
                                            p[:, 0:width - P], score[m][:, 0:width - P], negc[m][:, 0:width - P], 1.0, st[:, 0:1],
                                            ALU.add, ALU.max, st[:, 1:2]))
                                        last = st[:, 1:2]
                                dve.sem_inc(s("score_free"), 1)
                                nc.vector.tensor_scalar(st[:, 2:3], last, -1.0, None, ALU.mult).then_inc(s("negmax"), 1)
                        if step >= 2:
                            collect(step - 2)
                    if diff:
                        own.step(nc.vector.tensor_tensor(o_sq[:, :, :], o_row[:, :, :], o_row[:, :, :], ALU.mult))
                        own.step(nc.vector.tensor_reduce(o_ss[:, :], o_sq[:, :, :], AX.X, ALU.add))
                        nc.vector.tensor_scalar(o_ss[:, :], o_ss[:, :], 1.0 / P, EPS, ALU.mult, ALU.add).then_inc(s("mean"), 1)
                        dve.wait_ge(s("rstd"), n_head + 1)
                        nc.vector.tensor_tensor(o_row[:, :, :], o_row[:, :, :],
                                                o_ss[:, :].unsqueeze(2).broadcast_to([P, NT, P]), ALU.mult).then_inc(s("o_row"), 1)
                    else:
                        dve.sem_inc(s("o_row"), 1)
                        dve.sem_inc(s("negc_free"), 1)
                assert own.n == per, own.n


DVE_STEPS_DIFF = 2 * (2 + 3 * NT + 2 * NT + NT + 2)
DVE_STEPS_FOX = 2 * (2 * NT + 2 * (NT - 1) + 3 * NT)


def phase_route(nc, dram, g, sem):
    with ExitStack() as ctx:
        def sb(name, shape, dt=F32):
            return ctx.enter_context(nc.sbuf_tensor(f"c_{name}", shape, dt))

        def ps(name, shape, dt=F32):
            return ctx.enter_context(nc.psum_tensor(f"c_{name}", shape, dt))

        def s(name):
            return sem(f"c_{name}")

        w_out = sb("w_out", [P, KD, D])
        w_r = sb("w_r", [P, KD, E_])
        b_r = sb("b_r", [P, E_])
        g_moe = sb("g_moe", [P, D])
        before = sb("before", [P, P])
        ones = sb("ones", [P, P])
        tokens = sb("tokens", [P, NT], I32)
        zeros = sb("zeros", [P, E_ * T // P], I32)
        experts = sb("experts", [P, E_])
        experts_i = sb("experts_i", [P, E_], I32)
        passes_i = sb("passes_i", [1, NPASS], I32)
        passes = sb("passes", [1, NPASS])
        stage = [sb(f"stage{j}", [P, KD, P]) for j in range(2)]
        x_in = [sb(f"x_in{j}", [P, D]) for j in range(2)]
        h1 = [sb(f"h1{j}", [P, D]) for j in range(2)]
        hn = [sb(f"hn{j}", [P, D]) for j in range(2)]
        hT = [sb(f"hT{j}", [P, KD, P]) for j in range(2)]
        squares = [sb(f"squares{j}", [P, D]) for j in range(2)]
        ssq = sb("ssq", [P, 2])
        rstd = sb("rstd", [P, 2])
        logits = sb("logits", [P, E_])
        top = sb("top", [P, 8])
        top_i = sb("top_i", [P, 8], U32)
        top_f = sb("top_f", [P, 8])
        neg_top = sb("neg_top", [P, 1])
        gsum = sb("gsum", [P, 1])
        onehot = sb("onehot", [P, NT, TOPK, E_])
        chosen = sb("chosen", [P, E_])
        chosen_sum = sb("chosen_sum", [P, E_])
        place = sb("place", [P, NT, TOPK])
        place_e = sb("place_e", [P, TOPK, E_])
        lists = sb("lists", [P, NT, TOPK])
        lists_i = sb("lists_i", [P, NT, TOPK], I32)
        first = sb("first", [P, NT, TOPK])
        tmp4 = sb("tmp4", [P, TOPK])
        n_pass = sb("n_pass", [P, E_])
        n_tmp = sb("n_tmp", [P, E_])
        pass_end = sb("pass_end", [P, E_])
        pass_start = sb("pass_start", [P, E_])
        counts = sb("counts", [P, E_])
        ones32 = sb("ones32", [P, E_])
        big = sb("big", [P, NT * TOPK, E_])
        in_pass = sb("in_pass", [1, NPASS, E_])
        in_tmp = sb("in_tmp", [1, NPASS, E_])
        tab = sb("tab", [1, 3, NPASS])
        tab_t = sb("tab_t", [1, NPASS])
        acc = [ps(f"acc{j}", [P, D]) for j in range(2)]
        turned = ps("turned", [P, KD, P])
        rt_ps = ps("rt_ps", [P, E_])
        pl_ps = ps("pl_ps", [P, E_])
        ident, gates, dense = g["ident"], g["gates"], g["dense"]
        block = ctx.enter_context(nc.Block())
        H = KD // 2

        @block.sync
        def _(sp):
            wr = dram["w_out"][0].rearrange("(k p) n -> p k n", p=P)
            for k in range(0, KD, 2):
                sp.dma_start(w_out[:, k:k + 2, :], wr[:, k:k + 2, :]).then_inc(s("w_out"), 16)
            sp.dma_start(w_r[:, :, :], dram["w_router"][0].rearrange("(k p) n -> p k n", p=P)).then_inc(s("w_r"), 16)
            sp.dma_start(b_r[:, :], dram["b_router"][0].partition_broadcast(P)).then_inc(s("w_r"), 16)
            sp.dma_start(g_moe[:, :], dram["g_moe"][0].partition_broadcast(P)).then_inc(s("w_r"), 16)
            sp.dma_start(before[:, :], dram["c_before"]).then_inc(s("w_r"), 16)
            sp.dma_start(tokens[:, :], dram["c_tokens"]).then_inc(s("tokens"), 16)
            sp.wait_ge(s("zeros"), 1)
            sp.dma_start(dram["lists"].rearrange("(p n) a -> p (n a)", p=P), zeros[:, :]).then_inc(s("cleared"), 16)
            with sp.Fori(0, NT // 2) as i:
                for j in range(2):
                    sp.wait_ge(s("x_free"), 2 * i + j + 1)
                    sp.dma_start(x_in[j][:, :], dram["x"][0, ds((2 * i + j) * P, P), :]).then_inc(s(f"x{j}"), 16)
            sp.wait_ge(s("cleared"), 16)

        @block.gpsimd
        def _(pool):
            nc.gpsimd.memset(zeros[:, :], 0).then_inc(s("zeros"), 1)
            nc.gpsimd.iota(experts_i[:, :], pattern=[[1, E_]], base=0, channel_multiplier=0).then_inc(s("iota"), 1)
            nc.gpsimd.iota(passes_i[:, :], pattern=[[1, NPASS]], base=0, channel_multiplier=0).then_inc(s("iota"), 1)
            nc.gpsimd.memset(ones[:, :], 1.0).then_inc(s("ones"), 1)
            with pool.Fori(0, NT // 2) as i:
                for j in range(2):
                    pool.wait_ge(s("stage_free"), 2 * i + j + 1)
                    nc.gpsimd.tensor_copy(stage[j][:, :, :], g["mixT"][:, :, ds((2 * i + j) * P, P)]).then_inc(s("stage"), 1)
                for j in range(2):
                    pool.wait_ge(s("mean"), 2 * i + j + 1)
                    nc.gpsimd.tensor_tensor(rstd[:, j:j + 1], rstd[:, j:j + 1], g["minus_half"][:, 0:1], ALU.pow).then_inc(s("rstd"), 1)
            pool.wait_ge(s("cleared"), 16)
            pool.wait_ge(s("tokens"), 16)
            pool.wait_ge(s("lists"), 1)
            for t in range(NT):
                for k in range(TOPK):
                    nc.gpsimd.indirect_dma_start(
                        out=dram["lists"], out_offset=bass.IndirectOffsetOnAxis(ap=lists_i[:, t, k:k + 1], axis=0),
                        in_=tokens[:, t:t + 1], in_offset=None).then_inc(s("scattered"), 16)
            pool.wait_ge(s("scattered"), 16 * NT * TOPK)

        @block.tensor
        def _(pe):
            pe.sem_inc(s("stage_free"), 2)
            pe.wait_ge(s("w_out"), 64)
            pe.wait_ge(s("w_r"), 64)
            pe.wait_ge(s("ones"), 1)
            with pe.Fori(0, NT // 2) as i:
                for j in range(2):
                    t = 2 * i + j
                    pe.wait_ge(s("stage"), t + 1)
                    pe.wait_ge(s("x_free"), t + 1)
                    for c in range(2):
                        for k in range(KD):
                            ins = nc.tensor.matmul(acc[j][:, c * 512:(c + 1) * 512], stage[j][:, k, :],
                                                   w_out[:, k, c * 512:(c + 1) * 512], start=k == 0, stop=k == KD - 1)
                    ins.then_inc(s("acc"), 1)
                    pe.wait_ge(s("acc"), t + 1)
                    pe.sem_inc(s("stage_free"), 1)
                for j in range(2):
                    t = 2 * i + j
                    pe.wait_ge(s("hn"), t + 1)
                    pe.wait_ge(s("turned_free"), t + 1)
                    for k in range(KD):
                        ins = nc.tensor.transpose(turned[:, k, :], hn[j][:, k * P:(k + 1) * P], ident[:, :])
                    ins.then_inc(s("turned"), 1)
                    pe.wait_ge(s("hT"), t + 1)
                    for k in range(KD):
                        ins = nc.tensor.matmul(rt_ps[:, :], hT[j][:, k, :], w_r[:, k, :], start=k == 0, stop=k == KD - 1)
                    ins.then_inc(s("logits"), 1)
                    pe.wait_ge(s("chosen"), t + 1)
                    nc.tensor.matmul(pl_ps[:, :], before[:, :], chosen[:, :], start=True, stop=False)
                    nc.tensor.matmul(pl_ps[:, :], ones[:, :], chosen_sum[:, :], start=False, stop=True).then_inc(s("place"), 1)
            pe.wait_ge(s("chosen"), NT + 1)
            nc.tensor.matmul(pl_ps[:, :], ones[:, :], chosen_sum[:, :], start=True, stop=True).then_inc(s("place"), 1)

        @block.scalar
        def _(act):
            for j in range(2):
                act.sem_inc(s(f"h1_out{j}"), 16)
                act.sem_inc(s(f"hn_out{j}"), 16)
            with act.Fori(0, NT // 2) as i:
                for j in range(2):
                    t = 2 * i + j
                    act.wait_ge(s("h1"), t + 1)
                    nc.scalar.activation(squares[j][:, :], h1[j][:, :], ACT.Square, accum_out=ssq[:, j:j + 1]).then_inc(s("ssq"), 1)
                    act.dma_start(dram["h1"][ds(t * P, P), :], h1[j][:, :]).then_inc(s(f"h1_out{j}"), 16)
                for j in range(2):
                    t = 2 * i + j
                    act.wait_ge(s("hn"), t + 1)
                    act.dma_start(dram["hn"][ds(t * P, P), :], hn[j][:, :]).then_inc(s(f"hn_out{j}"), 16)
                    act.wait_ge(s("neg_top"), t + 1)
                    nc.scalar.activation(gates[:, ds(t * TOPK, TOPK)], top[:, 0:TOPK], ACT.Exp, bias=neg_top[:, 0:1],
                                         accum_out=gsum[:, 0:1]).then_inc(s("gates"), 1)
            for j in range(2):
                act.wait_ge(s(f"h1_out{j}"), 16 * (NT // 2) + 16)
                act.wait_ge(s(f"hn_out{j}"), 16 * (NT // 2) + 16)

        @block.vector
        def _(dve):
            dve.sem_inc(s("x_free"), 2)
            dve.sem_inc(s("turned_free"), 1)
            nc.vector.memset(chosen_sum[:, :], 0.0).then_inc(s("init"), 1)
            nc.vector.memset(ones32[:, :], 1.0).then_inc(s("init"), 1)
            dve.wait_ge(s("iota"), 2)
            nc.vector.tensor_copy(experts[:, :], experts_i[:, :]).then_inc(s("init"), 1)
            nc.vector.tensor_copy(passes[:, :], passes_i[:, :]).then_inc(s("init"), 1)
            dve.wait_ge(s("init"), 4)
            dve.wait_ge(s("w_r"), 64)
            per = 2 * (3 + 1 + TOPK + 4 + 5)
            with dve.Fori(0, NT // 2) as i:
                own = Steps(dve, s("dve"), i * per)
                for j in range(2):
                    t = 2 * i + j
                    dve.wait_ge(s("acc"), t + 1)
                    dve.wait_ge(s(f"x{j}"), 16 * i + 16)
                    dve.wait_ge(s(f"h1_out{j}"), 16 * i + 16)
                    dve.wait_ge(s(f"hn_out{j}"), 16 * i + 16)
                    nc.vector.tensor_tensor(h1[j][:, :], acc[j][:, :], x_in[j][:, :], ALU.add).then_inc(s("h1"), 1)
                    dve.wait_ge(s("h1"), t + 1)
                    dve.sem_inc(s("x_free"), 1)
                    dve.wait_ge(s("ssq"), t + 1)
                    nc.vector.tensor_scalar(rstd[:, j:j + 1], ssq[:, j:j + 1], 1.0 / D, EPS, ALU.mult, ALU.add).then_inc(s("mean"), 1)
                for j in range(2):
                    t = 2 * i + j
                    dve.wait_ge(s("rstd"), t + 1)
                    nc.vector.scalar_tensor_tensor(hn[j][:, :], h1[j][:, :], rstd[:, j:j + 1], g_moe[:, :], ALU.mult, ALU.mult).then_inc(s("hn"), 1)
                for j in range(2):
                    t = 2 * i + j
                    dve.wait_ge(s("turned"), t + 1)
                    nc.vector.tensor_copy(hT[j][:, :, :], turned[:, :, :]).then_inc(s("hT"), 1)
                    dve.wait_ge(s("hT"), t + 1)
                    dve.sem_inc(s("turned_free"), 1)
                    dve.wait_ge(s("logits"), t + 1)
                    own.step(nc.vector.tensor_tensor(logits[:, :], rt_ps[:, :], b_r[:, :], ALU.add))
                    settle(dve, s)
                    own.step(nc.vector.max(top[:, :], logits[:, :]))
                    settle(dve, s)
                    own.step(nc.vector.max_index(top_i[:, :], top[:, :], logits[:, :]))
                    nc.vector.tensor_scalar(neg_top[:, :], top[:, 0:1], -1.0, None, ALU.mult).then_inc(s("neg_top"), 1)
                    own.step(nc.vector.tensor_copy(top_f[:, :], top_i[:, :]))
                    for k in range(TOPK):
                        own.step(nc.vector.tensor_scalar(onehot[:, ds(t, 1), k, :].rearrange("p a e -> p (a e)"), experts[:, :],
                                                         top_f[:, k:k + 1], None, ALU.is_equal))
                    oh = onehot[:, ds(t, 1), :, :].rearrange("p a k e -> p (a k) e")
                    settle(dve, s)
                    nc.vector.tensor_reduce(chosen[:, :], oh.rearrange("p k e -> p e k"), AX.X, ALU.add).then_inc(s("chosen"), 1)
                    dve.wait_ge(s("gates"), t + 1)
                    gt = gates[:, ds(t * TOPK, TOPK)]
                    own.step(nc.vector.reciprocal(gsum[:, :], gsum[:, :]))
                    own.step(nc.vector.tensor_scalar(gt, gt, gsum[:, 0:1], None, ALU.mult))
                    own.step(nc.vector.tensor_tensor(place_e[:, :, :], oh, gt.unsqueeze(2).broadcast_to([P, TOPK, E_]), ALU.mult))
                    settle(dve, s)
                    own.step(nc.vector.tensor_reduce(dense[:, ds(t, 1), :].rearrange("p a e -> p (a e)"),
                                                     place_e[:, :, :].rearrange("p k e -> p e k"), AX.X, ALU.add))
                    dve.wait_ge(s("place"), t + 1)
                    own.step(nc.vector.tensor_copy(n_tmp[:, :], pl_ps[:, :]))
                    own.step(nc.vector.tensor_tensor(place_e[:, :, :], oh, n_tmp[:, :].unsqueeze(1).broadcast_to([P, TOPK, E_]), ALU.mult))
                    settle(dve, s)
                    own.step(nc.vector.tensor_reduce(place[:, ds(t, 1), :].rearrange("p a k -> p (a k)"),
                                                     place_e[:, :, :], AX.X, ALU.add))
                    own.step(nc.vector.tensor_tensor(chosen_sum[:, :], chosen_sum[:, :], chosen[:, :], ALU.add))
                    own.step(nc.vector.tensor_copy(lists[:, ds(t, 1), :].rearrange("p a k -> p (a k)"), top_f[:, 0:TOPK]))
                assert own.n == per, own.n
            own = Steps(dve, s("dve"), (NT // 2) * per)
            own.step(nc.vector.scalar_tensor_tensor(lists[:, :, :], lists[:, :, :], float(T), place[:, :, :], ALU.mult, ALU.add))
            nc.vector.tensor_copy(lists_i[:, :, :], lists[:, :, :]).then_inc(s("lists"), 1)
            dve.sem_inc(s("chosen"), 1)
            dve.wait_ge(s("place"), NT + 1)
            own.step(nc.vector.tensor_copy(counts[:, :], pl_ps[:, :]))
            own.step(nc.vector.tensor_scalar(n_pass[:, :], counts[:, :], 0.0, None, ALU.is_gt))
            for b in range(1, T // BR):
                own.step(nc.vector.tensor_scalar(n_tmp[:, :], counts[:, :], float(b * BR), None, ALU.is_gt))
                own.step(nc.vector.tensor_tensor(n_pass[:, :], n_pass[:, :], n_tmp[:, :], ALU.add))
            own.step(nc.vector.tensor_tensor_scan(pass_end[:, :], ones32[:, :], n_pass[:, :], 0.0, ALU.mult, ALU.add))
            own.step(nc.vector.tensor_tensor(pass_start[:, :], pass_end[:, :], n_pass[:, :], ALU.subtract))
            own.step(nc.vector.tensor_tensor(big[:, :, :], onehot[:, :, :, :].rearrange("p t k e -> p (t k) e"),
                                             pass_start[:, :].unsqueeze(1).broadcast_to([P, NT * TOPK, E_]), ALU.mult))
            own.step(nc.vector.tensor_reduce(first[:, :, :].rearrange("p t k -> p (t k)"), big[:, :, :], AX.X, ALU.add))
            own.step(nc.vector.scalar_tensor_tensor(first[:, :, :], first[:, :, :], float(BR), place[:, :, :], ALU.mult, ALU.add))
            own.step(nc.vector.tensor_copy(g["y_row"][:, :], first[:, :, :].rearrange("p t k -> p (t k)")))
            p_b = passes[0:1, :].unsqueeze(2).broadcast_to([1, NPASS, E_])

            def over(x):
                return x[0:1, :].unsqueeze(1).broadcast_to([1, NPASS, E_])

            own.step(nc.vector.tensor_tensor(in_pass[:, :, :], p_b, over(pass_start), ALU.is_ge))
            own.step(nc.vector.tensor_tensor(in_tmp[:, :, :], p_b, over(pass_end), ALU.is_ge))
            own.step(nc.vector.tensor_tensor(in_pass[:, :, :], in_pass[:, :, :], in_tmp[:, :, :], ALU.subtract))
            for n, values in enumerate((experts, pass_start, counts)):
                own.step(nc.vector.tensor_tensor(in_tmp[:, :, :], in_pass[:, :, :], over(values), ALU.mult))
                own.step(nc.vector.tensor_reduce(tab[:, n, :], in_tmp[:, :, :], AX.X, ALU.add))
            own.step(nc.vector.tensor_tensor(tab_t[:, :], passes[0:1, :], tab[:, 1, :], ALU.subtract))
            own.step(nc.vector.tensor_scalar(tab_t[:, :], tab_t[:, :], float(BR), None, ALU.mult))
            own.step(nc.vector.tensor_tensor(tab[:, 2, :], tab[:, 2, :], tab_t[:, :], ALU.subtract))
            own.step(nc.vector.tensor_scalar(tab[:, 2, :], tab[:, 2, :], 0.0, None, ALU.max))
            own.step(nc.vector.scalar_tensor_tensor(tab[:, 1, :], tab[:, 0, :], float(T), tab_t[:, :], ALU.mult, ALU.add))
            own.step(nc.vector.tensor_scalar(tab[:, 1, :], tab[:, 1, :], float(E_ * T - BR), None, ALU.min))
            own.step(nc.vector.tensor_copy(g["table"][:, 0:3 * NPASS], tab[:, :, :].rearrange("p a n -> p (a n)")))
            own.step(nc.vector.tensor_copy(g["table"][:, 3 * NPASS:], pass_end[0:1, E_ - 1:E_]))


def phase_experts(nc, dram, g, sem):
    with ExitStack() as ctx:
        def sb(name, shape, dt=F32):
            return ctx.enter_context(nc.sbuf_tensor(f"e_{name}", shape, dt))

        def ps(name, shape, dt=F32):
            return ctx.enter_context(nc.psum_tensor(f"e_{name}", shape, dt))

        def s(name):
            return sem(f"e_{name}")

        W = 512
        G1, G2 = 2 * FE // W, D // W
        KH = KD // 2
        C = 2 * (G1 + G2)
        AHEAD = 3
        RAW = C // 2
        WF = W // 2
        FT = WF // P
        NF = FE // P
        PB = BR // P
        raw = [sb(f"raw{c}", [P, KH, W]) for c in range(RAW)]
        hi = [sb(f"hi{n}", [P, KH, W], F32R) for n in range(AHEAD + 1)]
        lo = [sb(f"lo{n}", [P, KH, W], F32R) for n in range(AHEAD + 1)]
        b1 = sb("b1", [2 * E_, 2 * FE], F32R)
        sel = sb("sel", [2 * E_, P], F32R)
        rows_i = [sb(f"rows_i{b}", [P, 1], I32) for b in range(PB)]
        x_rows = sb("x_rows", [P, PB, D])
        xT_hi = sb("xT_hi", [P, KD, BR], F32R)
        xT_lo = sb("xT_lo", [P, KD, BR], F32R)
        gate = sb("gate", [P, PB, WF])
        lin = sb("lin", [P, PB, WF])
        sig = sb("sig", [P, PB, WF])
        act_rows = [sb(f"act_rows{n}", [P, PB, WF]) for n in range(2)]
        act_hi = sb("act_hi", [P, NF, PB, P], F32R)
        act_lo = sb("act_lo", [P, NF, PB, P], F32R)
        y = sb("y", [P, PB * D])
        warm = sb("warm", [P, 1])
        prod = [ps(f"prod{n}", [P, PB, W]) for n in range(2)]
        act_ps = [ps(f"act_ps{n}", [P, FT, PB, P]) for n in range(2)]
        turned = ps("turned", [P, KD, P])
        ident, table = g["ident"], g["table"]
        block = ctx.enter_context(nc.Block())

        share = {"dve": slice(0, 5 * W // 8), "pool": slice(5 * W // 8, W)}

        def expert(eng, p):
            return eng.value_load(table[0:1, ds(p, 1)], min_val=0, max_val=E_ - 1)

        def first_row(eng, p):
            return eng.value_load(table[0:1, ds(p + NPASS, 1)], min_val=0, max_val=E_ * T - BR)

        def rows_left(eng, p):
            return eng.value_load(table[0:1, ds(p + 2 * NPASS, 1)], min_val=0, max_val=T)

        def split_done(eng, p, c):
            for who in share:
                eng.wait_ge(s(f"lo_{who}"), C * (p + 1) + c + 1)

        def done(eng, p, c):
            eng.wait_ge(s("done"), C * (p + 1) + c + 1)

        def low(eng, vec, who, p, c):
            eng.wait_ge(s("hi"), C * p + c + 1)
            slot, cols = c % (AHEAD + 1), share[who]
            vec.tensor_tensor(lo[slot][:, :, cols], raw[c % RAW][:, :, cols], hi[slot][:, :, cols].bitcast(F32),
                              ALU.subtract).then_inc(s(f"lo_{who}"), 1)

        @block.sync
        def _(sp):
            for part in range(2):
                sp.dma_start(y[part * E_:(part + 1) * E_, :], dram["b_e1"][0]).then_inc(s("b1"), 16)
            w1 = dram["w_e1"][0].rearrange("e (k p) n -> p e k n", p=P)
            w2 = dram["w_e2"][0].rearrange("e (k p) n -> p e k n", p=P)
            with sp.Fori(0, NPASS - 1) as p:
                with sp.If(rows_left(sp, p) > 0):
                    e = expert(sp, p)
                    for c in range(C):
                        split_done(sp, p - (c < RAW), (c - RAW) % C)
                        if c < 2 * G1:
                            src, half, n = w1, c % 2, c // 2
                        else:
                            src, half, n = w2, (c - 2 * G1) // G2, (c - 2 * G1) % G2
                        sp.dma_start(raw[c % RAW][:, :, :],
                                     src[:, ds(e, 1), half * KH:(half + 1) * KH, n * W:(n + 1) * W].rearrange("p e k n -> p (e k) n")
                                     ).then_inc(s(f"w{c}"), 16)

        @block.gpsimd
        def _(pool):
            pool.sem_inc(s("lo_pool"), C)

            def fetch_numbers(start):
                for b in range(PB):
                    pool.dma_start(rows_i[b][:, :], dram["lists"][ds(start + b * P, P), :]).then_inc(s(f"rows{b}"), 16)

            def gather(n):
                for b in range(PB):
                    pool.wait_ge(s(f"rows{b}"), 16 * n + 16)
                    pool.wait_ge(s("x_turned"), PB * n + b + 1)
                    settle(pool, s)
                    nc.gpsimd.indirect_dma_start(out=x_rows[:, b, :], out_offset=None, in_=dram["hn"],
                                                 in_offset=bass.IndirectOffsetOnAxis(ap=rows_i[b][:, 0:1], axis=0)
                                                 ).then_inc(s(f"x{b}"), 16)

            def low_pool(p, c):
                low(pool, nc.gpsimd, "pool", p, c)

            fetch_numbers(first_row(pool, 0))
            gather(0)
            for c in range(AHEAD):
                low_pool(0, c)
            with pool.Fori(0, NPASS - 1) as p:
                with pool.If(rows_left(pool, p) > 0):
                    for b in range(PB):
                        pool.wait_ge(s(f"x{b}"), 16 * p + 16)
                    fetch_numbers(first_row(pool, p + 1))
                    for c in range(AHEAD, C):
                        low_pool(p, c)
                        if c == 5:
                            gather(p + 1)
                    with pool.If(rows_left(pool, p + 1) > 0):
                        for c in range(AHEAD):
                            low_pool(p + 1, c)

        @block.tensor
        def _(pe):
            pe.sem_inc(s("done"), C)
            pe.sem_inc(s("x_turned"), PB)
            pe.sem_inc(s("act_turned"), G1)

            def turn(n, b):
                pe.wait_ge(s(f"x{b}"), 16 * n + 16)
                pe.wait_ge(s("xT"), PB * n + b + 1)
                for k in range(KD):
                    ins = nc.tensor.transpose(turned[:, k, :], x_rows[:, b, k * P:(k + 1) * P], ident[:, :])
                ins.then_inc(s("x_turned"), 1)

            def turn_act(p, j, blocks):
                pe.wait_ge(s("act_rows"), G1 * p + G1 + j + 1)
                pe.wait_ge(s("act"), G1 * p + G1 + j - 1)
                for b in range(blocks):
                    for i in range(FT):
                        ins = nc.tensor.transpose(act_ps[j % 2][:, i, b, :], act_rows[j % 2][:, b, i * P:(i + 1) * P], ident[:, :])
                ins.then_inc(s("act_turned"), 1)

            def up(p, c, blocks):
                j, half = c // 2, c % 2
                split_done(pe, p, c)
                if half == 0:
                    if j < 2:
                        pe.wait_ge(s("y_free"), G2 * p + j + 1)
                    else:
                        pe.wait_ge(s("gate"), G1 * p + j - 1)
                        pe.wait_ge(s("lin"), G1 * p + j - 1)
                w_hi, w_lo = hi[c % (AHEAD + 1)], lo[c % (AHEAD + 1)]
                for b in range(blocks):
                    if half == 0:
                        nc.tensor.matmul(prod[j % 2][:, b, :], sel[:, :], b1[:, j * W:(j + 1) * W], start=True, stop=False)
                    for k in range(KH):
                        for i, (x, w) in enumerate(((xT_hi, w_hi), (xT_hi, w_lo), (xT_lo, w_hi))):
                            ins = nc.tensor.matmul(prod[j % 2][:, b, :], x[:, half * KH + k, b * P:(b + 1) * P], w[:, k, :],
                                                   start=False, stop=half == 1 and k == KH - 1 and i == 2)
                ins.then_inc(s("done"), 1)

            def down(p, n, blocks):
                c = 2 * G1 + n
                half, j = n // G2, n % G2
                split_done(pe, p, c)
                if half == 0:
                    pe.wait_ge(s("gate"), G1 * p + G1 - G2 + j + 1)
                    pe.wait_ge(s("lin"), G1 * p + G1 - G2 + j + 1)
                w_hi, w_lo = hi[c % (AHEAD + 1)], lo[c % (AHEAD + 1)]
                pe.wait_ge(s("act"), G1 * p + G1 + (half + 1) * G1 // 2)
                for b in range(blocks):
                    for k in range(KH):
                        for i, (a, w) in enumerate(((act_hi, w_hi), (act_hi, w_lo), (act_lo, w_hi))):
                            ins = nc.tensor.matmul(prod[j][:, b, :], a[:, half * KH + k, b, :], w[:, k, :],
                                                   start=half == 0 and k == 0 and i == 0,
                                                   stop=half == 1 and k == KH - 1 and i == 2)
                ins.then_inc(s("done"), 1)

            for b in range(PB):
                turn(0, b)
            with pe.Fori(0, NPASS - 1) as p:
                rows = rows_left(pe, p)

                def body(blocks):
                    pe.wait_ge(s("xT"), PB * p + PB + 1)
                    pe.wait_ge(s("sel"), 2 * p + 2)
                    for j in range(G1):
                        for half in range(2):
                            up(p, 2 * j + half, blocks)
                        if 0 < j < G1 - 1:
                            turn_act(p, j - 1, blocks)
                    turn(p + 1, 0)
                    down(p, 0, blocks)
                    turn_act(p, 2, blocks)
                    turn_act(p, 3, blocks)
                    down(p, 1, blocks)
                    turn(p + 1, 1)
                    down(p, 2, blocks)
                    down(p, 3, blocks)

                with pe.If(rows > 0):
                    with pe.If(rows > P):
                        body(2)
                    with pe.Else():
                        body(1)

        @block.scalar
        def _(act):
            act.sem_inc(s("y_out"), 16)

            def high(p, c):
                act.wait_ge(s(f"w{c}"), 16 * p + 16)
                done(act, p, c - AHEAD - 1)
                nc.scalar.activation(hi[c % (AHEAD + 1)][:, :, :], raw[c % RAW][:, :, :], ACT.Copy).then_inc(s("hi"), 1)

            def high_x(n, b):
                act.wait_ge(s("x_turned"), PB * n + PB + b + 1)
                nc.scalar.activation(xT_hi[:, :, b * P:(b + 1) * P], turned[:, :, :], ACT.Copy).then_inc(s("xT_hi"), 1)

            act.wait_ge(s("b1_whole"), 1)
            nc.scalar.activation(b1[:, :], y[0:2 * E_, :], ACT.Copy).then_inc(s("b1_hi"), 1)
            act.wait_ge(s("b1_split"), 1)
            act.sem_inc(s("y_free"), G2)
            for b in range(PB):
                high_x(0, b)
            for c in range(AHEAD + 1):
                high(0, c)
            with act.Fori(0, NPASS - 1) as p:
                rows = rows_left(act, p)
                y_rows = dram["y"][ds(p * BR, BR), :].rearrange("(b q) d -> q b d", q=P)

                def features(blocks, j):
                    act.wait_ge(s("gate"), G1 * p + j + 1)
                    nc.scalar.activation(sig[:, 0:blocks, :], gate[:, 0:blocks, :], ACT.Sigmoid, scale=ALPHA
                                         ).then_inc(s("sig"), 1)

                def high_act(blocks, j):
                    act.wait_ge(s("act_turned"), G1 * p + G1 + j + 1)
                    nc.scalar.activation(act_hi[:, FT * j:FT * (j + 1), 0:blocks, :], act_ps[j % 2][:, :, 0:blocks, :], ACT.Copy
                                         ).then_inc(s("act_hi"), 1)

                def y_out(blocks, c):
                    done(act, p, 2 * G1 + G2 + c)
                    nc.scalar.activation(y[:, :].rearrange("q (b d) -> q b d", b=PB)[:, 0:blocks, c * W:(c + 1) * W],
                                         prod[c][:, 0:blocks, :], ACT.Copy).then_inc(s("y_free"), 1)

                def body(blocks):
                    nc.scalar.activation(warm[:, :], ident[:, 0:1], ACT.Sigmoid).then_inc(s("warm"), 1)
                    high(p, 4)
                    for j in range(G1):
                        features(blocks, j)
                        if 0 < j < G1 - 1:
                            high_act(blocks, j - 1)
                        high(p, 2 * j + 5)
                        if j < G1 - 1:
                            high(p, 2 * j + 6)
                    high_x(p + 1, 0)
                    high_act(blocks, 2)
                    high_act(blocks, 3)

                def tail(blocks, last):
                    if not last:
                        high(p + 1, 0)
                        high(p + 1, 1)
                    high_x(p + 1, 1)
                    act.wait_ge(s("y_out"), 16 * p + 16)
                    y_out(blocks, 0)
                    if not last:
                        high(p + 1, 2)
                        high(p + 1, 3)
                    y_out(blocks, 1)
                    act.wait_ge(s("y_free"), G2 * p + 2 * G2)
                    act.dma_start(y_rows[:, 0:blocks, :], y[:, 0:blocks * D].rearrange("q (b d) -> q b d", b=blocks)
                                  ).then_inc(s("y_out"), 16)

                with act.If(rows > 0):
                    rows_next = rows_left(act, p + 1)
                    for big in (True, False):
                        with (act.If(rows > P) if big else act.If(rows <= P)):
                            body(1 + big)
                            for last in (False, True):
                                with (act.If(rows_next == 0) if last else act.If(rows_next > 0)):
                                    tail(1 + big, last)
            n = act.value_load(table[0:1, 3 * NPASS:3 * NPASS + 1], min_val=1, max_val=NPASS)
            act.wait_ge(s("y_out"), 16 * n + 16)
            settle(act, s)

        @block.vector
        def _(dve):
            dve.sem_inc(s("lo_dve"), C)
            dve.sem_inc(s("act"), G1)
            dve.sem_inc(s("act_rows"), G1)
            dve.sem_inc(s("xT"), 1)
            dve.sem_inc(s("turned_free"), 1)
            dve.wait_ge(s("b1"), 32)
            nc.vector.tensor_scalar(y[0:2 * E_, 1::2], y[0:2 * E_, 1::2], 1.0, None, ALU.add).then_inc(s("b1_whole"), 1)
            dve.wait_ge(s("b1_hi"), 1)
            dve.wait_ge(s("b1_whole"), 1)
            nc.vector.tensor_tensor(b1[E_:2 * E_, :], y[E_:2 * E_, :], b1[E_:2 * E_, :].bitcast(F32), ALU.subtract
                                    ).then_inc(s("b1_split"), 1)

            def select(p):
                e = expert(dve, p)
                for part in range(2):
                    nc.vector.tensor_copy(sel[part * E_:(part + 1) * E_, :],
                                          ident[part * E_:(part + 1) * E_, ds(e + part * E_, 1)].broadcast_to([E_, P])
                                          ).then_inc(s("sel"), 1)

            def low_x(n, b):
                cols = slice(b * P, (b + 1) * P)
                dve.wait_ge(s("xT_hi"), PB * n + b + 1)
                nc.vector.tensor_tensor(xT_lo[:, :, cols], turned[:, :, :], xT_hi[:, :, cols].bitcast(F32),
                                        ALU.subtract).then_inc(s("xT"), 1)

            def low_dve(p, c):
                low(dve, nc.vector, "dve", p, c)

            select(0)
            for b in range(PB):
                low_x(0, b)
            for c in range(AHEAD):
                low_dve(0, c)
            with dve.Fori(0, NPASS - 1) as p:
                rows = rows_left(dve, p)

                def features(blocks, j):
                    done(dve, p, 2 * j + 1)
                    dve.wait_ge(s("act_rows"), G1 * p + G1 + j)
                    nc.vector.tensor_scalar(gate[:, 0:blocks, :], prod[j % 2][:, 0:blocks, 0::2], LIMIT, None,
                                            ALU.min).then_inc(s("gate"), 1)
                    nc.vector.tensor_scalar(lin[:, 0:blocks, :], prod[j % 2][:, 0:blocks, 1::2], LIMIT + 1, 1 - LIMIT,
                                            ALU.min, ALU.max).then_inc(s("lin"), 1)
                    dve.wait_ge(s("sig"), G1 * p + j + 1)
                    nc.vector.tensor_tensor(gate[:, 0:blocks, :], gate[:, 0:blocks, :], sig[:, 0:blocks, :], ALU.mult
                                            ).then_inc(s("glu"), 1)
                    dve.wait_ge(s("glu"), G1 * p + j + 1)
                    dve.wait_ge(s("lin"), G1 * p + j + 1)
                    dve.wait_ge(s("act_turned"), G1 * p + G1 + j - 1)
                    nc.vector.tensor_tensor(act_rows[j % 2][:, 0:blocks, :], gate[:, 0:blocks, :], lin[:, 0:blocks, :],
                                            ALU.mult).then_inc(s("act_rows"), 1)

                def low_act(blocks, j):
                    dve.wait_ge(s("act_hi"), G1 * p + j + 1)
                    tiles = slice(FT * j, FT * (j + 1))
                    nc.vector.tensor_tensor(act_lo[:, tiles, 0:blocks, :], act_ps[j % 2][:, :, 0:blocks, :],
                                            act_hi[:, tiles, 0:blocks, :].bitcast(F32), ALU.subtract).then_inc(s("act"), 1)

                def body(blocks):
                    low_dve(p, 3)
                    for j in range(G1):
                        features(blocks, j)
                        if 0 < j < G1 - 1:
                            low_act(blocks, j - 1)
                        low_dve(p, 2 * j + 4)
                        low_dve(p, 2 * j + 5)
                    select(p + 1)
                    low_x(p + 1, 0)
                    low_act(blocks, 2)
                    low_act(blocks, 3)

                def tail(blocks, last):
                    if not last:
                        low_dve(p + 1, 0)
                    if not last:
                        low_dve(p + 1, 1)
                    low_x(p + 1, 1)
                    if not last:
                        low_dve(p + 1, 2)

                with dve.If(rows > 0):
                    rows_next = rows_left(dve, p + 1)
                    for big in (True, False):
                        with (dve.If(rows > P) if big else dve.If(rows <= P)):
                            body(1 + big)
                            for last in (False, True):
                                with (dve.If(rows_next == 0) if last else dve.If(rows_next > 0)):
                                    tail(1 + big, last)


def phase_finish(nc, dram, g, sem, out):
    with ExitStack() as ctx:
        def sb(name, shape, dt=F32):
            return ctx.enter_context(nc.sbuf_tensor(f"z_{name}", shape, dt))

        def ps(name, shape, dt=F32):
            return ctx.enter_context(nc.psum_tensor(f"z_{name}", shape, dt))

        def s(name):
            return sem(f"z_{name}")

        KP = PLE // P
        w_gate = sb("w_gate", [P, KD, D])
        w_proj = sb("w_proj", [P, KP, D])
        b2 = sb("b2", [E_, D])
        g_ple = sb("g_ple", [P, KD])
        g_final = sb("g_final", [P, D])
        y_rows = [sb(f"y_rows{j}", [P, TOPK, D]) for j in range(2)]
        dense_t = [sb(f"dense_t{j}", [P, E_]) for j in range(2)]
        denseT = [sb(f"denseT{j}", [E_, P]) for j in range(2)]
        h = [sb(f"h{j}", [P, D]) for j in range(2)]
        p_in = [sb(f"p_in{j}", [P, PLE]) for j in range(2)]
        pT = [sb(f"pT{j}", [P, KP, P]) for j in range(2)]
        hn = [sb(f"hn{j}", [P, D]) for j in range(2)]
        hT = [sb(f"hT{j}", [P, KD, P]) for j in range(2)]
        sig = [sb(f"sig{j}", [P, D]) for j in range(2)]
        squares = [sb(f"squares{j}", [P, D]) for j in range(2)]
        stat = [sb(f"stat{j}", [P, 2]) for j in range(2)]
        turned = ps("turned", [P, KD, P])
        bias_ps = ps("bias_ps", [P, D])
        gate_ps = ps("gate_ps", [P, D])
        proj_ps = ps("proj_ps", [P, D])
        ident, gates, dense = g["ident"], g["gates"], g["dense"]
        block = ctx.enter_context(nc.Block())
        TURNS = 6

        @block.sync
        def _(sp):
            sp.dma_start(b2[:, :], dram["b_e2"][0]).then_inc(s("w"), 16)
            sp.dma_start(w_proj[:, :, :], dram["w_ple_proj"][0].rearrange("(k p) n -> p k n", p=P)).then_inc(s("w"), 16)
            sp.dma_start(w_gate[:, :, :], dram["w_ple_gate"][0].rearrange("(k p) n -> p k n", p=P)).then_inc(s("w"), 16)
            sp.dma_start(g_ple[:, :], dram["g_ple"]).then_inc(s("w"), 16)
            sp.dma_start(g_final[:, :], dram["g_final"].partition_broadcast(P)).then_inc(s("w"), 16)
            for j in range(2):
                sp.sem_inc(s(f"out{j}"), 16)
            with sp.Fori(0, NT // 2) as i:
                for j in range(2):
                    t = 2 * i + j
                    sp.wait_ge(s(f"out{j}"), 16 * i + 16)
                    sp.dma_start(h[j][:, :], dram["h1"][ds(t * P, P), :]).then_inc(s(f"h{j}"), 16)
                    sp.wait_ge(s("p_free"), t + 1)
                    sp.dma_start(p_in[j][:, :], dram["p"][0, 0, ds(t * P, P), :]).then_inc(s(f"p{j}"), 16)
                for j in range(2):
                    t = 2 * i + j
                    sp.wait_ge(s("final"), t + 1)
                    sp.dma_start(out[0, ds(t * P, P), :], h[j][:, :]).then_inc(s(f"out{j}"), 16)
            for j in range(2):
                sp.wait_ge(s(f"out{j}"), 16 * (NT // 2) + 16)

        @block.gpsimd
        def _(pool):
            def gather(t):
                if t >= 2:
                    pool.wait_ge(s("h2"), t - 1)
                for k in range(TOPK):
                    nc.gpsimd.indirect_dma_start(out=y_rows[t % 2][:, k, :], out_offset=None, in_=dram["y"],
                                                 in_offset=bass.IndirectOffsetOnAxis(
                                                     ap=g["y_row"][:, t * TOPK + k:t * TOPK + k + 1], axis=0)
                                                 ).then_inc(s(f"y{t % 2}"), 16)

            def root(n, of):
                for j in range(2):
                    pool.wait_ge(s(f"mean{of}"), 2 * n + j + 1)
                    nc.gpsimd.tensor_tensor(stat[j][:, of:of + 1], stat[j][:, of:of + 1], g["minus_half"][:, 0:1],
                                            ALU.pow).then_inc(s(f"rstd{of}"), 1)

            for t in range(2):
                gather(t)
            for n in range(NT // 2):
                for j in range(2):
                    if n:
                        pool.wait_ge(s("dense_turned"), 2 * n - 1 + j)
                    nc.gpsimd.tensor_copy(dense_t[j][:, :], dense[:, 2 * n + j, :]).then_inc(s("dense"), 1)
                root(n, 0)
                for j in range(2):
                    if n + 1 < NT // 2:
                        gather(2 * n + 2 + j)
                root(n, 1)

        @block.tensor
        def _(pe):
            pe.sem_inc(s("p_free"), 2)
            pe.wait_ge(s("w"), 80)
            with pe.Fori(0, NT // 2) as i:
                for j in range(2):
                    t = 2 * i + j
                    pe.wait_ge(s("dense"), t + 1)
                    pe.wait_ge(s("turned_free"), TURNS * i + j + 1)
                    nc.tensor.transpose(turned[0:E_, 0, :], dense_t[j][:, :], ident[:, :]).then_inc(s("dense_turned"), 1)
                    pe.wait_ge(s("denseT"), t + 1)
                    pe.wait_ge(s("bias_free"), t + 1)
                    for c in range(2):
                        ins = nc.tensor.matmul(bias_ps[:, c * 512:(c + 1) * 512], denseT[j][:, :], b2[:, c * 512:(c + 1) * 512],
                                               start=True, stop=True)
                    ins.then_inc(s("bias"), 1)
                for j in range(2):
                    t = 2 * i + j
                    pe.wait_ge(s(f"p{j}"), 16 * i + 16)
                    pe.wait_ge(s("turned_free"), TURNS * i + j + 3)
                    for k in range(KP):
                        ins = nc.tensor.transpose(turned[:, k, :], p_in[j][:, k * P:(k + 1) * P], ident[:, :])
                    ins.then_inc(s("p_free"), 1)
                for j in range(2):
                    t = 2 * i + j
                    pe.wait_ge(s("pT"), t + 1)
                    pe.wait_ge(s("gate_free"), t + 1)
                    for c in range(2):
                        for k in range(KP):
                            nc.tensor.matmul(proj_ps[:, c * 512:(c + 1) * 512], pT[j][:, k, :],
                                             w_proj[:, k, c * 512:(c + 1) * 512], start=k == 0, stop=k == KP - 1)
                    pe.wait_ge(s("hn"), t + 1)
                    pe.wait_ge(s("turned_free"), TURNS * i + j + 5)
                    for k in range(KD):
                        ins = nc.tensor.transpose(turned[:, k, :], hn[j][:, k * P:(k + 1) * P], ident[:, :])
                    ins.then_inc(s("h_turned"), 1)
                    pe.wait_ge(s("hT"), t + 1)
                    for c in range(2):
                        for k in range(KD):
                            ins = nc.tensor.matmul(gate_ps[:, c * 512:(c + 1) * 512], hT[j][:, k, :],
                                                   w_gate[:, k, c * 512:(c + 1) * 512], start=k == 0, stop=k == KD - 1)
                    ins.then_inc(s("gate"), 1)

        @block.scalar
        def _(act):
            act.sem_inc(s("turned_free"), 1)
            with act.Fori(0, NT // 2) as i:
                for j in range(2):
                    t = 2 * i + j
                    act.wait_ge(s("dense_turned"), t + 1)
                    nc.scalar.activation(denseT[j][:, :], turned[0:E_, 0, :], ACT.Copy).then_inc(s("denseT"), 1)
                    act.wait_ge(s("denseT"), t + 1)
                    act.sem_inc(s("turned_free"), 1)
                for j in range(2):
                    t = 2 * i + j
                    act.wait_ge(s("p_free"), t + 3)
                    nc.scalar.activation(pT[j][:, :, :], turned[:, 0:KP, :], ACT.Copy).then_inc(s("pT"), 1)
                    act.wait_ge(s("pT"), t + 1)
                    act.sem_inc(s("turned_free"), 1)
                for j in range(2):
                    t = 2 * i + j
                    act.wait_ge(s("h2"), t + 1)
                    nc.scalar.activation(squares[j][:, :], h[j][:, :], ACT.Square, accum_out=stat[j][:, 0:1]).then_inc(s("ssq0"), 1)
                for j in range(2):
                    t = 2 * i + j
                    act.wait_ge(s("gate"), t + 1)
                    nc.scalar.activation(sig[j][:, :], gate_ps[:, :], ACT.Sigmoid).then_inc(s("sig"), 1)
                for j in range(2):
                    t = 2 * i + j
                    act.wait_ge(s("h3"), t + 1)
                    nc.scalar.activation(squares[j][:, :], h[j][:, :], ACT.Square, accum_out=stat[j][:, 1:2]).then_inc(s("ssq1"), 1)

        @block.vector
        def _(dve):
            dve.sem_inc(s("bias_free"), 1)
            dve.sem_inc(s("gate_free"), 1)
            dve.wait_ge(s("w"), 80)
            per = 2 * (TOPK + 2)
            with dve.Fori(0, NT // 2) as i:
                own = Steps(dve, s("dve"), i * per)
                for j in range(2):
                    t = 2 * i + j
                    dve.wait_ge(s(f"h{j}"), 16 * i + 16)
                    dve.wait_ge(s("bias"), t + 1)
                    own.step(nc.vector.tensor_tensor(h[j][:, :], h[j][:, :], bias_ps[:, :], ALU.add))
                    dve.sem_inc(s("bias_free"), 1)
                    dve.wait_ge(s(f"y{j}"), 16 * TOPK * i + 16 * TOPK)
                    for k in range(TOPK):
                        ins = nc.vector.scalar_tensor_tensor(h[j][:, :], y_rows[j][:, k, :], gates[:, ds(t * TOPK + k, 1)],
                                                             h[j][:, :], ALU.mult, ALU.add)
                        if k < TOPK - 1:
                            own.step(ins)
                    ins.then_inc(s("h2"), 1)
                for j in range(2):
                    t = 2 * i + j
                    dve.wait_ge(s("ssq0"), t + 1)
                    nc.vector.tensor_scalar(stat[j][:, 0:1], stat[j][:, 0:1], 1.0 / D, EPS, ALU.mult, ALU.add).then_inc(s("mean0"), 1)
                for j in range(2):
                    t = 2 * i + j
                    dve.wait_ge(s("rstd0"), t + 1)
                    nc.vector.tensor_scalar(hn[j][:, :], h[j][:, :], stat[j][:, 0:1], None, ALU.mult).then_inc(s("hn"), 1)
                for j in range(2):
                    t = 2 * i + j
                    dve.wait_ge(s("h_turned"), t + 1)
                    nc.vector.tensor_tensor(hT[j][:, :, :], turned[:, :, :], g_ple[:, :].unsqueeze(2).broadcast_to([P, KD, P]),
                                            ALU.mult).then_inc(s("hT"), 1)
                    dve.wait_ge(s("hT"), t + 1)
                    dve.sem_inc(s("turned_free"), 1)
                    dve.wait_ge(s("sig"), t + 1)
                    own.step(nc.vector.tensor_tensor(sig[j][:, :], sig[j][:, :], proj_ps[:, :], ALU.mult))
                    dve.sem_inc(s("gate_free"), 1)
                    nc.vector.tensor_tensor(h[j][:, :], h[j][:, :], sig[j][:, :], ALU.add).then_inc(s("h3"), 1)
                for j in range(2):
                    t = 2 * i + j
                    dve.wait_ge(s("ssq1"), t + 1)
                    nc.vector.tensor_scalar(stat[j][:, 1:2], stat[j][:, 1:2], 1.0 / D, EPS, ALU.mult, ALU.add).then_inc(s("mean1"), 1)
                for j in range(2):
                    t = 2 * i + j
                    dve.wait_ge(s("rstd1"), t + 1)
                    own.step(nc.vector.tensor_scalar(h[j][:, :], h[j][:, :], stat[j][:, 1:2], None, ALU.mult))
                    nc.vector.tensor_tensor(h[j][:, :], h[j][:, :], g_final[:, :], ALU.mult).then_inc(s("final"), 1)
                assert own.n == per, own.n


def constants():
    k = np.arange(P)
    ident = np.eye(P, dtype=np.float32)
    mask = np.zeros((P, T), np.float32)
    mask[:, T - P:][k[None, :] > k[:, None]] = NEG
    inv = np.zeros((P, 1), np.float32)
    rot = np.zeros((P, P), np.float32)
    half = ROT // 2
    for h in range(0, P, HD):
        for n in range(half):
            f = np.float32(500000.0) ** np.float32(-2.0 * n / ROT)
            inv[h + n] = inv[h + half + n] = f
            rot[h + half + n, h + n] = -1.0
            rot[h + n, h + half + n] = 1.0
    before = (k[:, None] < k[None, :]).astype(np.float32)
    tokens = (np.arange(NT)[None, :] * P + k[:, None]).astype(np.int32)
    return {"c_ident": ident, "c_mask": mask, "c_inv_freq": inv, "c_rot": rot, "c_before": before,
            "c_tokens": tokens}


def build(nc, dram, out):
    for name, shape, dt in (("negc", (N_FOX, T), F32), ("h1", (T, D), F32), ("hn", (T, D), F32),
                            ("lists", (E_ * T, 1), I32), ("y", (NPASS * BR, D), F32)):
        dram[name] = nc.dram_tensor(f"scratch_{name}", shape, dt, kind="Internal").ap()
    with ExitStack() as ctx:
        sems = {}

        def sem(name):
            if name not in sems:
                sems[name] = nc.alloc_semaphore(name=name)
            return sems[name]

        def clear():
            nc.clear_and_free_semaphores(list(sems.values()))
            sems.clear()
            nc.all_engine_barrier()

        def sb(name, shape, dt=F32):
            return ctx.enter_context(nc.sbuf_tensor(name, shape, dt))

        g = {"ident": sb("ident", [P, P]), "minus_half": sb("minus_half", [P, NT]), "gates": sb("gates", [P, NT * TOPK]),
             "dense": sb("dense", [P, NT, E_]), "y_row": sb("y_row", [P, NT * TOPK], I32),
             "table": sb("table", [1, 3 * NPASS + 1], I32)}
        with nc.sbuf_tensor("mixT", [P, KD, T], F32) as mixT:
            g["mixT"] = mixT
            with ExitStack() as inner:
                for name, shape in (("xT", [P, KD, T]), ("mask", [P, T]), ("rot", [P, P]), ("gain", [P, 1]),
                                    ("neg_lam", [P, 1]), ("sin", [P, T]), ("cos", [P, T])):
                    g[name] = inner.enter_context(nc.sbuf_tensor(name, shape, F32))
                phase_prepare(nc, dram, g, sem)
                clear()
                phase_attention(nc, dram, g, sem, True)
                clear()
                phase_attention(nc, dram, g, sem, False)
            clear()
            phase_route(nc, dram, g, sem)
            clear()
        phase_experts(nc, dram, g, sem)
        clear()
        phase_finish(nc, dram, g, sem, out)


_INS = ["x", "p", "positions", "g_attn", "w_in", "lambda_q1", "lambda_k1", "lambda_q2", "lambda_k2",
        "g_subln", "b_forget", "w_out", "g_moe", "w_router", "b_router", "w_e1", "b_e1", "w_e2", "b_e2",
        "g_ple", "w_ple_gate", "w_ple_proj", "g_final"]


def kernel(**inputs):
    import numpy as _np
    import concourse.bacc as _bacc
    from concourse import mybir as _mybir
    from concourse.bass_utils import run_bass_kernel_spmd as _run

    nc = _bacc.Bacc("TRN2", target_bir_lowering=False, num_devices=1)
    arrays, dram = {}, {}
    given = {name: _np.ascontiguousarray(inputs[name]) for name in _INS}
    for name in ("g_attn", "g_ple"):
        given[name] = _np.ascontiguousarray(given[name].reshape(KD, P).T)
    for name in ("b_forget", "g_subln"):
        given[name] = _np.ascontiguousarray(given[name].T)
    given.update(constants())
    for name, a in given.items():
        arrays[f"in_{name}_dram"] = a
        dram[name] = nc.dram_tensor(f"in_{name}_dram", a.shape, _mybir.dt.from_np(a.dtype), kind="ExternalInput").ap()
    out = nc.dram_tensor("out_0_dram", (1, T, D), _mybir.dt.float32, kind="ExternalOutput").ap()
    build(nc, dram, out)
    r = _run(nc, [arrays], core_ids=[0])
    return r.results[0]["out_0_dram"]
```

```python
from contextlib import ExitStack

import numpy as np
import concourse.bass as bass
from concourse import mybir

F32 = mybir.dt.float32
F32R = mybir.dt.float32r
I32 = mybir.dt.int32
U32 = mybir.dt.uint32
ALU = mybir.AluOpType
ACT = mybir.ActivationFunctionType
AX = mybir.AxisListType
ds = bass.ds

P = 128
D = 1024
T = 1024
KD = D // P
NT = T // P
HD = 64
N_DIFF = 4
N_FOX = 8
ROT = HD // 4
EPS = 1e-5
SCALE = HD ** -0.5
LAMBDA_INIT = 0.8 - 0.6
NEG = -1e30
E_ = 32
TOPK = 4
FE = 1024
PLE = 256
LIMIT = 7.0
ALPHA = 1.702
BR = 256
NPASS = (T * TOPK + E_ * (BR - 1)) // BR + 1
DQ0, DK0, DV0 = 0, 512, 1024
FQ0, FK0, FV0, FF0 = 1536, 2048, 2560, 3072
TWO_PI_1 = 6.28125
TWO_PI_2 = float(np.float32(2 * np.pi - 6.28125) // np.float32(2.0 ** -21) * 2.0 ** -21)
TWO_PI_3 = 2 * np.pi - 6.28125 - TWO_PI_2
PI_BELOW = 3.1415925
ROUND = 1.5 * 2.0 ** 23


class Steps:

    def __init__(self, eng, sem, start=0):
        self.eng, self.sem, self.start, self.n = eng, sem, start, 0

    def step(self, ins):
        self.n += 1
        ins.then_inc(self.sem, 1)
        self.eng.wait_ge(self.sem, self.start + self.n)


def settle(eng, sem):
    eng.sem_inc(sem("settled"), 1)


def phase_prepare(nc, dram, g, sem):
    with ExitStack() as ctx:
        def sb(name, shape, dt=F32):
            return ctx.enter_context(nc.sbuf_tensor(name, shape, dt))

        def ps(name, shape, dt=F32):
            return ctx.enter_context(nc.psum_tensor(name, shape, dt))

        x_in = [sb(f"x_in{j}", [P, D]) for j in range(2)]
        x_scaled = [sb(f"x_scaled{j}", [P, D]) for j in range(2)]
        squares = [sb(f"squares{j}", [P, D]) for j in range(2)]
        ssq = sb("ssq", [P, 2])
        rstd = sb("rstd", [P, 2])
        g_attn = sb("g_attn", [P, KD])
        pos_i = sb("pos_i", [P, T], I32)
        inv_freq = sb("inv_freq", [P, 1])
        ang = sb("ang", [P, T])
        turns = sb("turns", [P, T])
        reduced = sb("reduced", [P, T])
        lam_in = sb("lam_in", [P, 4, HD])
        lam_junk = sb("lam_junk", [P, HD])
        lam_s = sb("lam_s", [P, 2])
        lam_e = sb("lam_e", [P, 2])
        w_f = sb("w_f", [P, KD, N_FOX])
        b_f = sb("b_f", [N_FOX, 1])
        z = sb("z", [N_FOX, T])
        z_e = sb("z_e", [N_FOX, T])
        z_l = sb("z_l", [N_FOX, T])
        ones8 = sb("ones8", [N_FOX, T])
        turned = [ps(f"turned{j}", [P, KD, P]) for j in range(2)]
        z_ps = ps("z_ps", [N_FOX, T])
        xT, ident = g["xT"], g["ident"]
        block = ctx.enter_context(nc.Block())

        @block.sync
        def _(sp):
            sp.dma_start(ident[:, :], dram["c_ident"]).then_inc(sem("a_ident"), 16)
            sp.dma_start(g_attn[:, :], dram["g_attn"]).then_inc(sem("a_g"), 16)
            with sp.Fori(0, NT // 2) as i:
                for j in range(2):
                    sp.wait_ge(sem("a_x_free"), 2 * i + j + 1)
                    sp.dma_start(x_in[j][:, :], dram["x"][0, ds((2 * i + j) * P, P), :]).then_inc(sem(f"a_x{j}"), 16)
            sp.dma_start(pos_i[:, :], dram["positions"][0].partition_broadcast(P)).then_inc(sem("a_pos"), 16)
            sp.dma_start(inv_freq[:, :], dram["c_inv_freq"]).then_inc(sem("a_inv"), 16)
            sp.dma_start(w_f[:, :, :], dram["w_in"][0].rearrange("(k p) n -> p k n", p=P)[:, :, FF0:FF0 + N_FOX]).then_inc(sem("a_wf"), 16)
            sp.dma_start(b_f[:, :], dram["b_forget"]).then_inc(sem("a_bf"), 16)
            for n, name in enumerate(("lambda_q1", "lambda_k1", "lambda_q2", "lambda_k2")):
                sp.dma_start(lam_in[:, n, :], dram[name][0].partition_broadcast(P)).then_inc(sem("a_lam"), 16)
            sp.dma_start(g["mask"][:, :], dram["c_mask"]).then_inc(sem("a_mask"), 16)
            sp.dma_start(g["rot"][:, :], dram["c_rot"]).then_inc(sem("a_rot"), 16)
            sp.dma_start(g["gain"][:, 0:1], dram["g_subln"]).then_inc(sem("a_gain"), 16)
            sp.wait_ge(sem("a_negc"), 1)
            sp.dma_start(dram["negc"], z_e[:, :]).then_inc(sem("a_out"), 16)
            sp.wait_ge(sem("a_out"), 16)
            sp.wait_ge(sem("a_mask"), 16)
            sp.wait_ge(sem("a_rot"), 16)

        @block.scalar
        def _(act):
            with act.Fori(0, NT // 2) as i:
                for j in range(2):
                    act.wait_ge(sem(f"a_x{j}"), 16 * i + 16)
                    nc.scalar.activation(squares[j][:, :], x_in[j][:, :], ACT.Square,
                                         accum_out=ssq[:, j:j + 1]).then_inc(sem("a_ssq"), 1)
            act.wait_ge(sem("a_z"), 2)
            nc.scalar.activation(z_e[:, :], z_l[:, :], ACT.Exp).then_inc(sem("a_ze"), 1)
            act.wait_ge(sem("a_z"), 3)
            nc.scalar.activation(z_l[:, :], z_e[:, :], ACT.Ln).then_inc(sem("a_zl"), 1)
            act.wait_ge(sem("a_lams"), 2)
            nc.scalar.activation(lam_e[:, :], lam_s[:, :], ACT.Exp).then_inc(sem("a_lame"), 1)
            act.wait_ge(sem("a_red"), 1)
            nc.scalar.activation(g["sin"][:, :], reduced[:, :], ACT.Sin).then_inc(sem("a_sin"), 1)
            act.wait_ge(sem("a_red"), 2)
            nc.scalar.activation(g["cos"][:, :], reduced[:, :], ACT.Sin).then_inc(sem("a_sin"), 1)

        @block.gpsimd
        def _(pool):
            nc.gpsimd.memset(g["minus_half"][:, :], -0.5).then_inc(sem("a_half"), 1)
            pool.wait_ge(sem("a_half"), 1)
            with pool.Fori(0, NT // 2) as i:
                for j in range(2):
                    pool.wait_ge(sem("a_mean"), 2 * i + j + 1)
                    nc.gpsimd.tensor_tensor(rstd[:, j:j + 1], rstd[:, j:j + 1], g["minus_half"][:, 0:1], ALU.pow).then_inc(sem("a_rstd"), 1)

        @block.tensor
        def _(pe):
            pe.wait_ge(sem("a_ident"), 16)
            with pe.Fori(0, NT // 2) as i:
                for j in range(2):
                    pe.wait_ge(sem("a_xs"), 2 * i + j + 1)
                    pe.wait_ge(sem("a_turned_free"), 2 * i + j + 1)
                    for k in range(KD):
                        ins = nc.tensor.transpose(turned[j][:, k, :], x_scaled[j][:, k * P:(k + 1) * P], ident[:, :])
                    ins.then_inc(sem("a_turned"), 1)
            pe.wait_ge(sem("a_turned_free"), NT + 2)
            pe.wait_ge(sem("a_wf"), 16)
            for h in range(2):
                for k in range(KD):
                    ins = nc.tensor.matmul(z_ps[:, h * 512:(h + 1) * 512], w_f[:, k, :],
                                           xT[:, k, h * 512:(h + 1) * 512], start=k == 0, stop=k == KD - 1)
            ins.then_inc(sem("a_zps"), 1)

        @block.vector
        def _(dve):
            dve.sem_inc(sem("a_x_free"), 2)
            dve.sem_inc(sem("a_turned_free"), 2)
            dve.wait_ge(sem("a_g"), 16)
            with dve.Fori(0, NT // 2) as i:
                for j in range(2):
                    dve.wait_ge(sem("a_ssq"), 2 * i + j + 1)
                    nc.vector.tensor_scalar(rstd[:, j:j + 1], ssq[:, j:j + 1], 1.0 / D, EPS, ALU.mult, ALU.add).then_inc(sem("a_mean"), 1)
                for j in range(2):
                    dve.wait_ge(sem("a_rstd"), 2 * i + j + 1)
                    nc.vector.tensor_scalar(x_scaled[j][:, :], x_in[j][:, :], rstd[:, j:j + 1], None,
                                            ALU.mult).then_inc(sem("a_xs"), 1)
                    dve.wait_ge(sem("a_xs"), 2 * i + j + 1)
                    dve.sem_inc(sem("a_x_free"), 1)
                for j in range(2):
                    dve.wait_ge(sem("a_turned"), 2 * i + j + 1)
                    nc.vector.tensor_tensor(xT[:, :, ds((2 * i + j) * P, P)], turned[j][:, :, :],
                                            g_attn[:, :].unsqueeze(2).broadcast_to([P, KD, P]),
                                            ALU.mult).then_inc(sem("a_turned_free"), 1)
            own = Steps(dve, sem("a_dve"))
            dve.wait_ge(sem("a_zps"), 1)
            dve.wait_ge(sem("a_bf"), 16)
            own.step(nc.vector.memset(ones8[:, :], 1.0))
            nc.vector.tensor_scalar(z[:, :], z_ps[:, :], b_f[:, 0:1], None, ALU.add).then_inc(sem("a_z"), 1)
            dve.wait_ge(sem("a_z"), 1)
            nc.vector.scalar_tensor_tensor(z_l[:, :], z[:, :], -1.0, z[:, :], ALU.mult, ALU.min).then_inc(sem("a_z"), 1)
            dve.wait_ge(sem("a_ze"), 1)
            nc.vector.tensor_scalar(z_e[:, :], z_e[:, :], 1.0, None, ALU.add).then_inc(sem("a_z"), 1)
            dve.wait_ge(sem("a_zl"), 1)
            own.step(nc.vector.tensor_scalar(z[:, :], z[:, :], 0.0, None, ALU.min))
            own.step(nc.vector.tensor_tensor(z_l[:, :], z_l[:, :], z[:, :], ALU.subtract))
            nc.vector.tensor_tensor_scan(z_e[:, :], ones8[:, :], z_l[:, :], 0.0, ALU.mult, ALU.add).then_inc(sem("a_negc"), 1)
            dve.wait_ge(sem("a_lam"), 64)
            for n in range(2):
                nc.vector.tensor_tensor_reduce(lam_junk[:, :], lam_in[:, 2 * n, :], lam_in[:, 2 * n + 1, :], 1.0, 0.0,
                                               ALU.mult, ALU.add, lam_s[:, n:n + 1]).then_inc(sem("a_lams"), 1)
                dve.wait_ge(sem("a_lams"), n + 1)
            dve.wait_ge(sem("a_lame"), 1)
            own.step(nc.vector.tensor_tensor(g["neg_lam"][:, :], lam_e[:, 1:2], lam_e[:, 0:1], ALU.subtract))
            own.step(nc.vector.tensor_scalar(g["neg_lam"][:, :], g["neg_lam"][:, :], -LAMBDA_INIT, None, ALU.add))
            dve.wait_ge(sem("a_gain"), 16)
            own.step(nc.vector.tensor_scalar(g["gain"][:, :], g["gain"][:, :], 1.0 - LAMBDA_INIT, None, ALU.mult))
            dve.wait_ge(sem("a_pos"), 16)
            dve.wait_ge(sem("a_inv"), 16)
            own.step(nc.vector.tensor_copy(ang[:, :], pos_i[:, :]))
            own.step(nc.vector.tensor_scalar(ang[:, :], ang[:, :], inv_freq[:, 0:1], None, ALU.mult))
            for n, quarter in enumerate((0.0, 0.25)):
                own.step(nc.vector.tensor_scalar(turns[:, :], ang[:, :], float(1 / (2 * np.pi)), quarter, ALU.mult, ALU.add))
                own.step(nc.vector.tensor_scalar(turns[:, :], turns[:, :], ROUND, None, ALU.add))
                own.step(nc.vector.tensor_scalar(turns[:, :], turns[:, :], ROUND, None, ALU.subtract))
                if n:
                    dve.wait_ge(sem("a_sin"), 1)
                own.step(nc.vector.scalar_tensor_tensor(reduced[:, :], turns[:, :], -TWO_PI_1, ang[:, :], ALU.mult, ALU.add))
                own.step(nc.vector.scalar_tensor_tensor(reduced[:, :], turns[:, :], -TWO_PI_2, reduced[:, :], ALU.mult, ALU.add))
                own.step(nc.vector.scalar_tensor_tensor(reduced[:, :], turns[:, :], -TWO_PI_3, reduced[:, :], ALU.mult, ALU.add))
                own.step(nc.vector.tensor_scalar(reduced[:, :], reduced[:, :], quarter * 2 * np.pi, None, ALU.add))
                nc.vector.tensor_scalar(reduced[:, :], reduced[:, :], PI_BELOW, -PI_BELOW, ALU.min, ALU.max).then_inc(sem("a_red"), 1)


def phase_attention(nc, dram, g, sem, diff):
    tag = "d" if diff else "f"
    q0, k0, v0 = (DQ0, DK0, DV0) if diff else (FQ0, FK0, FV0)
    NH = 4
    with ExitStack() as ctx:
        def sb(name, shape, dt=F32):
            return ctx.enter_context(nc.sbuf_tensor(f"{tag}_{name}", shape, dt))

        def ps(name, shape, dt=F32):
            return ctx.enter_context(nc.psum_tensor(f"{tag}_{name}", shape, dt))

        def s(name):
            return sem(f"{tag}_{name}")

        w_qkv = [sb(f"w_qkv{j}", [P, 3, KD, P]) for j in range(2)]
        q_raw = sb("q_raw", [P, T])
        k_raw = sb("k_raw", [P, T])
        qT = sb("qT", [P, T]) if diff else q_raw
        kT = sb("kT", [P, T]) if diff else k_raw
        v = sb("v", [P, NT, P])
        prob = [[sb(f"prob{b}{m}", [P, T]) for m in range(2)] for b in range(2)]
        probT = [[sb(f"probT{b}{m}", [P, NT, P]) for m in range(1 if diff else 2)] for b in range(2)]
        stat = sb("stat", [P, NT, 2, 5])
        o_row = sb("o_row", [P, NT, P])
        o_sq = sb("o_sq", [P, NT, P])
        o_ss = sb("o_ss", [P, NT])
        if diff:
            zeros = sb("zeros", [P, D])
        if not diff:
            negc = [sb(f"negc{m}", [P, T]) for m in range(2)]
            negc_d = [sb(f"negc_d{m}", [P, NT, P]) for m in range(2)]
        score = [ps(f"score{m}", [P, T]) for m in range(2)]
        turned = ps("turned", [P, NT, P])
        o_ps = [ps(f"o_ps{b}", [P, P]) for b in range(2)]
        per_raw = 3 if diff else 2
        xT, mixT, ident = g["xT"], g["mixT"], g["ident"]
        nm = 1 if diff else 2
        wv = P // nm
        wr = dram["w_in"][0].rearrange("(k p) n -> p k n", p=P)
        block = ctx.enter_context(nc.Block())

        @block.sync
        def _(sp):
            with sp.Fori(0, NH // 2) as i:
                for j in range(2):
                    sp.wait_ge(s("w_free"), 2 * i + j + 1)
                    for n, c0 in enumerate((q0, k0, v0)):
                        sp.dma_start(w_qkv[j][:, n, :, :], wr[:, :, ds((2 * i + j) * P + c0, P)]).then_inc(s(f"w{j}"), 16)
                    if diff:
                        share = NPASS * BR // NH
                        sp.wait_ge(s("zeros"), 1)
                        sp.dma_start(dram["y"][ds((2 * i + j) * share, share), :].rearrange("(n p) d -> p n d", p=P),
                                     zeros[:, :].unsqueeze(1).broadcast_to([P, share // P, D])).then_inc(s("cleared"), 16)
                    if not diff:
                        sp.wait_ge(s("negc_free"), 2 * i + j + 1)
                        for m in range(2):
                            sp.dma_start(negc[m][:, :], dram["negc"][ds((2 * i + j) * 2 + m, 1), :].broadcast_to([P, T])
                                         ).then_inc(s("negc"), 16)
            if diff:
                sp.wait_ge(s("cleared"), 16 * NH)

        @block.tensor
        def _(pe):
            pe.sem_inc(s("w_free"), 2)
            with pe.Fori(0, NH // 2) as i:
                for j in range(2):
                    n_head = 2 * i + j
                    pe.wait_ge(s(f"w{j}"), 48 * i + 48)
                    for n in range(2):
                        pe.wait_ge(s("score_free"), (n_head + 1) * 2 * NT)
                        for h in range(2):
                            for k in range(KD):
                                ins = nc.tensor.matmul(score[n][:, h * 512:(h + 1) * 512], w_qkv[j][:, n, k, :],
                                                       xT[:, k, h * 512:(h + 1) * 512], start=k == 0, stop=k == KD - 1)
                        ins.then_inc(s("proj"), 1)
                    if diff:
                        for n, raw in enumerate((q_raw, k_raw)):
                            pe.wait_ge(s("raw"), per_raw * n_head + n + 1)
                            for h in range(2):
                                ins = nc.tensor.matmul(score[n][:, h * 512:(h + 1) * 512], g["rot"][:, :],
                                                       raw[:, h * 512:(h + 1) * 512], start=True, stop=True)
                            ins.then_inc(s("rotated"), 1)
                    def project_v(t):
                        pe.wait_ge(s("v_copied"), n_head * NT + t + 1)
                        if t == 0:
                            pe.wait_ge(s("o_free"), n_head * NT + 2)
                        for k in range(KD):
                            ins = nc.tensor.matmul(o_ps[t % 2][:, :], xT[:, k, t * P:(t + 1) * P], w_qkv[j][:, 2, k, :],
                                                   start=k == 0, stop=k == KD - 1)
                        ins.then_inc(s("v"), 1)
                        if t == NT - 1:
                            pe.wait_ge(s("v"), n_head * NT + NT)
                            pe.sem_inc(s("w_free"), 1)

                    if diff:
                        pe.wait_ge(s("turned_free"), n_head * (nm * NT + 1) + 1)
                        for t in range(NT):
                            for k in range(KD):
                                ins = nc.tensor.matmul(turned[:, t, :], xT[:, k, t * P:(t + 1) * P], w_qkv[j][:, 2, k, :],
                                                       start=k == 0, stop=k == KD - 1)
                        ins.then_inc(s("v"), 1)
                        pe.wait_ge(s("v"), n_head + 1)
                        pe.sem_inc(s("w_free"), 1)
                        pe.wait_ge(s("roped"), 2 * n_head + 2)
                    else:
                        for t in range(2):
                            project_v(t)
                        pe.wait_ge(s("raw"), per_raw * n_head + 2)

                    def turn(b, m):
                        pe.wait_ge(s("prob"), (n_head * NT + b) * nm + m + 1)
                        pe.wait_ge(s("turned_free"), n_head * (nm * NT + 1) + b * nm + m + 1)
                        if diff and b == 0:
                            pe.wait_ge(s("raw"), per_raw * n_head + 3)
                        for kb in range(b + 1):
                            ins = nc.tensor.transpose(turned[:, kb, :], prob[b % 2][m][:, kb * P:(kb + 1) * P], ident[:, :])
                        ins.then_inc(s("turned"), 1)

                    for step in range(NT + 2):
                        if step < NT:
                            width = (step + 1) * P
                            for m in range(2):
                                if step:
                                    pe.wait_ge(s("score_free"), (n_head + 1) * 2 * NT + 2 * step - 1 + m)
                                for c in range(0, width, 512):
                                    ins = nc.tensor.matmul(score[m][:, c:min(c + 512, width)],
                                                           qT[m * HD:(m + 1) * HD, step * P:(step + 1) * P],
                                                           kT[m * HD:(m + 1) * HD, c:min(c + 512, width)],
                                                           start=True, stop=True)
                                ins.then_inc(s("score"), 1)
                        if not diff and step < NT // 2 - 1:
                            for t in range(2):
                                project_v(2 * step + 2 + t)
                        if 1 <= step <= NT:
                            turn(step - 1, 0)
                        if step >= 2:
                            b = step - 2
                            pe.wait_ge(s("o_free"), n_head * NT + b + 1)
                            if diff and b == 0:
                                pe.wait_ge(s("raw"), per_raw * n_head + 3)
                            if not diff and b == 0:
                                pe.wait_ge(s("v_copied"), n_head * NT + NT + 2)
                            for m in range(nm):
                                pe.wait_ge(s("probT"), (n_head * NT + b) * nm + m + 1)
                                for kb in range(b + 1):
                                    ins = nc.tensor.matmul(o_ps[b % 2][:, m * wv:(m + 1) * wv], probT[b % 2][m][:, kb, :],
                                                           v[:, kb, m * wv:(m + 1) * wv], start=kb == 0, stop=kb == b)
                            ins.then_inc(s("o"), 1)
                        if not diff and 1 <= step <= NT:
                            turn(step - 1, 1)
                    pe.wait_ge(s("o_row"), n_head + 1)
                    pe.wait_ge(s("turned_free"), n_head * (nm * NT + 1) + nm * NT + 1)
                    for t in range(NT):
                        ins = nc.tensor.transpose(turned[:, t, :], o_row[:, t, :], ident[:, :])
                    ins.then_inc(s("o_turned"), 1)

        @block.scalar
        def _(act):
            act.sem_inc(s("turned_free"), 1)
            if not diff:
                act.sem_inc(s("v_copied"), 2)
            with act.Fori(0, NH // 2) as i:
                for j in range(2):
                    n_head = 2 * i + j
                    act.wait_ge(s("proj"), 2 * n_head + 1)
                    nc.scalar.activation(q_raw[:, :], score[0][:, :], ACT.Copy, scale=SCALE).then_inc(s("raw"), 1)
                    act.wait_ge(s("proj"), 2 * n_head + 2)
                    nc.scalar.activation(k_raw[:, :], score[1][:, :], ACT.Copy).then_inc(s("raw"), 1)

                    def copy_v(t):
                        act.wait_ge(s("v"), n_head * NT + t + 1)
                        nc.scalar.activation(v[:, t, :], o_ps[t % 2][:, :], ACT.Copy).then_inc(s("v_copied"), 1)

                    if diff:
                        act.wait_ge(s("v"), n_head + 1)
                        nc.scalar.activation(v[:, :, :], turned[:, :, :], ACT.Copy).then_inc(s("raw"), 1)
                    else:
                        for t in range(2):
                            copy_v(t)
                    for step in range(NT + 1):
                        if step < NT:
                            width = (step + 1) * P
                            for m in range(2):
                                act.wait_ge(s("negmax"), (n_head * NT + step) * 2 + m + 1)
                                nc.scalar.activation(prob[step % 2][m][:, 0:width], prob[step % 2][m][:, 0:width], ACT.Exp,
                                                     bias=stat[:, step, m, 2:3], accum_out=stat[:, step, m, 3:4]
                                                     ).then_inc(s("exp") if diff else s("prob"), 1)
                                if not diff and step < NT // 2 - 1:
                                    copy_v(2 * step + 2 + m)
                        if step >= 1:
                            b = step - 1
                            for m in range(nm):
                                act.wait_ge(s("turned"), (n_head * NT + b) * nm + m + 1)
                                if b >= 2:
                                    act.wait_ge(s("o"), n_head * NT + b - 1)
                                nc.scalar.activation(probT[b % 2][m][:, 0:b + 1, :], turned[:, 0:b + 1, :], ACT.Copy
                                                     ).then_inc(s("probT"), 1)
                                act.wait_ge(s("probT"), (n_head * NT + b) * nm + m + 1)
                                act.sem_inc(s("turned_free"), 1)
                    act.wait_ge(s("o_turned"), n_head + 1)
                    out = mixT[:, ds(n_head + (0 if diff else N_DIFF), 1), :].rearrange("p a t -> p (a t)")
                    nc.scalar.activation(out, turned[:, :, :].rearrange("p a t -> p (a t)"), ACT.Copy,
                                         scale=g["gain"][:, 0:1] if diff else 1.0).then_inc(s("turned_free"), 1)

        @block.gpsimd
        def _(pool):
            if diff:
                nc.gpsimd.memset(zeros[:, :], 0.0).then_inc(s("zeros"), 1)
                with pool.Fori(0, NH // 2) as i:
                    for j in range(2):
                        n_head = 2 * i + j
                        for n, (raw, to) in enumerate(((q_raw, qT), (k_raw, kT))):
                            pool.wait_ge(s("raw"), per_raw * n_head + n + 1)
                            nc.gpsimd.tensor_tensor(to[:, :], raw[:, :], g["cos"][:, :], ALU.mult).then_inc(s("cos"), 1)
                        pool.wait_ge(s("mean"), n_head + 1)
                        nc.gpsimd.tensor_tensor(o_ss[:, :], o_ss[:, :], g["minus_half"][:, :], ALU.pow).then_inc(s("rstd"), 1)
            else:
                pool.sem_inc(s("negc_free"), 1)
                with pool.Fori(0, NH // 2) as i:
                    for j in range(2):
                        n_head = 2 * i + j
                        for m in range(2):
                            pool.wait_ge(s("negc"), 32 * n_head + 32)
                            nc.gpsimd.tensor_tensor(negc_d[m][:, :, :], negc[m][:, :].rearrange("p (a t) -> p a t", t=P),
                                                    g["mask"][:, T - P:T].unsqueeze(1).broadcast_to([P, NT, P]),
                                                    ALU.add).then_inc(s("negc_d"), 1)

        @block.vector
        def _(dve):
            dve.sem_inc(s("score_free"), 2 * NT)
            dve.sem_inc(s("o_free"), 2)
            per = DVE_STEPS_DIFF if diff else DVE_STEPS_FOX
            with dve.Fori(0, NH // 2) as i:
                own = Steps(dve, s("dve"), i * per)
                for j in range(2):
                    n_head = 2 * i + j
                    if diff:
                        for n, to in enumerate((qT, kT)):
                            dve.wait_ge(s("rotated"), 2 * n_head + n + 1)
                            own.step(nc.vector.tensor_tensor(prob[0][n][:, :], score[n][:, :], g["sin"][:, :], ALU.mult))
                            dve.wait_ge(s("cos"), 2 * n_head + n + 1)
                            nc.vector.tensor_tensor(to[:, :], to[:, :], prob[0][n][:, :], ALU.add).then_inc(s("roped"), 1)
                    else:
                        dve.wait_ge(s("negc_d"), 2 * n_head + 2)

                    def normalise(b):
                        dve.wait_ge(s("exp"), (n_head * NT + b) * 2 + 2)
                        w = (b + 1) * P
                        own.step(nc.vector.reciprocal(stat[:, b, :, 4:5], stat[:, b, :, 3:4]))
                        own.step(nc.vector.tensor_tensor(stat[:, b, 1, 4:5], stat[:, b, 1, 4:5], g["neg_lam"][:, :], ALU.mult))
                        own.step(nc.vector.tensor_scalar(prob[b % 2][1][:, 0:w], prob[b % 2][1][:, 0:w],
                                                         stat[:, b, 1, 4:5], None, ALU.mult))
                        nc.vector.scalar_tensor_tensor(prob[b % 2][0][:, 0:w], prob[b % 2][0][:, 0:w], stat[:, b, 0, 4:5],
                                                       prob[b % 2][1][:, 0:w], ALU.mult, ALU.add).then_inc(s("prob"), 1)

                    def collect(b):
                        dve.wait_ge(s("o"), n_head * NT + b + 1)
                        if diff:
                            ins = nc.vector.tensor_copy(o_row[:, b, :], o_ps[b % 2][:, :])
                        else:
                            own.step(nc.vector.reciprocal(stat[:, b, :, 4:5], stat[:, b, :, 3:4]))
                            for m in range(2):
                                ins = nc.vector.tensor_scalar(o_row[:, b, m * wv:(m + 1) * wv], o_ps[b % 2][:, m * wv:(m + 1) * wv],
                                                              stat[:, b, m, 4:5], None, ALU.mult)
                                if m == 0:
                                    own.step(ins)
                        own.step(ins)
                        dve.sem_inc(s("o_free"), 1)

                    dve.wait_ge(s("turned_free"), n_head * (nm * NT + 1) + 1)
                    for step in range(NT + 2):
                        if diff and 1 <= step <= NT:
                            normalise(step - 1)
                        if step < NT:
                            width = (step + 1) * P
                            for m in range(2):
                                dve.wait_ge(s("score"), (n_head * NT + step) * 2 + m + 1)
                                if step >= 2:
                                    dve.wait_ge(s("turned"), (n_head * NT + step - 2) * nm + min(m, nm - 1) + 1)
                                p = prob[step % 2][m]
                                st = stat[:, step, m, :]
                                settle(dve, s)
                                if diff:
                                    own.step(nc.vector.tensor_tensor_reduce(
                                        p[:, 0:width], score[m][:, 0:width], g["mask"][:, T - width:T], 1.0, 3 * NEG,
                                        ALU.add, ALU.max, st[:, 0:1]))
                                    last = st[:, 0:1]
                                else:
                                    own.step(nc.vector.tensor_tensor_reduce(
                                        p[:, width - P:width], score[m][:, width - P:width], negc_d[m][:, step, :], 1.0, 3 * NEG,
                                        ALU.add, ALU.max, st[:, 0:1]))
                                    last = st[:, 0:1]
                                    if step:
                                        settle(dve, s)
                                        own.step(nc.vector.tensor_tensor_reduce(
                                            p[:, 0:width - P], score[m][:, 0:width - P], negc[m][:, 0:width - P], 1.0, st[:, 0:1],
                                            ALU.add, ALU.max, st[:, 1:2]))
                                        last = st[:, 1:2]
                                dve.sem_inc(s("score_free"), 1)
                                nc.vector.tensor_scalar(st[:, 2:3], last, -1.0, None, ALU.mult).then_inc(s("negmax"), 1)
                        if step >= 2:
                            collect(step - 2)
                    if diff:
                        own.step(nc.vector.tensor_tensor(o_sq[:, :, :], o_row[:, :, :], o_row[:, :, :], ALU.mult))
                        own.step(nc.vector.tensor_reduce(o_ss[:, :], o_sq[:, :, :], AX.X, ALU.add))
                        nc.vector.tensor_scalar(o_ss[:, :], o_ss[:, :], 1.0 / P, EPS, ALU.mult, ALU.add).then_inc(s("mean"), 1)
                        dve.wait_ge(s("rstd"), n_head + 1)
                        nc.vector.tensor_tensor(o_row[:, :, :], o_row[:, :, :],
                                                o_ss[:, :].unsqueeze(2).broadcast_to([P, NT, P]), ALU.mult).then_inc(s("o_row"), 1)
                    else:
                        dve.sem_inc(s("o_row"), 1)
                        dve.sem_inc(s("negc_free"), 1)
                assert own.n == per, own.n


DVE_STEPS_DIFF = 2 * (2 + 3 * NT + 2 * NT + NT + 2)
DVE_STEPS_FOX = 2 * (2 * NT + 2 * (NT - 1) + 3 * NT)


def phase_route(nc, dram, g, sem):
    with ExitStack() as ctx:
        def sb(name, shape, dt=F32):
            return ctx.enter_context(nc.sbuf_tensor(f"c_{name}", shape, dt))

        def ps(name, shape, dt=F32):
            return ctx.enter_context(nc.psum_tensor(f"c_{name}", shape, dt))

        def s(name):
            return sem(f"c_{name}")

        w_out = sb("w_out", [P, KD, D])
        w_r = sb("w_r", [P, KD, E_])
        b_r = sb("b_r", [P, E_])
        g_moe = sb("g_moe", [P, D])
        before = sb("before", [P, P])
        ones = sb("ones", [P, P])
        tokens = sb("tokens", [P, NT], I32)
        zeros = sb("zeros", [P, E_ * T // P], I32)
        experts = sb("experts", [P, E_])
        experts_i = sb("experts_i", [P, E_], I32)
        passes_i = sb("passes_i", [1, NPASS], I32)
        passes = sb("passes", [1, NPASS])
        stage = [sb(f"stage{j}", [P, KD, P]) for j in range(2)]
        x_in = [sb(f"x_in{j}", [P, D]) for j in range(2)]
        h1 = [sb(f"h1{j}", [P, D]) for j in range(2)]
        hn = [sb(f"hn{j}", [P, D]) for j in range(2)]
        hT = [sb(f"hT{j}", [P, KD, P]) for j in range(2)]
        squares = [sb(f"squares{j}", [P, D]) for j in range(2)]
        ssq = sb("ssq", [P, 2])
        rstd = sb("rstd", [P, 2])
        logits = sb("logits", [P, E_])
        top = sb("top", [P, 8])
        top_i = sb("top_i", [P, 8], U32)
        top_f = sb("top_f", [P, 8])
        neg_top = sb("neg_top", [P, 1])
        gsum = sb("gsum", [P, 1])
        onehot = sb("onehot", [P, NT, TOPK, E_])
        chosen = sb("chosen", [P, E_])
        chosen_sum = sb("chosen_sum", [P, E_])
        place = sb("place", [P, NT, TOPK])
        place_e = sb("place_e", [P, TOPK, E_])
        row = sb("row", [P, TOPK])
        lists_i = sb("lists_i", [P, NT, TOPK], I32)
        first = sb("first", [P, NT, TOPK])
        n_pass = sb("n_pass", [P, E_])
        n_tmp = sb("n_tmp", [P, E_])
        pass_end = sb("pass_end", [P, E_])
        pass_start = sb("pass_start", [P, E_])
        counts = sb("counts", [P, E_])
        ones32 = sb("ones32", [P, E_])
        big = sb("big", [P, NT * TOPK, E_])
        in_pass = sb("in_pass", [1, NPASS, E_])
        in_tmp = sb("in_tmp", [1, NPASS, E_])
        tab = sb("tab", [1, 3, NPASS])
        tab_t = sb("tab_t", [1, NPASS])
        acc = [ps(f"acc{j}", [P, D]) for j in range(2)]
        turned = ps("turned", [P, KD, P])
        rt_ps = ps("rt_ps", [P, E_])
        pl_ps = ps("pl_ps", [P, E_])
        ident, gates, dense = g["ident"], g["gates"], g["dense"]
        block = ctx.enter_context(nc.Block())

        @block.sync
        def _(sp):
            wr = dram["w_out"][0].rearrange("(k p) n -> p k n", p=P)
            for k in range(0, KD, 2):
                sp.dma_start(w_out[:, k:k + 2, :], wr[:, k:k + 2, :]).then_inc(s(f"w_out{k}"), 16)
            sp.dma_start(w_r[:, :, :], dram["w_router"][0].rearrange("(k p) n -> p k n", p=P)).then_inc(s("w_r"), 16)
            sp.dma_start(b_r[:, :], dram["b_router"][0].partition_broadcast(P)).then_inc(s("w_r"), 16)
            sp.dma_start(g_moe[:, :], dram["g_moe"][0].partition_broadcast(P)).then_inc(s("w_r"), 16)
            sp.dma_start(before[:, :], dram["c_before"]).then_inc(s("w_r"), 16)
            sp.dma_start(tokens[:, :], dram["c_tokens"]).then_inc(s("tokens"), 16)
            sp.wait_ge(s("zeros"), 1)
            sp.dma_start(dram["lists"].rearrange("(p n) a -> p (n a)", p=P), zeros[:, :]).then_inc(s("cleared"), 16)
            with sp.Fori(0, NT // 2) as i:
                for j in range(2):
                    sp.wait_ge(s("x_free"), 2 * i + j + 1)
                    sp.dma_start(x_in[j][:, :], dram["x"][0, ds((2 * i + j) * P, P), :]).then_inc(s(f"x{j}"), 16)
            sp.wait_ge(s("cleared"), 16)

        def pipeline(eng, step):
            step(0, 0)
            with eng.Fori(0, NT // 2 - 1) as i:
                for c in (1, 2):
                    step(i, c)
            step(0, NT - 1)

        @block.gpsimd
        def _(pool):
            nc.gpsimd.memset(zeros[:, :], 0).then_inc(s("zeros"), 1)
            nc.gpsimd.iota(experts_i[:, :], pattern=[[1, E_]], base=0, channel_multiplier=0).then_inc(s("iota"), 1)
            nc.gpsimd.iota(passes_i[:, :], pattern=[[1, NPASS]], base=0, channel_multiplier=0).then_inc(s("iota"), 1)
            nc.gpsimd.memset(ones[:, :], 1.0).then_inc(s("ones"), 1)

            def put_stage(t):
                pool.wait_ge(s("stage_free"), t + 1)
                nc.gpsimd.tensor_copy(stage[t % 2][:, :, :], g["mixT"][:, :, t * P:(t + 1) * P]).then_inc(s("stage"), 1)

            def root(t):
                pool.wait_ge(s("mean"), t + 1)
                j = t % 2
                nc.gpsimd.tensor_tensor(rstd[:, j:j + 1], rstd[:, j:j + 1], g["minus_half"][:, 0:1], ALU.pow).then_inc(s("rstd"), 1)

            def scatter(t):
                pool.wait_ge(s("lists"), t + 1)
                for k in range(TOPK):
                    nc.gpsimd.indirect_dma_start(
                        out=dram["lists"], out_offset=bass.IndirectOffsetOnAxis(ap=lists_i[:, t, k:k + 1], axis=0),
                        in_=tokens[:, t:t + 1], in_offset=None).then_inc(s("scattered"), 16)

            put_stage(0)
            put_stage(1)
            root(0)
            pool.wait_ge(s("cleared"), 16)
            pool.wait_ge(s("tokens"), 16)
            for t in range(NT):
                if t + 2 < NT:
                    put_stage(t + 2)
                if t + 1 < NT:
                    root(t + 1)
                if t:
                    scatter(t - 1)
            scatter(NT - 1)
            pool.wait_ge(s("scattered"), 16 * NT * TOPK)

        @block.tensor
        def _(pe):
            pe.sem_inc(s("stage_free"), 2)

            def project(i, c):
                t, j = 2 * i + c, c % 2
                pe.wait_ge(s("stage"), t + 1)
                pe.wait_ge(s("x_free"), t + 1)
                for n in range(2):
                    for k in range(KD):
                        if c == 0 and n == 0 and k % 2 == 0:
                            pe.wait_ge(s(f"w_out{k}"), 16)
                        ins = nc.tensor.matmul(acc[j][:, n * 512:(n + 1) * 512], stage[j][:, k, :],
                                               w_out[:, k, n * 512:(n + 1) * 512], start=k == 0, stop=k == KD - 1)
                ins.then_inc(s("acc"), 1)

            def count(t):
                pe.wait_ge(s("chosen"), t + 1)
                nc.tensor.matmul(pl_ps[:, :], before[:, :], chosen[:, :], start=True, stop=False)
                nc.tensor.matmul(pl_ps[:, :], ones[:, :], chosen_sum[:, :], start=False, stop=True).then_inc(s("place"), 1)

            def step(i, c):
                t, j = 2 * i + c, c % 2
                if c < NT - 1:
                    project(i, c + 1)
                pe.wait_ge(s("hn"), t + 1)
                pe.wait_ge(s("hT"), t + 1)
                for k in range(KD):
                    ins = nc.tensor.transpose(turned[:, k, :], hn[j][:, k * P:(k + 1) * P], ident[:, :])
                ins.then_inc(s("turned"), 1)
                pe.wait_ge(s("turned"), t + 1)
                if c < NT - 1:
                    pe.sem_inc(s("stage_free"), 1)
                if c:
                    count(t - 1)
                pe.wait_ge(s("hT"), t + 2)
                for k in range(KD):
                    ins = nc.tensor.matmul(rt_ps[:, :], hT[j][:, k, :], w_r[:, k, :], start=k == 0, stop=k == KD - 1)
                ins.then_inc(s("logits"), 1)

            project(0, 0)
            pe.wait_ge(s("acc"), 1)
            pe.sem_inc(s("stage_free"), 1)
            pe.wait_ge(s("w_r"), 64)
            pe.wait_ge(s("ones"), 1)
            pipeline(pe, step)
            count(NT - 1)
            pe.wait_ge(s("chosen"), NT + 1)
            nc.tensor.matmul(pl_ps[:, :], ones[:, :], chosen_sum[:, :], start=True, stop=True).then_inc(s("place"), 1)

        @block.scalar
        def _(act):
            for j in range(2):
                act.sem_inc(s(f"h1_out{j}"), 16)
                act.sem_inc(s(f"hn_out{j}"), 16)

            def squares_of(i, c):
                t, j = 2 * i + c, c % 2
                act.wait_ge(s("h1"), t + 1)
                nc.scalar.activation(squares[j][:, :], h1[j][:, :], ACT.Square, accum_out=ssq[:, j:j + 1]).then_inc(s("ssq"), 1)
                act.dma_start(dram["h1"][ds(t * P, P), :], h1[j][:, :]).then_inc(s(f"h1_out{j}"), 16)

            def store(i, c):
                t, j = 2 * i + c, c % 2
                act.wait_ge(s("hn"), t + 1)
                act.dma_start(dram["hn"][ds(t * P, P), :], hn[j][:, :]).then_inc(s(f"hn_out{j}"), 16)

            def step(i, c):
                t = 2 * i + c
                if c < NT - 1:
                    squares_of(i, c + 1)
                act.wait_ge(s("neg_top"), t + 1)
                nc.scalar.activation(gates[:, ds(t * TOPK, TOPK)], top[:, 0:TOPK], ACT.Exp, bias=neg_top[:, 0:1],
                                     accum_out=gsum[:, 0:1]).then_inc(s("gates"), 1)
                if c < NT - 1:
                    store(i, c + 1)

            squares_of(0, 0)
            store(0, 0)
            pipeline(act, step)
            for j in range(2):
                act.wait_ge(s(f"h1_out{j}"), 16 * (NT // 2) + 16)
                act.wait_ge(s(f"hn_out{j}"), 16 * (NT // 2) + 16)

        @block.vector
        def _(dve):
            dve.sem_inc(s("x_free"), 2)
            nc.vector.memset(chosen_sum[:, :], 0.0).then_inc(s("init"), 1)
            nc.vector.memset(ones32[:, :], 1.0).then_inc(s("init"), 1)
            dve.wait_ge(s("iota"), 2)
            nc.vector.tensor_copy(experts[:, :], experts_i[:, :]).then_inc(s("init"), 1)
            nc.vector.tensor_copy(passes[:, :], passes_i[:, :]).then_inc(s("init"), 1)
            dve.wait_ge(s("init"), 4)
            dve.wait_ge(s("w_r"), 64)

            def add(i, c):
                t, n_j, j = 2 * i + c, i + c // 2, c % 2
                dve.wait_ge(s("acc"), t + 1)
                dve.wait_ge(s(f"x{j}"), 16 * n_j + 16)
                dve.wait_ge(s(f"h1_out{j}"), 16 * n_j + 16)
                dve.wait_ge(s(f"hn_out{j}"), 16 * n_j + 16)
                nc.vector.tensor_tensor(h1[j][:, :], acc[j][:, :], x_in[j][:, :], ALU.add).then_inc(s("h1"), 1)
                dve.wait_ge(s("h1"), t + 1)
                dve.sem_inc(s("x_free"), 1)
                dve.wait_ge(s("ssq"), t + 1)
                nc.vector.tensor_scalar(rstd[:, j:j + 1], ssq[:, j:j + 1], 1.0 / D, EPS, ALU.mult, ALU.add).then_inc(s("mean"), 1)

            def norm(i, c):
                t, j = 2 * i + c, c % 2
                dve.wait_ge(s("rstd"), t + 1)
                nc.vector.scalar_tensor_tensor(hn[j][:, :], h1[j][:, :], rstd[:, j:j + 1], g_moe[:, :], ALU.mult, ALU.mult
                                               ).then_inc(s("hn"), 1)

            def choose(i, c):
                t = 2 * i + c
                own = Steps(dve, s("choose"), t * (4 + TOPK + 4))
                dve.wait_ge(s("logits"), t + 1)
                own.step(nc.vector.tensor_tensor(logits[:, :], rt_ps[:, :], b_r[:, :], ALU.add))
                settle(dve, s)
                own.step(nc.vector.max(top[:, :], logits[:, :]))
                settle(dve, s)
                own.step(nc.vector.max_index(top_i[:, :], top[:, :], logits[:, :]))
                nc.vector.tensor_scalar(neg_top[:, :], top[:, 0:1], -1.0, None, ALU.mult).then_inc(s("neg_top"), 1)
                own.step(nc.vector.tensor_copy(top_f[:, :], top_i[:, :]))
                for k in range(TOPK):
                    own.step(nc.vector.tensor_scalar(onehot[:, ds(t, 1), k, :].rearrange("p a e -> p (a e)"), experts[:, :],
                                                     top_f[:, k:k + 1], None, ALU.is_equal))
                oh = onehot[:, ds(t, 1), :, :].rearrange("p a k e -> p (a k) e")
                settle(dve, s)
                nc.vector.tensor_reduce(chosen[:, :], oh.rearrange("p k e -> p e k"), AX.X, ALU.add).then_inc(s("chosen"), 1)
                dve.wait_ge(s("gates"), t + 1)
                gt = gates[:, ds(t * TOPK, TOPK)]
                own.step(nc.vector.reciprocal(gsum[:, :], gsum[:, :]))
                own.step(nc.vector.tensor_scalar(gt, gt, gsum[:, 0:1], None, ALU.mult))
                own.step(nc.vector.tensor_tensor(place_e[:, :, :], oh, gt.unsqueeze(2).broadcast_to([P, TOPK, E_]), ALU.mult))
                settle(dve, s)
                own.step(nc.vector.tensor_reduce(dense[:, ds(t, 1), :].rearrange("p a e -> p (a e)"),
                                                 place_e[:, :, :].rearrange("p k e -> p e k"), AX.X, ALU.add))
                assert own.n == 4 + TOPK + 4, own.n

            def put(i, c):
                t = 2 * i + c
                own = Steps(dve, s("put"), t * 6)
                oh = onehot[:, ds(t, 1), :, :].rearrange("p a k e -> p (a k) e")
                place_t = place[:, ds(t, 1), :].rearrange("p a k -> p (a k)")
                dve.wait_ge(s("place"), t + 1)
                own.step(nc.vector.tensor_copy(n_tmp[:, :], pl_ps[:, :]))
                own.step(nc.vector.tensor_tensor(place_e[:, :, :], oh, n_tmp[:, :].unsqueeze(1).broadcast_to([P, TOPK, E_]), ALU.mult))
                settle(dve, s)
                own.step(nc.vector.tensor_reduce(place_t, place_e[:, :, :], AX.X, ALU.add))
                own.step(nc.vector.tensor_tensor(chosen_sum[:, :], chosen_sum[:, :], chosen[:, :], ALU.add))
                own.step(nc.vector.scalar_tensor_tensor(row[:, :], top_f[:, 0:TOPK], float(T), place_t, ALU.mult, ALU.add))
                own.step(nc.vector.tensor_copy(lists_i[:, ds(t, 1), :].rearrange("p a k -> p (a k)"), row[:, :]))
                dve.sem_inc(s("lists"), 1)

            def step(i, c):
                t, j = 2 * i + c, c % 2
                dve.wait_ge(s("turned"), t + 1)
                nc.vector.tensor_copy(hT[j][:, :, :], turned[:, :, :]).then_inc(s("hT"), 1)
                if c:
                    put(i, c - 1)
                if c < NT - 1:
                    add(i, c + 1)
                choose(i, c)
                if c < NT - 1:
                    norm(i, c + 1)

            dve.sem_inc(s("hT"), 1)
            add(0, 0)
            norm(0, 0)
            pipeline(dve, step)
            put(0, NT - 1)
            own = Steps(dve, s("dve"))
            dve.sem_inc(s("chosen"), 1)
            dve.wait_ge(s("place"), NT + 1)
            own.step(nc.vector.tensor_copy(counts[:, :], pl_ps[:, :]))
            own.step(nc.vector.tensor_scalar(n_pass[:, :], counts[:, :], 0.0, None, ALU.is_gt))
            for b in range(1, T // BR):
                own.step(nc.vector.tensor_scalar(n_tmp[:, :], counts[:, :], float(b * BR), None, ALU.is_gt))
                own.step(nc.vector.tensor_tensor(n_pass[:, :], n_pass[:, :], n_tmp[:, :], ALU.add))
            own.step(nc.vector.tensor_tensor_scan(pass_end[:, :], ones32[:, :], n_pass[:, :], 0.0, ALU.mult, ALU.add))
            own.step(nc.vector.tensor_tensor(pass_start[:, :], pass_end[:, :], n_pass[:, :], ALU.subtract))
            own.step(nc.vector.tensor_tensor(big[:, :, :], onehot[:, :, :, :].rearrange("p t k e -> p (t k) e"),
                                             pass_start[:, :].unsqueeze(1).broadcast_to([P, NT * TOPK, E_]), ALU.mult))
            own.step(nc.vector.tensor_reduce(first[:, :, :].rearrange("p t k -> p (t k)"), big[:, :, :], AX.X, ALU.add))
            own.step(nc.vector.scalar_tensor_tensor(first[:, :, :], first[:, :, :], float(BR), place[:, :, :], ALU.mult, ALU.add))
            own.step(nc.vector.tensor_copy(g["y_row"][:, :], first[:, :, :].rearrange("p t k -> p (t k)")))
            p_b = passes[0:1, :].unsqueeze(2).broadcast_to([1, NPASS, E_])

            def over(x):
                return x[0:1, :].unsqueeze(1).broadcast_to([1, NPASS, E_])

            own.step(nc.vector.tensor_tensor(in_pass[:, :, :], p_b, over(pass_start), ALU.is_ge))
            own.step(nc.vector.tensor_tensor(in_tmp[:, :, :], p_b, over(pass_end), ALU.is_ge))
            own.step(nc.vector.tensor_tensor(in_pass[:, :, :], in_pass[:, :, :], in_tmp[:, :, :], ALU.subtract))
            for n, values in enumerate((experts, pass_start, counts)):
                own.step(nc.vector.tensor_tensor(in_tmp[:, :, :], in_pass[:, :, :], over(values), ALU.mult))
                own.step(nc.vector.tensor_reduce(tab[:, n, :], in_tmp[:, :, :], AX.X, ALU.add))
            own.step(nc.vector.tensor_tensor(tab_t[:, :], passes[0:1, :], tab[:, 1, :], ALU.subtract))
            own.step(nc.vector.tensor_scalar(tab_t[:, :], tab_t[:, :], float(BR), None, ALU.mult))
            own.step(nc.vector.tensor_tensor(tab[:, 2, :], tab[:, 2, :], tab_t[:, :], ALU.subtract))
            own.step(nc.vector.tensor_scalar(tab[:, 2, :], tab[:, 2, :], 0.0, None, ALU.max))
            own.step(nc.vector.scalar_tensor_tensor(tab[:, 1, :], tab[:, 0, :], float(T), tab_t[:, :], ALU.mult, ALU.add))
            own.step(nc.vector.tensor_scalar(tab[:, 1, :], tab[:, 1, :], float(E_ * T - BR), None, ALU.min))
            own.step(nc.vector.tensor_copy(g["table"][:, 0:3 * NPASS], tab[:, :, :].rearrange("p a n -> p (a n)")))
            own.step(nc.vector.tensor_copy(g["table"][:, 3 * NPASS:], pass_end[0:1, E_ - 1:E_]))


def phase_experts(nc, dram, g, sem):
    with ExitStack() as ctx:
        def sb(name, shape, dt=F32):
            return ctx.enter_context(nc.sbuf_tensor(f"e_{name}", shape, dt))

        def ps(name, shape, dt=F32):
            return ctx.enter_context(nc.psum_tensor(f"e_{name}", shape, dt))

        def s(name):
            return sem(f"e_{name}")

        W = 512
        G1, G2 = 2 * FE // W, D // W
        KH = KD // 2
        C = 2 * (G1 + G2)
        AHEAD = 3
        RAW = C // 2
        WF = W // 2
        FT = WF // P
        NF = FE // P
        PB = BR // P
        raw = [sb(f"raw{c}", [P, KH, W]) for c in range(RAW)]
        hi = [sb(f"hi{n}", [P, KH, W], F32R) for n in range(AHEAD + 1)]
        lo = [sb(f"lo{n}", [P, KH, W], F32R) for n in range(AHEAD + 1)]
        b1 = sb("b1", [2 * E_, 2 * FE], F32R)
        sel = sb("sel", [2 * E_, P], F32R)
        rows_i = [sb(f"rows_i{b}", [P, 1], I32) for b in range(PB)]
        x_rows = sb("x_rows", [P, PB, D])
        xT_hi = sb("xT_hi", [P, KD, BR], F32R)
        xT_lo = sb("xT_lo", [P, KD, BR], F32R)
        gate = sb("gate", [P, PB, WF])
        lin = sb("lin", [P, PB, WF])
        sig = sb("sig", [P, PB, WF])
        act_rows = [sb(f"act_rows{n}", [P, PB, WF]) for n in range(2)]
        act_hi = sb("act_hi", [P, NF, PB, P], F32R)
        act_lo = sb("act_lo", [P, NF, PB, P], F32R)
        y = sb("y", [P, PB * D])
        warm = sb("warm", [P, 1])
        prod = [ps(f"prod{n}", [P, PB, W]) for n in range(2)]
        act_ps = [ps(f"act_ps{n}", [P, FT, PB, P]) for n in range(2)]
        turned = ps("turned", [P, KD, P])
        ident, table = g["ident"], g["table"]
        block = ctx.enter_context(nc.Block())

        share = {"dve": slice(0, 5 * W // 8), "pool": slice(5 * W // 8, W)}

        def expert(eng, p):
            return eng.value_load(table[0:1, ds(p, 1)], min_val=0, max_val=E_ - 1)

        def first_row(eng, p):
            return eng.value_load(table[0:1, ds(p + NPASS, 1)], min_val=0, max_val=E_ * T - BR)

        def rows_left(eng, p):
            return eng.value_load(table[0:1, ds(p + 2 * NPASS, 1)], min_val=0, max_val=T)

        def split_done(eng, p, c):
            for who in share:
                eng.wait_ge(s(f"lo_{who}"), C * (p + 1) + c + 1)

        def done(eng, p, c):
            eng.wait_ge(s("done"), C * (p + 1) + c + 1)

        def low(eng, vec, who, p, c):
            eng.wait_ge(s("hi"), C * p + c + 1)
            slot, cols = c % (AHEAD + 1), share[who]
            vec.tensor_tensor(lo[slot][:, :, cols], raw[c % RAW][:, :, cols], hi[slot][:, :, cols].bitcast(F32),
                              ALU.subtract).then_inc(s(f"lo_{who}"), 1)

        @block.sync
        def _(sp):
            for part in range(2):
                sp.dma_start(y[part * E_:(part + 1) * E_, :], dram["b_e1"][0]).then_inc(s("b1"), 16)
            w1 = dram["w_e1"][0].rearrange("e (k p) n -> p e k n", p=P)
            w2 = dram["w_e2"][0].rearrange("e (k p) n -> p e k n", p=P)
            with sp.Fori(0, NPASS - 1) as p:
                with sp.If(rows_left(sp, p) > 0):
                    e = expert(sp, p)
                    for c in range(C):
                        split_done(sp, p - (c < RAW), (c - RAW) % C)
                        if c < 2 * G1:
                            src, half, n = w1, c % 2, c // 2
                        else:
                            src, half, n = w2, (c - 2 * G1) // G2, (c - 2 * G1) % G2
                        sp.dma_start(raw[c % RAW][:, :, :],
                                     src[:, ds(e, 1), half * KH:(half + 1) * KH, n * W:(n + 1) * W].rearrange("p e k n -> p (e k) n")
                                     ).then_inc(s(f"w{c}"), 16)

        @block.gpsimd
        def _(pool):
            pool.sem_inc(s("lo_pool"), C)

            def fetch_numbers(start):
                for b in range(PB):
                    pool.dma_start(rows_i[b][:, :], dram["lists"][ds(start + b * P, P), :]).then_inc(s(f"rows{b}"), 16)

            def gather(n):
                for b in range(PB):
                    pool.wait_ge(s(f"rows{b}"), 16 * n + 16)
                    pool.wait_ge(s("x_turned"), PB * n + b + 1)
                    settle(pool, s)
                    nc.gpsimd.indirect_dma_start(out=x_rows[:, b, :], out_offset=None, in_=dram["hn"],
                                                 in_offset=bass.IndirectOffsetOnAxis(ap=rows_i[b][:, 0:1], axis=0)
                                                 ).then_inc(s(f"x{b}"), 16)

            def low_pool(p, c):
                low(pool, nc.gpsimd, "pool", p, c)

            fetch_numbers(first_row(pool, 0))
            gather(0)
            for c in range(AHEAD):
                low_pool(0, c)
            with pool.Fori(0, NPASS - 1) as p:
                with pool.If(rows_left(pool, p) > 0):
                    for b in range(PB):
                        pool.wait_ge(s(f"x{b}"), 16 * p + 16)
                    fetch_numbers(first_row(pool, p + 1))
                    for c in range(AHEAD, C):
                        low_pool(p, c)
                        if c == 5:
                            gather(p + 1)
                    with pool.If(rows_left(pool, p + 1) > 0):
                        for c in range(AHEAD):
                            low_pool(p + 1, c)

        @block.tensor
        def _(pe):
            pe.sem_inc(s("done"), C)
            pe.sem_inc(s("x_turned"), PB)
            pe.sem_inc(s("act_turned"), G1)

            def turn(n, b):
                pe.wait_ge(s(f"x{b}"), 16 * n + 16)
                pe.wait_ge(s("xT"), PB * n + b + 1)
                for k in range(KD):
                    ins = nc.tensor.transpose(turned[:, k, :], x_rows[:, b, k * P:(k + 1) * P], ident[:, :])
                ins.then_inc(s("x_turned"), 1)

            def turn_act(p, j, blocks):
                pe.wait_ge(s("act_rows"), G1 * p + G1 + j + 1)
                pe.wait_ge(s("act"), G1 * p + G1 + j - 1)
                for b in range(blocks):
                    for i in range(FT):
                        ins = nc.tensor.transpose(act_ps[j % 2][:, i, b, :], act_rows[j % 2][:, b, i * P:(i + 1) * P], ident[:, :])
                ins.then_inc(s("act_turned"), 1)

            def up(p, c, blocks):
                j, half = c // 2, c % 2
                split_done(pe, p, c)
                if half == 0:
                    if j < 2:
                        pe.wait_ge(s("y_free"), G2 * p + j + 1)
                    else:
                        pe.wait_ge(s("gate"), G1 * p + j - 1)
                        pe.wait_ge(s("lin"), G1 * p + j - 1)
                w_hi, w_lo = hi[c % (AHEAD + 1)], lo[c % (AHEAD + 1)]
                for b in range(blocks):
                    if half == 0:
                        nc.tensor.matmul(prod[j % 2][:, b, :], sel[:, :], b1[:, j * W:(j + 1) * W], start=True, stop=False)
                    for k in range(KH):
                        for i, (x, w) in enumerate(((xT_hi, w_hi), (xT_hi, w_lo), (xT_lo, w_hi))):
                            ins = nc.tensor.matmul(prod[j % 2][:, b, :], x[:, half * KH + k, b * P:(b + 1) * P], w[:, k, :],
                                                   start=False, stop=half == 1 and k == KH - 1 and i == 2)
                ins.then_inc(s("done"), 1)

            def down(p, n, blocks):
                c = 2 * G1 + n
                half, j = n // G2, n % G2
                split_done(pe, p, c)
                if half == 0:
                    pe.wait_ge(s("gate"), G1 * p + G1 - G2 + j + 1)
                    pe.wait_ge(s("lin"), G1 * p + G1 - G2 + j + 1)
                w_hi, w_lo = hi[c % (AHEAD + 1)], lo[c % (AHEAD + 1)]
                pe.wait_ge(s("act"), G1 * p + G1 + (half + 1) * G1 // 2)
                for b in range(blocks):
                    for k in range(KH):
                        for i, (a, w) in enumerate(((act_hi, w_hi), (act_hi, w_lo), (act_lo, w_hi))):
                            ins = nc.tensor.matmul(prod[j][:, b, :], a[:, half * KH + k, b, :], w[:, k, :],
                                                   start=half == 0 and k == 0 and i == 0,
                                                   stop=half == 1 and k == KH - 1 and i == 2)
                ins.then_inc(s("done"), 1)

            for b in range(PB):
                turn(0, b)
            with pe.Fori(0, NPASS - 1) as p:
                rows = rows_left(pe, p)

                def body(blocks):
                    pe.wait_ge(s("xT"), PB * p + PB + 1)
                    pe.wait_ge(s("sel"), 2 * p + 2)
                    for j in range(G1):
                        for half in range(2):
                            up(p, 2 * j + half, blocks)
                        if 0 < j < G1 - 1:
                            turn_act(p, j - 1, blocks)
                    turn(p + 1, 0)
                    down(p, 0, blocks)
                    turn_act(p, 2, blocks)
                    turn_act(p, 3, blocks)
                    down(p, 1, blocks)
                    turn(p + 1, 1)
                    down(p, 2, blocks)
                    down(p, 3, blocks)

                with pe.If(rows > 0):
                    with pe.If(rows > P):
                        body(2)
                    with pe.Else():
                        body(1)

        @block.scalar
        def _(act):
            act.sem_inc(s("y_out"), 16)

            def high(p, c):
                act.wait_ge(s(f"w{c}"), 16 * p + 16)
                done(act, p, c - AHEAD - 1)
                nc.scalar.activation(hi[c % (AHEAD + 1)][:, :, :], raw[c % RAW][:, :, :], ACT.Copy).then_inc(s("hi"), 1)

            def high_x(n, b):
                act.wait_ge(s("x_turned"), PB * n + PB + b + 1)
                nc.scalar.activation(xT_hi[:, :, b * P:(b + 1) * P], turned[:, :, :], ACT.Copy).then_inc(s("xT_hi"), 1)

            act.wait_ge(s("b1_whole"), 1)
            nc.scalar.activation(b1[:, :], y[0:2 * E_, :], ACT.Copy).then_inc(s("b1_hi"), 1)
            act.wait_ge(s("b1_split"), 1)
            act.sem_inc(s("y_free"), G2)
            for b in range(PB):
                high_x(0, b)
            for c in range(AHEAD + 1):
                high(0, c)
            with act.Fori(0, NPASS - 1) as p:
                rows = rows_left(act, p)
                y_rows = dram["y"][ds(p * BR, BR), :].rearrange("(b q) d -> q b d", q=P)

                def features(blocks, j):
                    act.wait_ge(s("gate"), G1 * p + j + 1)
                    nc.scalar.activation(sig[:, 0:blocks, :], gate[:, 0:blocks, :], ACT.Sigmoid, scale=ALPHA
                                         ).then_inc(s("sig"), 1)

                def high_act(blocks, j):
                    act.wait_ge(s("act_turned"), G1 * p + G1 + j + 1)
                    nc.scalar.activation(act_hi[:, FT * j:FT * (j + 1), 0:blocks, :], act_ps[j % 2][:, :, 0:blocks, :], ACT.Copy
                                         ).then_inc(s("act_hi"), 1)

                def y_out(blocks, c):
                    done(act, p, 2 * G1 + G2 + c)
                    nc.scalar.activation(y[:, :].rearrange("q (b d) -> q b d", b=PB)[:, 0:blocks, c * W:(c + 1) * W],
                                         prod[c][:, 0:blocks, :], ACT.Copy).then_inc(s("y_free"), 1)

                def body(blocks):
                    nc.scalar.activation(warm[:, :], ident[:, 0:1], ACT.Sigmoid).then_inc(s("warm"), 1)
                    high(p, 4)
                    for j in range(G1):
                        features(blocks, j)
                        if 0 < j < G1 - 1:
                            high_act(blocks, j - 1)
                        high(p, 2 * j + 5)
                        if j < G1 - 1:
                            high(p, 2 * j + 6)
                    high_x(p + 1, 0)
                    high_act(blocks, 2)
                    high_act(blocks, 3)

                def tail(blocks, last):
                    if not last:
                        high(p + 1, 0)
                        high(p + 1, 1)
                    high_x(p + 1, 1)
                    act.wait_ge(s("y_out"), 16 * p + 16)
                    y_out(blocks, 0)
                    if not last:
                        high(p + 1, 2)
                        high(p + 1, 3)
                    y_out(blocks, 1)
                    act.wait_ge(s("y_free"), G2 * p + 2 * G2)
                    act.dma_start(y_rows[:, 0:blocks, :], y[:, 0:blocks * D].rearrange("q (b d) -> q b d", b=blocks)
                                  ).then_inc(s("y_out"), 16)

                with act.If(rows > 0):
                    rows_next = rows_left(act, p + 1)
                    for big in (True, False):
                        with (act.If(rows > P) if big else act.If(rows <= P)):
                            body(1 + big)
                            for last in (False, True):
                                with (act.If(rows_next == 0) if last else act.If(rows_next > 0)):
                                    tail(1 + big, last)
            n = act.value_load(table[0:1, 3 * NPASS:3 * NPASS + 1], min_val=1, max_val=NPASS)
            act.wait_ge(s("y_out"), 16 * n + 16)
            settle(act, s)

        @block.vector
        def _(dve):
            dve.sem_inc(s("lo_dve"), C)
            dve.sem_inc(s("act"), G1)
            dve.sem_inc(s("act_rows"), G1)
            dve.sem_inc(s("xT"), 1)
            dve.wait_ge(s("b1"), 32)
            nc.vector.tensor_scalar(y[0:2 * E_, 1::2], y[0:2 * E_, 1::2], 1.0, None, ALU.add).then_inc(s("b1_whole"), 1)
            dve.wait_ge(s("b1_hi"), 1)
            dve.wait_ge(s("b1_whole"), 1)
            nc.vector.tensor_tensor(b1[E_:2 * E_, :], y[E_:2 * E_, :], b1[E_:2 * E_, :].bitcast(F32), ALU.subtract
                                    ).then_inc(s("b1_split"), 1)

            def select(p):
                e = expert(dve, p)
                for part in range(2):
                    nc.vector.tensor_copy(sel[part * E_:(part + 1) * E_, :],
                                          ident[part * E_:(part + 1) * E_, ds(e + part * E_, 1)].broadcast_to([E_, P])
                                          ).then_inc(s("sel"), 1)

            def low_x(n, b):
                cols = slice(b * P, (b + 1) * P)
                dve.wait_ge(s("xT_hi"), PB * n + b + 1)
                nc.vector.tensor_tensor(xT_lo[:, :, cols], turned[:, :, :], xT_hi[:, :, cols].bitcast(F32),
                                        ALU.subtract).then_inc(s("xT"), 1)

            def low_dve(p, c):
                low(dve, nc.vector, "dve", p, c)

            select(0)
            for b in range(PB):
                low_x(0, b)
            for c in range(AHEAD):
                low_dve(0, c)
            with dve.Fori(0, NPASS - 1) as p:
                rows = rows_left(dve, p)

                def features(blocks, j):
                    done(dve, p, 2 * j + 1)
                    dve.wait_ge(s("act_rows"), G1 * p + G1 + j)
                    nc.vector.tensor_scalar(gate[:, 0:blocks, :], prod[j % 2][:, 0:blocks, 0::2], LIMIT, None,
                                            ALU.min).then_inc(s("gate"), 1)
                    nc.vector.tensor_scalar(lin[:, 0:blocks, :], prod[j % 2][:, 0:blocks, 1::2], LIMIT + 1, 1 - LIMIT,
                                            ALU.min, ALU.max).then_inc(s("lin"), 1)
                    dve.wait_ge(s("sig"), G1 * p + j + 1)
                    nc.vector.tensor_tensor(gate[:, 0:blocks, :], gate[:, 0:blocks, :], sig[:, 0:blocks, :], ALU.mult
                                            ).then_inc(s("glu"), 1)
                    dve.wait_ge(s("glu"), G1 * p + j + 1)
                    dve.wait_ge(s("lin"), G1 * p + j + 1)
                    dve.wait_ge(s("act_turned"), G1 * p + G1 + j - 1)
                    nc.vector.tensor_tensor(act_rows[j % 2][:, 0:blocks, :], gate[:, 0:blocks, :], lin[:, 0:blocks, :],
                                            ALU.mult).then_inc(s("act_rows"), 1)

                def low_act(blocks, j):
                    dve.wait_ge(s("act_hi"), G1 * p + j + 1)
                    tiles = slice(FT * j, FT * (j + 1))
                    nc.vector.tensor_tensor(act_lo[:, tiles, 0:blocks, :], act_ps[j % 2][:, :, 0:blocks, :],
                                            act_hi[:, tiles, 0:blocks, :].bitcast(F32), ALU.subtract).then_inc(s("act"), 1)

                def body(blocks):
                    low_dve(p, 3)
                    for j in range(G1):
                        features(blocks, j)
                        if 0 < j < G1 - 1:
                            low_act(blocks, j - 1)
                        low_dve(p, 2 * j + 4)
                        low_dve(p, 2 * j + 5)
                    select(p + 1)
                    low_x(p + 1, 0)
                    low_act(blocks, 2)
                    low_act(blocks, 3)

                def tail(blocks, last):
                    if not last:
                        low_dve(p + 1, 0)
                    if not last:
                        low_dve(p + 1, 1)
                    low_x(p + 1, 1)
                    if not last:
                        low_dve(p + 1, 2)

                with dve.If(rows > 0):
                    rows_next = rows_left(dve, p + 1)
                    for big in (True, False):
                        with (dve.If(rows > P) if big else dve.If(rows <= P)):
                            body(1 + big)
                            for last in (False, True):
                                with (dve.If(rows_next == 0) if last else dve.If(rows_next > 0)):
                                    tail(1 + big, last)


def phase_finish(nc, dram, g, sem, out):
    with ExitStack() as ctx:
        def sb(name, shape, dt=F32):
            return ctx.enter_context(nc.sbuf_tensor(f"z_{name}", shape, dt))

        def ps(name, shape, dt=F32):
            return ctx.enter_context(nc.psum_tensor(f"z_{name}", shape, dt))

        def s(name):
            return sem(f"z_{name}")

        KP = PLE // P
        w_gate = sb("w_gate", [P, KD, D])
        w_proj = sb("w_proj", [P, KP, D])
        b2 = sb("b2", [E_, D])
        g_ple = sb("g_ple", [P, KD])
        g_final = sb("g_final", [P, D])
        y_rows = [sb(f"y_rows{j}", [P, TOPK, D]) for j in range(2)]
        dense_t = [sb(f"dense_t{j}", [P, E_]) for j in range(2)]
        denseT = [sb(f"denseT{j}", [E_, P]) for j in range(2)]
        h1 = [sb(f"h1{j}", [P, D]) for j in range(2)]
        h = [sb(f"h{j}", [P, D]) for j in range(2)]
        p_in = [sb(f"p_in{j}", [P, PLE]) for j in range(2)]
        pT = [sb(f"pT{j}", [P, KP, P]) for j in range(2)]
        hn = [sb(f"hn{j}", [P, D]) for j in range(2)]
        hT = [sb(f"hT{j}", [P, KD, P]) for j in range(2)]
        sig = [sb(f"sig{j}", [P, D]) for j in range(2)]
        squares = [sb(f"squares{j}", [P, D]) for j in range(2)]
        result = [sb(f"result{j}", [P, D]) for j in range(2)]
        stat = [sb(f"stat{j}", [P, 2]) for j in range(2)]
        turned = ps("turned", [P, KD, P])
        bias_ps = ps("bias_ps", [P, D])
        gate_ps = ps("gate_ps", [P, D])
        proj_ps = ps("proj_ps", [P, D])
        ident, gates, dense = g["ident"], g["gates"], g["dense"]
        block = ctx.enter_context(nc.Block())

        def pipeline(eng, step):
            step(0, 0)
            with eng.Fori(0, NT // 2 - 1) as i:
                for c in (1, 2):
                    step(i, c)
            step(0, NT - 1)

        @block.sync
        def _(sp):
            sp.dma_start(b2[:, :], dram["b_e2"][0]).then_inc(s("b2"), 16)

            def load(i, c):
                t, n, j = 2 * i + c, i + c // 2, c % 2
                sp.wait_ge(s("h1_free"), t + 1)
                sp.dma_start(h1[j][:, :], dram["h1"][ds(t * P, P), :]).then_inc(s(f"h1{j}"), 16)
                sp.wait_ge(s("p_free"), t + 1)
                sp.dma_start(p_in[j][:, :], dram["p"][0, 0, ds(t * P, P), :]).then_inc(s(f"p{j}"), 16)

            load(0, 0)
            sp.dma_start(g_ple[:, :], dram["g_ple"]).then_inc(s("g_ple"), 16)
            sp.dma_start(w_proj[:, :, :], dram["w_ple_proj"][0].rearrange("(k p) n -> p k n", p=P)).then_inc(s("w_proj"), 16)
            sp.dma_start(w_gate[:, :, :], dram["w_ple_gate"][0].rearrange("(k p) n -> p k n", p=P)).then_inc(s("w_gate"), 16)
            sp.dma_start(g_final[:, :], dram["g_final"].partition_broadcast(P)).then_inc(s("g_final"), 16)
            with sp.Fori(0, NT // 2 - 1) as i:
                for c in (1, 2):
                    load(i, c)
            load(0, NT - 1)

        @block.gpsimd
        def _(pool):
            def gather(t):
                if t >= 2:
                    pool.wait_ge(s("h2"), t - 1)
                for k in range(TOPK):
                    nc.gpsimd.indirect_dma_start(out=y_rows[t % 2][:, k, :], out_offset=None, in_=dram["y"],
                                                 in_offset=bass.IndirectOffsetOnAxis(
                                                     ap=g["y_row"][:, t * TOPK + k:t * TOPK + k + 1], axis=0)
                                                 ).then_inc(s(f"y{t % 2}"), 16)

            def root(t, of):
                pool.wait_ge(s(f"mean{of}"), t + 1)
                nc.gpsimd.tensor_tensor(stat[t % 2][:, of:of + 1], stat[t % 2][:, of:of + 1], g["minus_half"][:, 0:1],
                                        ALU.pow).then_inc(s(f"rstd{of}"), 1)

            def place_dense(t):
                if t >= 2:
                    pool.wait_ge(s("dense_turned"), t - 1)
                nc.gpsimd.tensor_copy(dense_t[t % 2][:, :], dense[:, t, :]).then_inc(s("dense"), 1)

            for t in range(2):
                place_dense(t)
            for t in range(2):
                gather(t)
            root(0, 0)
            for t in range(NT):
                if t:
                    root(t - 1, 1)
                if t + 2 < NT:
                    gather(t + 2)
                    place_dense(t + 2)
                if t + 1 < NT:
                    root(t + 1, 0)
            root(NT - 1, 1)

        @block.tensor
        def _(pe):
            pe.sem_inc(s("p_free"), 2)

            def turn_dense(i, c):
                t, j = 2 * i + c, c % 2
                pe.wait_ge(s("dense"), t + 1)
                pe.wait_ge(s("bias_free"), t + 1)
                nc.tensor.transpose(bias_ps[0:E_, 0:P], dense_t[j][:, :], ident[:, :]).then_inc(s("dense_turned"), 1)

            def biases(i, c):
                t, j = 2 * i + c, c % 2
                pe.wait_ge(s("denseT"), t + 1)
                for n in range(2):
                    ins = nc.tensor.matmul(bias_ps[:, n * 512:(n + 1) * 512], denseT[j][:, :], b2[:, n * 512:(n + 1) * 512],
                                           start=True, stop=True)
                ins.then_inc(s("bias"), 1)

            def step(i, c):
                t, n_j, j = 2 * i + c, i + c // 2, c % 2
                if c < NT - 1:
                    turn_dense(i, c + 1)
                pe.wait_ge(s("hn"), t + 1)
                pe.wait_ge(s("hT"), t + 1)
                for k in range(KD):
                    ins = nc.tensor.transpose(turned[:, k, :], hn[j][:, k * P:(k + 1) * P], ident[:, :])
                ins.then_inc(s("h_turned"), 1)
                if c < NT - 1:
                    biases(i, c + 1)
                pe.wait_ge(s(f"p{j}"), 16 * n_j + 16)
                pe.wait_ge(s("proj_free"), t + 1)
                for k in range(KP):
                    ins = nc.tensor.transpose(proj_ps[:, k * P:(k + 1) * P], p_in[j][:, k * P:(k + 1) * P], ident[:, :])
                ins.then_inc(s("p_free"), 1)
                pe.wait_ge(s("pT"), t + 1)
                for n in range(2):
                    for k in range(KP):
                        nc.tensor.matmul(proj_ps[:, n * 512:(n + 1) * 512], pT[j][:, k, :],
                                         w_proj[:, k, n * 512:(n + 1) * 512], start=k == 0, stop=k == KP - 1)
                if c == 0:
                    pe.wait_ge(s("w_gate"), 16)
                pe.wait_ge(s("hT"), t + 2)
                pe.wait_ge(s("sig"), t + 1)
                for n in range(2):
                    for k in range(KD):
                        ins = nc.tensor.matmul(gate_ps[:, n * 512:(n + 1) * 512], hT[j][:, k, :],
                                               w_gate[:, k, n * 512:(n + 1) * 512], start=k == 0, stop=k == KD - 1)
                ins.then_inc(s("gate"), 1)

            pe.wait_ge(s("b2"), 16)
            turn_dense(0, 0)
            biases(0, 0)
            pe.wait_ge(s("w_proj"), 16)
            pipeline(pe, step)

        @block.scalar
        def _(act):
            act.sem_inc(s("sig"), 1)

            def turn_dense(i, c):
                t, j = 2 * i + c, c % 2
                act.wait_ge(s("dense_turned"), t + 1)
                nc.scalar.activation(denseT[j][:, :], bias_ps[0:E_, 0:P], ACT.Copy).then_inc(s("denseT"), 1)

            def turn_p(i, c):
                t, j = 2 * i + c, c % 2
                act.wait_ge(s("p_free"), t + 3)
                nc.scalar.activation(pT[j][:, :, :], proj_ps[:, 0:PLE].rearrange("p (k t) -> p k t", t=P), ACT.Copy
                                     ).then_inc(s("pT"), 1)

            def sum_squares(i, c, of, ready):
                t, j = 2 * i + c, c % 2
                act.wait_ge(s(ready), t + 1)
                nc.scalar.activation(squares[j][:, :], h[j][:, :], ACT.Square, accum_out=stat[j][:, of:of + 1]
                                     ).then_inc(s(f"ssq{of}"), 1)

            def sigmoid(i, c):
                t, j = 2 * i + c, c % 2
                act.wait_ge(s("gate"), t + 1)
                nc.scalar.activation(sig[j][:, :], gate_ps[:, :], ACT.Sigmoid).then_inc(s("sig"), 1)

            def store(i, c):
                t, j = 2 * i + c, c % 2
                act.wait_ge(s("final"), t + 1)
                act.dma_start(out[0, ds(t * P, P), :], result[j][:, :]).then_inc(s(f"out{j}"), 16)

            def step(i, c):
                if c:
                    sigmoid(i, c - 1)
                if c < NT - 1:
                    turn_dense(i, c + 1)
                turn_p(i, c)
                if c:
                    sum_squares(i, c - 1, 1, "h3")
                    store(i, c - 1)
                if c < NT - 1:
                    sum_squares(i, c + 1, 0, "h2")

            for j in range(2):
                act.sem_inc(s(f"out{j}"), 16)
            turn_dense(0, 0)
            sum_squares(0, 0, 0, "h2")
            pipeline(act, step)
            sigmoid(0, NT - 1)
            sum_squares(0, NT - 1, 1, "h3")
            store(0, NT - 1)
            for j in range(2):
                act.wait_ge(s(f"out{j}"), 16 * (NT // 2) + 16)

        @block.vector
        def _(dve):
            dve.sem_inc(s("h1_free"), 2)
            dve.sem_inc(s("bias_free"), 1)
            dve.sem_inc(s("proj_free"), 1)
            dve.sem_inc(s("hT"), 1)

            def combine(i, c):
                t, n_j, j = 2 * i + c, i + c // 2, c % 2
                own = Steps(dve, s("h2_steps"), t * TOPK)
                dve.wait_ge(s(f"h1{j}"), 16 * n_j + 16)
                dve.wait_ge(s("bias"), t + 1)
                own.step(nc.vector.tensor_tensor(h[j][:, :], h1[j][:, :], bias_ps[:, :], ALU.add))
                dve.sem_inc(s("bias_free"), 1)
                dve.sem_inc(s("h1_free"), 1)
                dve.wait_ge(s(f"y{j}"), 16 * TOPK * n_j + 16 * TOPK)
                for k in range(TOPK):
                    ins = nc.vector.scalar_tensor_tensor(h[j][:, :], y_rows[j][:, k, :], gates[:, ds(t * TOPK + k, 1)],
                                                         h[j][:, :], ALU.mult, ALU.add)
                    if k < TOPK - 1:
                        own.step(ins)
                ins.then_inc(s("h2"), 1)
                dve.wait_ge(s("ssq0"), t + 1)
                nc.vector.tensor_scalar(stat[j][:, 0:1], stat[j][:, 0:1], 1.0 / D, EPS, ALU.mult, ALU.add).then_inc(s("mean0"), 1)
                dve.wait_ge(s("rstd0"), t + 1)
                nc.vector.tensor_scalar(hn[j][:, :], h[j][:, :], stat[j][:, 0:1], None, ALU.mult).then_inc(s("hn"), 1)

            def turn(i, c):
                t, j = 2 * i + c, c % 2
                dve.wait_ge(s("h_turned"), t + 1)
                nc.vector.tensor_tensor(hT[j][:, :, :], turned[:, :, :], g_ple[:, :].unsqueeze(2).broadcast_to([P, KD, P]),
                                        ALU.mult).then_inc(s("hT"), 1)

            def finish(i, c):
                t, n_j, j = 2 * i + c, i + c // 2, c % 2
                dve.wait_ge(s("sig"), t + 2)
                nc.vector.tensor_tensor(sig[j][:, :], sig[j][:, :], proj_ps[:, :], ALU.mult).then_inc(s("proj_free"), 1)
                dve.wait_ge(s("proj_free"), t + 2)
                nc.vector.tensor_tensor(h[j][:, :], h[j][:, :], sig[j][:, :], ALU.add).then_inc(s("h3"), 1)
                dve.wait_ge(s("ssq1"), t + 1)
                nc.vector.tensor_scalar(stat[j][:, 1:2], stat[j][:, 1:2], 1.0 / D, EPS, ALU.mult, ALU.add).then_inc(s("mean1"), 1)
                dve.wait_ge(s("rstd1"), t + 1)
                dve.wait_ge(s(f"out{j}"), 16 * n_j + 16)
                nc.vector.scalar_tensor_tensor(result[j][:, :], h[j][:, :], stat[j][:, 1:2], g_final[:, :],
                                               ALU.mult, ALU.mult).then_inc(s("final"), 1)
                dve.wait_ge(s("final"), t + 1)

            def step(i, c):
                turn(i, c)
                if c:
                    finish(i, c - 1)
                if c < NT - 1:
                    combine(i, c + 1)

            combine(0, 0)
            dve.wait_ge(s("g_ple"), 16)
            dve.wait_ge(s("g_final"), 16)
            pipeline(dve, step)
            finish(0, NT - 1)


def constants():
    k = np.arange(P)
    ident = np.eye(P, dtype=np.float32)
    mask = np.zeros((P, T), np.float32)
    mask[:, T - P:][k[None, :] > k[:, None]] = NEG
    inv = np.zeros((P, 1), np.float32)
    rot = np.zeros((P, P), np.float32)
    half = ROT // 2
    for h in range(0, P, HD):
        for n in range(half):
            f = np.float32(500000.0) ** np.float32(-2.0 * n / ROT)
            inv[h + n] = inv[h + half + n] = f
            rot[h + half + n, h + n] = -1.0
            rot[h + n, h + half + n] = 1.0
    before = (k[:, None] < k[None, :]).astype(np.float32)
    tokens = (np.arange(NT)[None, :] * P + k[:, None]).astype(np.int32)
    return {"c_ident": ident, "c_mask": mask, "c_inv_freq": inv, "c_rot": rot, "c_before": before,
            "c_tokens": tokens}


def build(nc, dram, out):
    for name, shape, dt in (("negc", (N_FOX, T), F32), ("h1", (T, D), F32), ("hn", (T, D), F32),
                            ("lists", (E_ * T, 1), I32), ("y", (NPASS * BR, D), F32)):
        dram[name] = nc.dram_tensor(f"scratch_{name}", shape, dt, kind="Internal").ap()
    with ExitStack() as ctx:
        sems = {}

        def sem(name):
            if name not in sems:
                sems[name] = nc.alloc_semaphore(name=name)
            return sems[name]

        def clear():
            nc.clear_and_free_semaphores(list(sems.values()))
            sems.clear()
            nc.all_engine_barrier()

        def sb(name, shape, dt=F32):
            return ctx.enter_context(nc.sbuf_tensor(name, shape, dt))

        g = {"ident": sb("ident", [P, P]), "minus_half": sb("minus_half", [P, NT]), "gates": sb("gates", [P, NT * TOPK]),
             "dense": sb("dense", [P, NT, E_]), "y_row": sb("y_row", [P, NT * TOPK], I32),
             "table": sb("table", [1, 3 * NPASS + 1], I32)}
        with nc.sbuf_tensor("mixT", [P, KD, T], F32) as mixT:
            g["mixT"] = mixT
            with ExitStack() as inner:
                for name, shape in (("xT", [P, KD, T]), ("mask", [P, T]), ("rot", [P, P]), ("gain", [P, 1]),
                                    ("neg_lam", [P, 1]), ("sin", [P, T]), ("cos", [P, T])):
                    g[name] = inner.enter_context(nc.sbuf_tensor(name, shape, F32))
                phase_prepare(nc, dram, g, sem)
                clear()
                phase_attention(nc, dram, g, sem, True)
                clear()
                phase_attention(nc, dram, g, sem, False)
            clear()
            phase_route(nc, dram, g, sem)
            clear()
        phase_experts(nc, dram, g, sem)
        clear()
        phase_finish(nc, dram, g, sem, out)


_INS = ["x", "p", "positions", "g_attn", "w_in", "lambda_q1", "lambda_k1", "lambda_q2", "lambda_k2",
        "g_subln", "b_forget", "w_out", "g_moe", "w_router", "b_router", "w_e1", "b_e1", "w_e2", "b_e2",
        "g_ple", "w_ple_gate", "w_ple_proj", "g_final"]


def kernel(**inputs):
    import numpy as _np
    import concourse.bacc as _bacc
    from concourse import mybir as _mybir
    from concourse.bass_utils import run_bass_kernel_spmd as _run

    nc = _bacc.Bacc("TRN2", target_bir_lowering=False, num_devices=1)
    arrays, dram = {}, {}
    given = {name: _np.ascontiguousarray(inputs[name]) for name in _INS}
    for name in ("g_attn", "g_ple"):
        given[name] = _np.ascontiguousarray(given[name].reshape(KD, P).T)
    for name in ("b_forget", "g_subln"):
        given[name] = _np.ascontiguousarray(given[name].T)
    given.update(constants())
    for name, a in given.items():
        arrays[f"in_{name}_dram"] = a
        dram[name] = nc.dram_tensor(f"in_{name}_dram", a.shape, _mybir.dt.from_np(a.dtype), kind="ExternalInput").ap()
    out = nc.dram_tensor("out_0_dram", (1, T, D), _mybir.dt.float32, kind="ExternalOutput").ap()
    build(nc, dram, out)
    r = _run(nc, [arrays], core_ids=[0])
    return r.results[0]["out_0_dram"]
```
